# Optimizing a Trainium2 kernel written in Bass

```python
import numpy as np
import jax, jax.numpy as jnp
from jax import lax
import math

D_MODEL = 1024
BATCH = 1
SEQ = 256
DEPTH = 2

D_MIX = D_MODEL
D_FF = 2816
NSA_HEADS = 8
NSA_KV_GROUPS = 2
NSA_HEAD_DIM = 64
NSA_GROUP_SIZE = NSA_HEADS // NSA_KV_GROUPS
NSA_OUT = NSA_HEADS * NSA_HEAD_DIM
NSA_KV_DIM = NSA_KV_GROUPS * NSA_HEAD_DIM
CMP_BLOCK = 32
CMP_STRIDE = 16
SLC_BLOCK = 64
SLC_TOPK = 8
WINDOW = 512
Q_BLOCK = 128
POOL_WINDOWS = (2, 4, 8, 16)
POOL_GROUPS = 4
POOL_GROUP_DIM = 64
POOL_DIM = POOL_GROUPS * POOL_GROUP_DIM
GLA_HEADS = 4
GLA_KEY_DIM = 32
GLA_VAL_DIM = 64
GLA_GATE_RANK = 16
GLA_TAU = 16.0
GLA_CHUNK = 64
GLA_QK = GLA_HEADS * GLA_KEY_DIM
GLA_OUT = GLA_HEADS * GLA_VAL_DIM
IN_SPLITS = (NSA_OUT, NSA_KV_DIM, NSA_KV_DIM, NSA_KV_DIM, NSA_KV_DIM, NSA_KV_DIM, NSA_KV_DIM,
             3 * NSA_HEADS, POOL_DIM, GLA_QK, GLA_QK, GLA_OUT, GLA_GATE_RANK, GLA_OUT)
D_IN = NSA_OUT + 6 * NSA_KV_DIM + 3 * NSA_HEADS + POOL_DIM + 2 * GLA_QK + 2 * GLA_OUT + GLA_GATE_RANK
ALPHA = (2.0 * DEPTH) ** 0.25
BETA = (8.0 * DEPTH) ** -0.25
LN_EPS = 1e-5
RMS_EPS = 1e-6


def layer_norm(x, g, b):
    xf = x.astype(jnp.float32)
    mu = jnp.mean(xf, axis=-1, keepdims=True)
    var = jnp.mean(jnp.square(xf - mu), axis=-1, keepdims=True)
    y = (xf - mu) * lax.rsqrt(var + LN_EPS)
    return (y * g + b).astype(x.dtype)

def swiglu(x, wg, wu, wd):
    return (jax.nn.silu(x @ wg) * (x @ wu)) @ wd

def masked_softmax(s, mask):
    s = jnp.where(mask, s.astype(jnp.float32), -jnp.inf)
    m = jnp.max(s, axis=-1, keepdims=True)
    m = jnp.where(jnp.isfinite(m), m, 0.0)
    e = jnp.exp(s - m)
    d = jnp.sum(e, axis=-1, keepdims=True)
    return e / jnp.where(d > 0, d, 1.0)

def compress_tokens(z, pe, w1, w2):
    B, S, G, D = z.shape
    chunks = z.reshape(B, S // CMP_STRIDE, CMP_STRIDE, G, D)
    blocks = jnp.concatenate([chunks[:, :-1], chunks[:, 1:]], axis=2)
    blocks = blocks + pe[None, None, :, None, :]
    flat = jnp.transpose(blocks, (0, 1, 3, 2, 4)).reshape(B, -1, G, CMP_BLOCK * D)
    return jax.nn.gelu(flat @ w1) @ w2

def nsa_mixer(q, kc_raw, vc_raw, ks, vs, kw, vw, gates, pe_k, w1_k, w2_k, pe_v, w1_v, w2_v):
    B, S = q.shape[:2]
    G, R, HD = NSA_KV_GROUPS, NSA_GROUP_SIZE, NSA_HEAD_DIM
    q = q.reshape(B, S, G, R, HD) * (HD ** -0.5)
    kc = compress_tokens(kc_raw, pe_k, w1_k, w2_k)
    vc = compress_tokens(vc_raw, pe_v, w1_v, w2_v)
    n_cmp = kc.shape[1]
    cmp_end = jnp.arange(n_cmp) * CMP_STRIDE + CMP_BLOCK - 1
    n_slc = S // SLC_BLOCK
    topk = min(SLC_TOPK, n_slc)
    c_start = jnp.arange(n_cmp)[:, None] * CMP_STRIDE
    s_start = jnp.arange(n_slc)[None, :] * SLC_BLOCK
    overlap = ((c_start <= s_start + SLC_BLOCK - 1) & (c_start + CMP_BLOCK - 1 >= s_start)).astype(jnp.float32)
    ks_blk = jnp.transpose(ks.reshape(B, n_slc, SLC_BLOCK, G, HD), (0, 3, 1, 2, 4))
    vs_blk = jnp.transpose(vs.reshape(B, n_slc, SLC_BLOCK, G, HD), (0, 3, 1, 2, 4))
    pad = ((0, 0), (WINDOW, 0), (0, 0), (0, 0))
    kw_pad = jnp.pad(kw, pad)
    vw_pad = jnp.pad(vw, pad)
    n_qb = S // Q_BLOCK
    q_blocks = jnp.swapaxes(q.reshape(B, n_qb, Q_BLOCK, G, R, HD), 0, 1)
    g_blocks = jnp.swapaxes(gates.reshape(B, n_qb, Q_BLOCK, G, R, 3), 0, 1)
    blk_ids = jnp.arange(n_slc)
    gather = jax.vmap(jax.vmap(lambda kb, ix: kb[ix]))

    def one_block(args):
        qi, qb, gb = args
        t = qi * Q_BLOCK + jnp.arange(Q_BLOCK)
        s_c = jnp.einsum('bqgrd,bngd->bgrqn', qb, kc)
        p_c = masked_softmax(s_c, cmp_end[None, :] <= t[:, None])
        o_c = jnp.einsum('bgrqn,bngd->bqgrd', p_c.astype(vc.dtype), vc)
        imp = jnp.einsum('bgrqn,nm->bgqm', p_c, overlap)
        cur = (t // SLC_BLOCK)[:, None]
        forced = (blk_ids == 0) | (blk_ids == cur) | (blk_ids == cur - 1)
        future = blk_ids[None, :] * SLC_BLOCK > t[:, None]
        imp = jnp.where(forced, jnp.inf, jnp.where(future, -jnp.inf, imp))
        _, sel = lax.top_k(imp, topk)
        k_sel = gather(ks_blk, sel).reshape(B, G, Q_BLOCK, topk * SLC_BLOCK, HD)
        v_sel = gather(vs_blk, sel).reshape(B, G, Q_BLOCK, topk * SLC_BLOCK, HD)
        kpos = (sel[..., None] * SLC_BLOCK + jnp.arange(SLC_BLOCK)).reshape(B, G, Q_BLOCK, topk * SLC_BLOCK)
        s_s = jnp.einsum('bqgrd,bgqkd->bgrqk', qb, k_sel)
        p_s = masked_softmax(s_s, (kpos <= t[:, None])[:, :, None])
        o_s = jnp.einsum('bgrqk,bgqkd->bqgrd', p_s.astype(v_sel.dtype), v_sel)
        start = qi * Q_BLOCK
        k_win = lax.dynamic_slice_in_dim(kw_pad, start, Q_BLOCK + WINDOW, axis=1)
        v_win = lax.dynamic_slice_in_dim(vw_pad, start, Q_BLOCK + WINDOW, axis=1)
        kp = start - WINDOW + jnp.arange(Q_BLOCK + WINDOW)
        mask_w = (kp[None, :] <= t[:, None]) & (kp[None, :] > t[:, None] - WINDOW) & (kp[None, :] >= 0)
        s_w = jnp.einsum('bqgrd,bkgd->bgrqk', qb, k_win)
        p_w = masked_softmax(s_w, mask_w)
        o_w = jnp.einsum('bgrqk,bkgd->bqgrd', p_w.astype(v_win.dtype), v_win)
        o = gb[..., 0:1] * o_c + gb[..., 1:2] * o_s + gb[..., 2:3] * o_w
        return o.reshape(B, Q_BLOCK, G * R * HD)

    out = lax.map(one_block, (jnp.arange(n_qb), q_blocks, g_blocks))
    return jnp.swapaxes(out, 0, 1).reshape(B, S, NSA_OUT)

def pool_mixer(u, pool_w, pool_scale):
    B, S, _ = u.shape
    uf = u.astype(jnp.float32).reshape(B, S, POOL_GROUPS, POOL_GROUP_DIM)
    c = jnp.pad(jnp.cumsum(uf, axis=1), ((0, 0), (1, 0), (0, 0), (0, 0)))
    t = jnp.arange(S)
    means = []
    for gi, w in enumerate(POOL_WINDOWS):
        cg = c[:, :, gi]
        lower = jnp.pad(cg, ((0, 0), (w, 0), (0, 0)))[:, 1:S + 1]
        cnt = jnp.minimum(w, t + 1).astype(jnp.float32)[None, :, None]
        means.append((cg[:, 1:] - lower) / cnt)
    pooled = (jnp.stack(means, axis=2) - uf).astype(u.dtype)
    y = jnp.einsum('bsgc,gcd->bsgd', pooled, pool_w).reshape(B, S, POOL_DIM)
    return y * pool_scale

def gla_mixer(q, k, v, a_lr, r, wa2, ba, norm_g):
    B, S = q.shape[:2]
    H, DK, DV, C = GLA_HEADS, GLA_KEY_DIM, GLA_VAL_DIM, GLA_CHUNK
    nc = S // C
    log_a = jax.nn.log_sigmoid((a_lr @ wa2 + ba).astype(jnp.float32)) / GLA_TAU
    qf = q.astype(jnp.float32).reshape(B, nc, C, H, DK) * (DK ** -0.5)
    kf = k.astype(jnp.float32).reshape(B, nc, C, H, DK)
    vf = v.astype(jnp.float32).reshape(B, nc, C, H, DV)
    b = jnp.cumsum(log_a.reshape(B, nc, C, H, DK), axis=2)
    b_last = b[:, :, -1:]
    q_t = qf * jnp.exp(b)
    k_t = kf * jnp.exp(-b)
    causal = jnp.tril(jnp.ones((C, C), dtype=bool))
    A = jnp.where(causal, jnp.einsum('bnihk,bnjhk->bnhij', q_t, k_t), 0.0)
    o_intra = jnp.einsum('bnhij,bnjhv->bnihv', A, vf)
    dS = jnp.einsum('bnjhk,bnjhv->nbhkv', kf * jnp.exp(b_last - b), vf)
    decay = jnp.swapaxes(jnp.exp(b_last[:, :, 0]), 0, 1)

    def step(state, inp):
        d, ds = inp
        return d[..., None] * state + ds, state

    _, s_in = lax.scan(step, jnp.zeros((B, H, DK, DV), jnp.float32), (decay, dS))
    o_inter = jnp.einsum('bnihk,nbhkv->bnihv', q_t, s_in)
    o = (o_intra + o_inter).reshape(B, S, H, DV)
    o = o * lax.rsqrt(jnp.mean(jnp.square(o), axis=-1, keepdims=True) + RMS_EPS)
    o = o.reshape(B, S, GLA_OUT) * norm_g
    return (o * jax.nn.silu(r.astype(jnp.float32))).astype(q.dtype)

def token_mix(x, w_in, w_out, cmp_pe, cmp_w1, cmp_w2, pool_w, pool_scale, gla_wa2, gla_ba, gla_norm_g):
    B, S, _ = x.shape
    h = x @ w_in
    split_pts = np.cumsum(IN_SPLITS)[:-1].tolist()
    (nq, kc, vc, ks, vs, kw, vw, gl, u, gq, gk, gv, ga, gr) = jnp.split(h, split_pts, axis=-1)
    kv = lambda z: z.reshape(B, S, NSA_KV_GROUPS, NSA_HEAD_DIM)
    gates = jax.nn.sigmoid(gl).reshape(B, S, NSA_HEADS, 3)
    o_a = nsa_mixer(nq, kv(kc), kv(vc), kv(ks), kv(vs), kv(kw), kv(vw), gates,
                    cmp_pe[0], cmp_w1[0], cmp_w2[0], cmp_pe[1], cmp_w1[1], cmp_w2[1])
    o_b = pool_mixer(u, pool_w, pool_scale)
    o_c = gla_mixer(gq, gk, gv, ga, gr, gla_wa2, gla_ba, gla_norm_g)
    return jnp.concatenate([o_a, o_b, o_c], axis=-1) @ w_out

def first_inputs(seed: int = 0) -> dict:
    key = jax.random.key(seed)
    ks = jax.random.split(key, 16)
    nrm = lambda k, shape, s: jax.random.normal(k, shape, jnp.float32) * s
    L = DEPTH
    return {
        "x": nrm(ks[0], (BATCH, SEQ, D_MODEL), 1.0),
        "ln_g": 1.0 + nrm(ks[1], (L, 3, D_MODEL), 0.05),
        "ln_b": nrm(ks[2], (L, 3, D_MODEL), 0.01),
        "ffn_wg": nrm(ks[3], (L, 2, D_MODEL, D_FF), D_MODEL ** -0.5),
        "ffn_wu": nrm(ks[4], (L, 2, D_MODEL, D_FF), D_MODEL ** -0.5),
        "ffn_wd": nrm(ks[5], (L, 2, D_FF, D_MODEL), BETA * D_FF ** -0.5),
        "w_in": nrm(ks[6], (L, D_MODEL, D_IN), D_MODEL ** -0.5),
        "w_out": nrm(ks[7], (L, D_MIX, D_MODEL), BETA * D_MIX ** -0.5),
        "cmp_pe": nrm(ks[8], (L, 2, CMP_BLOCK, NSA_HEAD_DIM), 0.1),
        "cmp_w1": nrm(ks[9], (L, 2, CMP_BLOCK * NSA_HEAD_DIM, NSA_HEAD_DIM), (CMP_BLOCK * NSA_HEAD_DIM) ** -0.5),
        "cmp_w2": nrm(ks[10], (L, 2, NSA_HEAD_DIM, NSA_HEAD_DIM), NSA_HEAD_DIM ** -0.5),
        "pool_w": nrm(ks[11], (L, POOL_GROUPS, POOL_GROUP_DIM, POOL_GROUP_DIM), POOL_GROUP_DIM ** -0.5),
        "pool_scale": 1.0 + nrm(ks[12], (L, POOL_DIM), 0.1),
        "gla_wa2": nrm(ks[13], (L, GLA_GATE_RANK, GLA_QK), GLA_GATE_RANK ** -0.5),
        "gla_ba": nrm(ks[14], (L, GLA_QK), 0.1),
        "gla_norm_g": 1.0 + nrm(ks[15], (L, GLA_OUT), 0.05),
    }

def first_block(x, ln_g, ln_b, ffn_wg, ffn_wu, ffn_wd, w_in, w_out, cmp_pe, cmp_w1, cmp_w2,
              pool_w, pool_scale, gla_wa2, gla_ba, gla_norm_g):
    for l in range(DEPTH):
        x = layer_norm(ALPHA * x + 0.5 * swiglu(x, ffn_wg[l, 0], ffn_wu[l, 0], ffn_wd[l, 0]), ln_g[l, 0], ln_b[l, 0])
        m = token_mix(x, w_in[l], w_out[l], cmp_pe[l], cmp_w1[l], cmp_w2[l], pool_w[l], pool_scale[l],
                      gla_wa2[l], gla_ba[l], gla_norm_g[l])
        x = layer_norm(ALPHA * x + m, ln_g[l, 1], ln_b[l, 1])
        x = layer_norm(ALPHA * x + 0.5 * swiglu(x, ffn_wg[l, 1], ffn_wu[l, 1], ffn_wd[l, 1]), ln_g[l, 2], ln_b[l, 2])
    return x


MLSTM_INNER = 2 * D_MODEL
MLSTM_HEADS = 4
MLSTM_HEAD_DIM = MLSTM_INNER // MLSTM_HEADS
MLSTM_CONV = 4
QKV_BLOCK = 4
MLSTM_CHUNK = 128
S5_GROUP = 16
S5_GROUPS = D_MODEL // S5_GROUP
S5_STATE = 64
S5_CHUNK = 128
DT_MIN = 0.001
DT_MAX = 0.1
N_EXPERTS = 8
TOP_K = 2
N_EVEN = (DEPTH + 1) // 2
N_ODD = DEPTH // 2
DEEPNORM_ALPHA = (2 * DEPTH) ** 0.25
DEEPNORM_BETA = (8 * DEPTH) ** -0.25


def layer_norm_2(x, g, b):
    xf = x.astype(jnp.float32)
    mu = jnp.mean(xf, -1, keepdims=True)
    var = jnp.mean(jnp.square(xf - mu), -1, keepdims=True)
    return ((xf - mu) * lax.rsqrt(var + LN_EPS) * g.astype(jnp.float32) + b.astype(jnp.float32)).astype(x.dtype)

def causal_depthwise_conv(x, w, b):
    K, C = w.shape
    y = lax.conv_general_dilated(x, w[:, None, :].astype(x.dtype), window_strides=(1,), padding=[(K - 1, 0)],
                                 dimension_numbers=('NWC', 'WIO', 'NWC'), feature_group_count=C)
    return y + b

def block_diag_proj(x, w):
    nb, blk, _ = w.shape
    xb = x.reshape(x.shape[:-1] + (nb, blk))
    return jnp.einsum('bsni,nio->bsno', xb, w).reshape(x.shape)

def swiglu_2(x, w13, w2):
    gate, up = jnp.split(x @ w13, 2, axis=-1)
    return (jax.nn.silu(gate) * up) @ w2

def mlstm_chunkwise(q, k, v, log_i, log_f):
    Bsz, NH, S, DH = q.shape
    L = MLSTM_CHUNK
    NC = S // L

    def chunks(t):
        return jnp.moveaxis(t.reshape((Bsz, NH, NC, L) + t.shape[3:]), 2, 0)

    causal = jnp.tril(jnp.ones((L, L), dtype=bool))

    def step(carry, inp):
        C, n, m = carry
        qc, kc, vc, ic, fc = inp
        b = jnp.cumsum(fc, axis=-1)
        d_log = jnp.where(causal, b[..., :, None] - b[..., None, :] + ic[..., None, :], -jnp.inf)
        inter = b + m[..., None]
        m_t = jnp.maximum(inter, jnp.max(d_log, axis=-1))
        scores = jnp.einsum('bhtd,bhsd->bhts', qc, kc) * jnp.exp(d_log - m_t[..., None])
        dec = jnp.exp(inter - m_t)
        num = jnp.einsum('bhts,bhse->bhte', scores, vc) + dec[..., None] * jnp.einsum('bhtd,bhde->bhte', qc, C)
        den = jnp.sum(scores, -1) + dec * jnp.einsum('bhtd,bhd->bht', qc, n)
        h = num / jnp.maximum(jnp.abs(den), jnp.exp(-m_t))[..., None]
        b_last = b[..., -1]
        g = b_last[..., None] - b + ic
        m_new = jnp.maximum(b_last + m, jnp.max(g, axis=-1))
        wk = jnp.exp(g - m_new[..., None])[..., None] * kc
        dC = jnp.exp(b_last + m - m_new)
        C_new = dC[..., None, None] * C + jnp.einsum('bhsd,bhse->bhde', wk, vc)
        n_new = dC[..., None] * n + jnp.sum(wk, axis=2)
        return (C_new, n_new, m_new), h

    init = (jnp.zeros((Bsz, NH, DH, DH), jnp.float32), jnp.zeros((Bsz, NH, DH), jnp.float32),
            jnp.zeros((Bsz, NH), jnp.float32))
    _, h = lax.scan(step, init, (chunks(q), chunks(k), chunks(v), chunks(log_i), chunks(log_f)))
    return jnp.moveaxis(h, 0, 2).reshape(Bsz, NH, S, DH)

def mlstm_mixer(u, w_in, conv_w, conv_b, wq, wk, wv, w_gates, b_gates, norm_w, skip, w_out):
    Bsz, S, _ = u.shape
    xm, z = jnp.split(u @ w_in, 2, axis=-1)
    xc = jax.nn.silu(causal_depthwise_conv(xm, conv_w, conv_b))
    q = block_diag_proj(xc, wq)
    k = block_diag_proj(xc, wk)
    v = block_diag_proj(xm, wv)
    wg_q, wg_k, wg_v = jnp.split(w_gates, 3, axis=0)
    gates = (q @ wg_q + k @ wg_k + v @ wg_v + b_gates).astype(jnp.float32)
    i_pre, f_pre = jnp.split(gates, 2, axis=-1)
    log_f = jax.nn.log_sigmoid(f_pre)

    def heads(t):
        return t.reshape(Bsz, S, MLSTM_HEADS, MLSTM_HEAD_DIM).transpose(0, 2, 1, 3).astype(jnp.float32)

    h = mlstm_chunkwise(heads(q) * (MLSTM_HEAD_DIM ** -0.5), heads(k), heads(v),
                        i_pre.transpose(0, 2, 1), log_f.transpose(0, 2, 1))
    mu = jnp.mean(h, -1, keepdims=True)
    var = jnp.mean(jnp.square(h - mu), -1, keepdims=True)
    h = ((h - mu) * lax.rsqrt(var + LN_EPS)).transpose(0, 2, 1, 3).reshape(Bsz, S, MLSTM_INNER).astype(u.dtype)
    h = (h * norm_w + skip * xc) * jax.nn.silu(z)
    return h @ w_out

def _complex_affine_combine(e1, e2):
    a1r, a1i, b1r, b1i = e1
    a2r, a2i, b2r, b2i = e2
    return (a2r * a1r - a2i * a1i, a2r * a1i + a2i * a1r,
            a2r * b1r - a2i * b1i + b2r, a2r * b1i + a2i * b1r + b2i)

def s5_mixer(u, lam_re, lam_im, b_re, b_im, c_re, c_im, d_skip, log_dt, w_glu, b_glu):
    Bsz, S, _ = u.shape
    G, P, H = b_re.shape
    L = S5_CHUNK
    NC = S // L
    f32 = lambda t: t.astype(jnp.float32)
    lr, li = f32(lam_re), f32(lam_im)
    dt = jnp.exp(f32(log_dt))[:, None]
    mag = jnp.exp(lr * dt)
    ar, ai = mag * jnp.cos(li * dt), mag * jnp.sin(li * dt)
    den = lr * lr + li * li
    kr = ((ar - 1.0) * lr + ai * li) / den
    ki = (ai * lr - (ar - 1.0) * li) / den
    br, bi = f32(b_re), f32(b_im)
    bbar_re = kr[..., None] * br - ki[..., None] * bi
    bbar_im = kr[..., None] * bi + ki[..., None] * br
    cr, ci = f32(c_re), f32(c_im)
    steps = jnp.arange(1, L + 1, dtype=jnp.float32)[:, None, None]
    pmag = jnp.exp(steps * lr * dt)
    pr = (pmag * jnp.cos(steps * li * dt))[:, None]
    pi_ = (pmag * jnp.sin(steps * li * dt))[:, None]
    uf = f32(u).reshape(Bsz, NC, L, G, H).transpose(1, 2, 0, 3, 4)

    def step(carry, uc):
        xr0, xi0 = carry
        bur = jnp.einsum('lbgh,gph->lbgp', uc, bbar_re)
        bui = jnp.einsum('lbgh,gph->lbgp', uc, bbar_im)
        a_r = jnp.broadcast_to(ar, bur.shape)
        a_i = jnp.broadcast_to(ai, bur.shape)
        _, _, sr, si = lax.associative_scan(_complex_affine_combine, (a_r, a_i, bur, bui), axis=0)
        xr = pr * xr0 - pi_ * xi0 + sr
        xi = pr * xi0 + pi_ * xr0 + si
        y = jnp.einsum('ghp,lbgp->lbgh', cr, xr) - jnp.einsum('ghp,lbgp->lbgh', ci, xi)
        return (xr[-1], xi[-1]), y

    init = (jnp.zeros((Bsz, G, P), jnp.float32), jnp.zeros((Bsz, G, P), jnp.float32))
    _, y = lax.scan(step, init, uf)
    y = y.transpose(2, 0, 1, 3, 4).reshape(Bsz, S, G * H) + f32(d_skip) * f32(u)
    g = jax.nn.gelu(y).astype(u.dtype)
    val, gate = jnp.split(g @ w_glu + b_glu, 2, axis=-1)
    return val * jax.nn.sigmoid(gate)

def moe_ffn(u, w_router, w13, w2):
    Bsz, S, D = u.shape
    t = u.reshape(-1, D)
    logits = (t @ w_router).astype(jnp.float32)
    top_val, top_idx = lax.top_k(logits, TOP_K)
    top_w = jax.nn.softmax(top_val, axis=-1)
    out = jnp.zeros_like(t)
    for e in range(N_EXPERTS):
        gate_e = jnp.sum(jnp.where(top_idx == e, top_w, 0.0), axis=-1).astype(t.dtype)
        out = out + gate_e[:, None] * swiglu_2(t, w13[e], w2[e])
    return out.reshape(Bsz, S, D)

def second_inputs(seed: int = 0) -> dict:
    key = jax.random.key(seed)
    ks = iter(jax.random.split(key, 40))
    f32 = jnp.float32

    def nrm(shape, std):
        return std * jax.random.normal(next(ks), shape, f32)

    D, Di, NH, G, P, H, F, E = D_MODEL, MLSTM_INNER, MLSTM_HEADS, S5_GROUPS, S5_STATE, S5_GROUP, D_FF, N_EXPERTS
    beta = DEEPNORM_BETA
    x = nrm((BATCH, SEQ, D), 1.0)
    c = nrm((BATCH, D), 1.0)
    ada_w = nrm((DEPTH, D, 6 * D), 0.2 * D ** -0.5)
    ada_b = nrm((DEPTH, 6 * D), 0.01)
    ln_mix_g = 1.0 + nrm((DEPTH, D), 0.01)
    ln_mix_b = nrm((DEPTH, D), 0.01)
    ln_ffn_g = 1.0 + nrm((DEPTH, D), 0.01)
    ln_ffn_b = nrm((DEPTH, D), 0.01)
    mlstm_w_in = nrm((N_EVEN, D, 2 * Di), D ** -0.5)
    mlstm_conv_w = nrm((N_EVEN, MLSTM_CONV, Di), MLSTM_CONV ** -0.5)
    mlstm_conv_b = nrm((N_EVEN, Di), 0.01)
    mlstm_wq = nrm((N_EVEN, Di // QKV_BLOCK, QKV_BLOCK, QKV_BLOCK), QKV_BLOCK ** -0.5)
    mlstm_wk = nrm((N_EVEN, Di // QKV_BLOCK, QKV_BLOCK, QKV_BLOCK), QKV_BLOCK ** -0.5)
    mlstm_wv = nrm((N_EVEN, Di // QKV_BLOCK, QKV_BLOCK, QKV_BLOCK), QKV_BLOCK ** -0.5)
    mlstm_w_gates = nrm((N_EVEN, 3 * Di, 2 * NH), (3 * Di) ** -0.5)
    mlstm_b_gates = jnp.concatenate([nrm((N_EVEN, NH), 0.1),
                                     jnp.linspace(3.0, 6.0, NH, dtype=f32)[None] + nrm((N_EVEN, NH), 0.01)], axis=-1)
    mlstm_norm_w = 1.0 + nrm((N_EVEN, Di), 0.01)
    mlstm_skip = 1.0 + nrm((N_EVEN, Di), 0.01)
    mlstm_w_out = nrm((N_EVEN, Di, D), beta * Di ** -0.5)
    ffn_w13 = nrm((N_EVEN, D, 2 * F), D ** -0.5)
    ffn_w2 = nrm((N_EVEN, F, D), beta * F ** -0.5)
    s5_lambda_re = -0.5 + nrm((N_ODD, G, P), 0.01)
    s5_lambda_im = jnp.tile((math.pi * jnp.arange(P, dtype=f32))[None, None, :], (N_ODD, G, 1))
    s5_b_re = nrm((N_ODD, G, P, H), (2 * H) ** -0.5)
    s5_b_im = nrm((N_ODD, G, P, H), (2 * H) ** -0.5)
    s5_c_re = nrm((N_ODD, G, H, P), (2 * P) ** -0.5)
    s5_c_im = nrm((N_ODD, G, H, P), (2 * P) ** -0.5)
    s5_d = nrm((N_ODD, D), 1.0)
    s5_log_dt = jax.random.uniform(next(ks), (N_ODD, G), f32, math.log(DT_MIN), math.log(DT_MAX))
    s5_w_glu = jnp.concatenate([nrm((N_ODD, D, D), beta * D ** -0.5), nrm((N_ODD, D, D), D ** -0.5)], axis=-1)
    s5_b_glu = nrm((N_ODD, 2 * D), 0.01)
    moe_router = nrm((N_ODD, D, E), D ** -0.5)
    moe_w13 = nrm((N_ODD, E, D, 2 * F), D ** -0.5)
    moe_w2 = nrm((N_ODD, E, F, D), beta * F ** -0.5)
    return {"x": x, "c": c, "ada_w": ada_w, "ada_b": ada_b, "ln_mix_g": ln_mix_g, "ln_mix_b": ln_mix_b,
            "ln_ffn_g": ln_ffn_g, "ln_ffn_b": ln_ffn_b,
            "mlstm_w_in": mlstm_w_in, "mlstm_conv_w": mlstm_conv_w, "mlstm_conv_b": mlstm_conv_b,
            "mlstm_wq": mlstm_wq, "mlstm_wk": mlstm_wk, "mlstm_wv": mlstm_wv, "mlstm_w_gates": mlstm_w_gates,
            "mlstm_b_gates": mlstm_b_gates, "mlstm_norm_w": mlstm_norm_w, "mlstm_skip": mlstm_skip,
            "mlstm_w_out": mlstm_w_out, "ffn_w13": ffn_w13, "ffn_w2": ffn_w2,
            "s5_lambda_re": s5_lambda_re, "s5_lambda_im": s5_lambda_im, "s5_b_re": s5_b_re, "s5_b_im": s5_b_im,
            "s5_c_re": s5_c_re, "s5_c_im": s5_c_im, "s5_d": s5_d, "s5_log_dt": s5_log_dt,
            "s5_w_glu": s5_w_glu, "s5_b_glu": s5_b_glu,
            "moe_router": moe_router, "moe_w13": moe_w13, "moe_w2": moe_w2}

def second_block(x, c, ada_w, ada_b, ln_mix_g, ln_mix_b, ln_ffn_g, ln_ffn_b,
              mlstm_w_in, mlstm_conv_w, mlstm_conv_b, mlstm_wq, mlstm_wk, mlstm_wv, mlstm_w_gates,
              mlstm_b_gates, mlstm_norm_w, mlstm_skip, mlstm_w_out, ffn_w13, ffn_w2,
              s5_lambda_re, s5_lambda_im, s5_b_re, s5_b_im, s5_c_re, s5_c_im, s5_d, s5_log_dt,
              s5_w_glu, s5_b_glu, moe_router, moe_w13, moe_w2):
    cond = jax.nn.silu(c)
    for i in range(DEPTH):
        j = i // 2
        mod = cond @ ada_w[i] + ada_b[i]
        sh_m, sc_m, g_m, sh_f, sc_f, g_f = [t[:, None, :] for t in jnp.split(mod, 6, axis=-1)]
        u = x * (1.0 + sc_m) + sh_m
        if i % 2 == 0:
            y = mlstm_mixer(u, mlstm_w_in[j], mlstm_conv_w[j], mlstm_conv_b[j], mlstm_wq[j], mlstm_wk[j],
                            mlstm_wv[j], mlstm_w_gates[j], mlstm_b_gates[j], mlstm_norm_w[j], mlstm_skip[j],
                            mlstm_w_out[j])
        else:
            y = s5_mixer(u, s5_lambda_re[j], s5_lambda_im[j], s5_b_re[j], s5_b_im[j], s5_c_re[j], s5_c_im[j],
                         s5_d[j], s5_log_dt[j], s5_w_glu[j], s5_b_glu[j])
        x = layer_norm_2(DEEPNORM_ALPHA * x + (1.0 + g_m) * y, ln_mix_g[i], ln_mix_b[i])
        u = x * (1.0 + sc_f) + sh_f
        if i % 2 == 0:
            y = swiglu_2(u, ffn_w13[j], ffn_w2[j])
        else:
            y = moe_ffn(u, moe_router[j], moe_w13[j], moe_w2[j])
        x = layer_norm_2(DEEPNORM_ALPHA * x + (1.0 + g_f) * y, ln_ffn_g[i], ln_ffn_b[i])
    return x


def setup_inputs(seed=0):
    out = dict(first_inputs(seed))
    for name, value in second_inputs(seed + 1).items():
        if name != "x":
            out[name + "_2"] = value
    return out


def reference(
    x, ln_g, ln_b, ffn_wg, ffn_wu, ffn_wd, w_in, w_out, cmp_pe, cmp_w1, cmp_w2, pool_w,
    pool_scale, gla_wa2, gla_ba, gla_norm_g, c_2, ada_w_2, ada_b_2, ln_mix_g_2, ln_mix_b_2,
    ln_ffn_g_2, ln_ffn_b_2, mlstm_w_in_2, mlstm_conv_w_2, mlstm_conv_b_2, mlstm_wq_2,
    mlstm_wk_2, mlstm_wv_2, mlstm_w_gates_2, mlstm_b_gates_2, mlstm_norm_w_2, mlstm_skip_2,
    mlstm_w_out_2, ffn_w13_2, ffn_w2_2, s5_lambda_re_2, s5_lambda_im_2, s5_b_re_2, s5_b_im_2,
    s5_c_re_2, s5_c_im_2, s5_d_2, s5_log_dt_2, s5_w_glu_2, s5_b_glu_2, moe_router_2, moe_w13_2,
    moe_w2_2,
):
    x = first_block(
        x, ln_g, ln_b, ffn_wg, ffn_wu, ffn_wd, w_in, w_out, cmp_pe, cmp_w1, cmp_w2, pool_w,
        pool_scale, gla_wa2, gla_ba, gla_norm_g,
    )
    return second_block(
        x, c_2, ada_w_2, ada_b_2, ln_mix_g_2, ln_mix_b_2, ln_ffn_g_2, ln_ffn_b_2, mlstm_w_in_2,
        mlstm_conv_w_2, mlstm_conv_b_2, mlstm_wq_2, mlstm_wk_2, mlstm_wv_2, mlstm_w_gates_2,
        mlstm_b_gates_2, mlstm_norm_w_2, mlstm_skip_2, mlstm_w_out_2, ffn_w13_2, ffn_w2_2,
        s5_lambda_re_2, s5_lambda_im_2, s5_b_re_2, s5_b_im_2, s5_c_re_2, s5_c_im_2, s5_d_2,
        s5_log_dt_2, s5_w_glu_2, s5_b_glu_2, moe_router_2, moe_w13_2, moe_w2_2,
    )


_drawn_inputs = setup_inputs


def setup_inputs(seed=0):
    import zlib

    import numpy as np

    out = dict(_drawn_inputs(seed))
    spreads = {}
    factors = {'cmp_pe': 3.684,
     'gla_ba': 3.363,
     'gla_norm_g': 3.501,
     'ada_b_2': 2.834,
     'ln_mix_b_2': 3.331,
     'ln_ffn_g_2': 8.388,
     'ln_ffn_b_2': 9.415,
     'mlstm_conv_b_2': 4.379,
     'mlstm_norm_w_2': 35.122,
     'mlstm_skip_2': 42.294,
     's5_lambda_re_2': 64.0,
     's5_lambda_im_2': 54.36,
     's5_b_re_2': 47.824,
     's5_b_im_2': 63.448,
     's5_c_re_2': 63.232,
     's5_c_im_2': 49.792,
     's5_log_dt_2': 40.752,
     's5_b_glu_2': 23.86,
     'ln_mix_g_2': 3.007}
    for name, (base, spread) in spreads.items():
        noise = np.random.default_rng([zlib.crc32(name.encode()), seed]).standard_normal(out[name].shape)
        drawn = base * np.exp(spread * noise) if base else spread * noise
        out[name] = __import__('jax').numpy.asarray(drawn.astype(out[name].dtype))
    for name, factor in factors.items():
        out[name] = (out[name] * factor).astype(out[name].dtype)
    return out
```

```python
from contextlib import ExitStack

import numpy as np

import concourse.bass as bass
from concourse import mybir

F32 = mybir.dt.float32
U32 = mybir.dt.uint32
ALU = mybir.AluOpType
ACT = mybir.ActivationFunctionType
AX_X = mybir.AxisListType.X

P = 128
SEQ = 256
NT = SEQ // P
D = 1024
KD = D // P
DEPTH = 2
D_FF = 2816
CHUNK = 512
CHUNKS = [(c, min(CHUNK, D_FF - c)) for c in range(0, D_FF, CHUNK)]
NC = len(CHUNKS)
NG = NC * NT
FT = D_FF // P
ALPHA = (2.0 * DEPTH) ** 0.25
LN_EPS = 1e-5
RMS_EPS = 1e-6
NEG = -1e30

HEADS, HD, GROUPS = 8, 64, 2
REP = HEADS // GROUPS
CMP_BLOCK, CMP_STRIDE = 32, 16
N_CMP = SEQ // CMP_STRIDE - 1
POOL_WINDOWS = (2, 4, 8, 16)
GLA_H, GLA_K, GLA_V, GLA_CHUNK, GLA_TAU = 4, 32, 64, 64, 16.0
IN_SIZES = [("nq", 512), ("kc", 128), ("vc", 128), ("ks", 128), ("vs", 128), ("kw", 128), ("vw", 128),
            ("gl", 24), ("u", 256), ("gq", 128), ("gk", 128), ("gv", 256), ("ga", 16), ("gr", 256)]
D_IN = sum(n for _, n in IN_SIZES)
IN_PANELS = [(0, 512), (512, 512), (1024, 280), (1304, 512), (1816, 272), (2088, 256)]

ML_INNER, ML_HEADS, ML_CONV, QKV_BLOCK = 2 * D, 4, 4, 4
ML_HD = ML_INNER // ML_HEADS
ML_T = ML_INNER // P
S5_G, S5_H, S5_P = 64, 16, 64
S5_T = S5_G * S5_P // P
EXPERTS = 8

SLOTS = 4
SLOT = KD * CHUNK


def shape_constants():
    p = np.arange(P)[:, None]
    f = np.arange(P)[None, :]
    t = np.arange(SEQ)
    parts = {}
    parts["ident"] = (p == f)
    parts["ones"] = np.ones((P, P))
    parts["upto"] = (p <= f)
    causal = np.where(f <= p, 0.0, NEG)
    parts["causal"] = np.concatenate([np.zeros((P, P)), causal], 1)
    n = np.arange(CMP_STRIDE)
    end = n * CMP_STRIDE + CMP_BLOCK - 1
    seen = np.stack([(end[None, :] <= p + P * i) & (n[None, :] < N_CMP) for i in range(NT)], 1)
    parts["cmp_seen"] = seen.reshape(P, -1)
    parts["cmp_bias"] = np.where(seen, 0.0, NEG).reshape(P, -1)
    parts["head_rows"] = (p // CMP_STRIDE == np.arange(HEADS)[None, :])
    parts["blk4"] = (p // QKV_BLOCK == np.arange(P // QKV_BLOCK)[None, :])
    bands = []
    for w in POOL_WINDOWS:
        s = np.arange(SEQ)[:, None]
        band = ((s <= t) & (s > t - w)) / np.minimum(w, t + 1.0)[None, :] - (s == t)
        bands += [band[0:P, :], band[P:, P:]]
    parts["bands"] = np.concatenate(bands, 1)
    parts["gla_keep"] = ((p <= f) & (p // GLA_CHUNK == f // GLA_CHUNK))
    parts["gla_go"] = np.tile((t % GLA_CHUNK != 0)[None, :], (P, 1))
    parts["steps"] = np.tile(t[None, :], (P, 1))
    parts["b_own"] = (p // S5_P == np.arange(2)[None, :])
    grp = np.arange(P)[None, None, :] // S5_H
    parts["c_own"] = (grp == 2 * np.arange(4)[None, :, None] + (np.arange(P) // S5_P)[:, None, None]).reshape(P, -1)
    parts["experts"] = np.tile(np.arange(EXPERTS)[None, :], (P, 1))
    at, cols, start = {}, [], 0
    for name, a in parts.items():
        a = np.asarray(a, np.float32)
        at[name] = (start, a.shape[1])
        cols.append(a)
        start += a.shape[1]
    return at, np.ascontiguousarray(np.concatenate(cols, 1))


class Count:

    def __init__(self, sem):
        self.sem, self.value = sem, 0

    def one(self):
        self.value += 1
        return self.sem, 1

    def now(self):
        return self.sem, self.value


class Events:

    def __init__(self, sem, names):
        self.sem, self.names = sem, list(names)
        self.at = {n: i + 1 for i, n in enumerate(self.names)}
        assert len(self.at) == len(self.names)
        self.made = 0

    def inc(self, name, rep=0):
        assert self.at[name] + rep * len(self.names) == self.made + 1, (name, self.names[self.made % len(self.names)])
        self.made += 1
        return self.sem, 1

    def after(self, name, rep=0):
        return self.sem, rep * len(self.names) + self.at[name]


class Panel:

    def __init__(self, slot, landed, over, before):
        self.slot, self.landed, self.over, self.before = slot, landed, over, before


class Ring:

    def __init__(self, freed):
        self.freed, self.uses, self.landed = freed, [0] * (SLOTS + 1), [0] * (SLOTS + 1)
        self.over, self.next = [None] * (SLOTS + 1), 0

    def take(self, slot=None, dmas=1, over=None):
        if slot is None:
            slot = self.next
            self.next = (slot + 1) % SLOTS
        self.landed[slot] += 16 * dmas
        if over is None:
            self.uses[slot] += 1
            over = self.freed[slot], self.uses[slot]
        before, self.over[slot] = self.over[slot], over
        return Panel(slot, self.landed[slot], over, before)


TAIL = SLOTS
STAGES = ["ffn0", "ln0", "mix0", "ln1", "ffn1", "ln2", "ffn2", "ln3", "mix1", "ln4", "ffn3", "ln5",
          "mlstm", "ln6", "ffn4", "ln7", "s5", "ln8", "moe", "ln9"]


def build_program(nc, A, out, const_at, upto=None):
    stages = STAGES if upto is None else STAGES[:STAGES.index(upto) + 1]
    with ExitStack() as ctx:
        program(nc, A, out, const_at, stages, ctx)


def program(nc, A, out, const_at, stages, ctx):
    def sb(name, shape, dt=F32):
        return ctx.enter_context(nc.sbuf_tensor(name, shape, dt))

    def sem(name):
        return ctx.enter_context(nc.semaphore(name))

    psum = ctx.enter_context(nc.psum_tensor("psum", [P, 8, 512], F32))
    n_const = sum(n for _, n in const_at.values())
    consts = sb("consts", [P, n_const])

    def const(name):
        start, n = const_at[name]
        return consts[:, start:start + n]

    ident, ones = const("ident"), const("ones")
    ring = sb("ring", [P, SLOTS, SLOT])
    tail = sb("tail", [P, SLOT // 2])
    x = sb("x", [P, NT, D])
    xT = sb("xT", [P, KD, SEQ])
    z = sb("z", [P, NT, D])
    lnp = sb("lnp", [P, 3, D])
    bn = sb("bn", [P, NT, 2, 6])
    mv = sb("mv", [P, NT, 2])
    std = sb("std", [P, NT])
    rstd = sb("rstd", [P, NT])
    eps = sb("eps", [P, 4])

    cols_a_nat = sb("cols_a_nat", [P, P])
    cols_b_nat = sb("cols_b_nat", [P, P])
    lam_nat = sb("lam_nat", [96, P])
    dt_nat = sb("dt_nat", [96, 2])
    pe_nat = sb("pe_nat", [CMP_BLOCK, DEPTH * 2, 2, HD])
    cols_a = sb("cols_a", [P, 120])
    cols_b = sb("cols_b", [P, 110])
    lam = sb("lam", [P, 96])
    pe_col = sb("pe_col", [P, DEPTH * 2, CMP_BLOCK])
    cond = sb("cond", [P, KD])
    w2bd = sb("w2bd", [P, DEPTH * 2, P])
    poolbd = sb("poolbd", [P, DEPTH * 2, P])
    gla_wa2 = sb("gla_wa2", [16, DEPTH, P])
    gla_norm = sb("gla_norm", [P, DEPTH, GLA_H * GLA_V])
    qkv_w = sb("qkv_w", [P, 3, ML_T, QKV_BLOCK])
    gate_w = sb("gate_w", [P, 3 * ML_T, 2 * ML_HEADS])
    gate_b = sb("gate_b", [P, 2 * ML_HEADS])
    ada_gb = sb("ada_gb", [8, CHUNK])
    over = sb("over", [1, 1], mybir.dt.int32)
    router = sb("router", [P, KD, EXPERTS])
    mod_col = sb("mod_col", [P, DEPTH, 6, KD])
    gate_dram = nc.dram_tensor("gate_rows", [4, D], F32, kind="Internal").ap()

    ARENA = 17400
    arena = sb("arena", [P, ARENA])

    class Carve:

        def __init__(self, start=0, end=ARENA, of=None):
            self.at, self.end, self.of = start, end, arena if of is None else of

        def take(self, *dims, parts=P):
            n = int(np.prod(dims))
            v = self.of[0:parts, self.at:self.at + n]
            self.at += n
            assert self.at <= self.end, (self.at, self.end)
            if len(dims) == 1:
                return v
            names = "abcd"[:len(dims)]
            return v.rearrange(f"p ({' '.join(names)}) -> p {' '.join(names)}", **dict(zip(names[1:], dims[1:])))

    ring_landed = [sem(f"ring_landed{i}") for i in range(SLOTS + 1)]
    ring_freed = [sem(f"ring_freed{i}") for i in range(SLOTS + 1)]
    x_landed, consts_landed, params_landed = sem("x_landed"), sem("consts_landed"), sem("params_landed")
    params_clear = sem("params_clear")
    param_rows = sem("param_rows")
    param_cols = sem("param_cols")
    param_ready = sem("param_ready")
    dve_step, act_step, pool_step = sem("dve_step"), sem("act_step"), sem("pool_step")
    lnp_landed = sem("lnp_landed")
    acc_done = sem("acc_done")
    var_ready, std_ready = sem("var_ready"), sem("std_ready")
    scaled, x_ready = sem("scaled"), sem("x_ready")
    x_turned, xT_ready = sem("x_turned"), sem("xT_ready")
    up_done, act_ready, h_ready = sem("up_done"), sem("act_ready"), sem("h_ready")
    h_turned, hT_ready = sem("h_turned"), sem("hT_ready")
    ada_ready, mod_done, mod_ready, gate_row_ready, gate_stored = (
        sem("ada_ready"), sem("mod_done"), sem("mod_ready"), sem("gate_row_ready"), sem("gate_stored"))
    s5_landed = sem("s5_landed")
    route_done, routed, route_exp = sem("route_done"), sem("routed"), sem("route_exp")
    chosen, ranked, over_ready = sem("chosen"), sem("ranked"), sem("over_ready")
    pick_ready, gathered, xg_ready = sem("pick_ready"), sem("gathered"), sem("xg_ready")
    spread_ready, spread_turned, spread_copied = sem("spread_ready"), sem("spread_turned"), sem("spread_copied")
    half_done, half_copied, scattered = sem("half_done"), sem("half_copied"), sem("scattered")
    moe_added = sem("moe_added")
    out_stored = sem("out_stored")
    NPARAM = [0]

    mixP = Events(sem("mix_pe"), ["q0", "q1", "kcvc", "vs", "kskw", "vwgl", "cmp1", "u", "gqk", "gv", "ga", "gr", "pre",
                                  "cmp2", "pool1", "kdT", "pool2", "dS", "at", "gla0", "gla1", "sc", "s0", "pcT", "oc0",
                                  "oc1", "s1", "t0", "s2", "v0", "t1", "s3", "v1", "t2", "s4", "v2", "t3", "s5", "v3",
                                  "t4", "s6", "v4", "t5", "s7", "v5", "t6", "v6", "t7", "v7", "oA0", "oA1", "oC", "wo0"])
    mixA = Events(sem("mix_act"), ["q0", "q1", "vs", "kskw", "vw", "gates", "g1", "ga", "sr", "abs", "ex", "ln1", "pool1",
                                   "eb", "enb", "ekd", "kdT", "pool2", "sq0", "sq1", "ss_std", "pc_exp", "pcT", "e0", "e1",
                                   "pT0", "e2", "pT1", "e3", "pT2", "e4", "pT3", "e5", "pT4", "e6", "pT5", "e7", "pT6",
                                   "pT7", "oT"])
    mixV = Events(sem("mix_dve"), ["zc", "u", "gqk", "gv", "g1rep", "gl_v", "gl_b", "gl_dd", "kcT", "vblk", "gl_kd",
                                   "s_blk", "at", "ss", "pc_bias", "pc_sub", "oC0", "oC1", "pc", "p0", "m0", "oc0", "oc1",
                                   "p1", "m1", "p2", "m2", "ot0_0", "oA0_0", "p3", "m3", "p4", "m4", "ot1_0", "oA1_0",
                                   "p5", "m5", "p6", "m6", "ot0_1", "oA0_1", "p7", "m7", "ot1_1", "oA1_1"])
    mixG = Events(sem("mix_pool"), ["zeros", "sr"])

    eight = range(8)
    mlP = Events(sem("ml_pe"), [f"in{j}" for j in range(16)] + [f"v{j}" for j in eight] + [f"vT{j}" for j in eight] +
                 [f"q{j}" for j in eight] + [f"k{j}" for j in eight] +
                 ["gates", "F", "abc", "S0", "S1", "T0", "n0", "n1", "n2", "n3", "T1", "n4", "n5", "n6", "n7"] +
                 [f"h{j}" for j in eight] + ["wo0", "wo1", "wo2"])
    mlA = Events(sem("ml_act"), [f"in{j}" for j in eight] + [f"{n}" for j in eight for n in (f"in{8 + j}", f"xc{j}")] +
                 [f"{n}{j}" for n in ("vT", "q", "k") for j in eight] +
                 ["abs", "ex", "ln1", "skip", "E0", "E1", "em", "T0", "T1", "hstd"])
    mlV = Events(sem("ml_dve"), ["bd_v"] + [f"conv{j}" for j in eight] + ["bd_q"] + [f"v{j}" for j in eight] +
                 ["bd_k", "gts", "logf", "diag", "am0", "am1", "m0", "m1", "sd0", "sd1"] + [f"h{j}" for j in eight] +
                 ["h_mv", "hn"] + [f"hs{j}" for j in eight])
    mlG = Events(sem("ml_pool"), [f"y{j}" for j in eight])

    s5P = Events(sem("s5_pe"), [f"bt{i}" for i in range(4)] + ["bu0", "ct0"] +
                 [n for k in range(1, 8) for n in (f"bu{k}", f"ct{k}", f"y{k - 1}")] + ["y7"] + [f"glu{i}" for i in range(4)])
    s5A = Events(sem("s5_act"), ["dt", "mag", "abs", "cos"] + [f"bt{i}" for i in range(4)] +
                 [n for k in eight for n in (f"abs{k}", f"rot{k}") + (("gelu0",) if k == 4 else ())] + ["gelu1"] +
                 [f"sig{i}" for i in range(4)])
    s5V = Events(sem("s5_dve"), ["lam_dt", "turn", "b_wide", "w0", "scan0", "ct0"] +
                 [n for k in range(1, 8) for n in (f"w{k}", f"scan{k}", f"ct{k}", f"y{k - 1}")] + ["y7"])
    s5G = Events(sem("s5_pool"), ["angle0", "angle1"] +
                 [n for k in eight for n in (f"x{k}",) + ((f"angle{k + 2}",) if k < 6 else ())])

    rg = Ring(ring_freed)
    ACC_AFTER = {0: 1, 1: 3, 2: 4, 3: 6, 4: 8, "moe": 9}
    PN = {}

    def plan_ffn(key, ada):
        for c in range(NC):
            if c < NC - 1:
                PN[key, "g", c] = rg.take()
                PN[key, "u", c] = rg.take()
            else:
                PN[key, "g", c] = PN[key, "u", c] = rg.take(dmas=2)
            if ada:
                PN[key, "ada", c] = rg.take(over=(ada_ready, key * NC + c + 1))
        for c in range(NC - 1):
            PN[key, "d", c] = rg.take()
        PN[key, "d", NC - 1] = rg.take(TAIL, over=(acc_done, ACC_AFTER[key]))

    STRIDE = {}
    for st in stages:
        if st.startswith("ffn"):
            plan_ffn(int(st[3:]), int(st[3:]) < 4)
        elif st.startswith("mix"):
            l = int(st[3:])
            for i in range(len(IN_PANELS)):
                if i == 3:
                    PN["mix", l, "w1"] = rg.take(dmas=4, over=mixP.after("cmp1", l))
                last_use = ("q1", "vs", "vwgl", "gqk", "ga", "gr")[i]
                PN["mix", l, "in", i] = rg.take(dmas=HEADS if i == 0 else 1, over=mixP.after(last_use, l))
            PN["mix", l, "out", 0] = rg.take(over=mixP.after("wo0", l))
            PN["mix", l, "out", 1] = rg.take(over=(acc_done, 2 + 3 * l))
        elif st == "mlstm":
            for i in range(8):
                PN["ml", "in", i] = rg.take(over=mlP.after(f"in{2 * i + 1}"))
            for name, last_use in (("q", "S1"), ("h", "h7"), ("s", "n7")):
                PN["ml", "scratch_" + name] = rg.take(dmas=0, over=mlP.after(last_use))
            for i in range(4):
                PN["ml", "out", i] = rg.take(over=mlP.after(f"wo{i}") if i < 3 else (acc_done, 7))
        elif st == "s5":
            for name in "sx":
                PN["s5", "scratch_" + name] = rg.take(dmas=0, over=s5P.after("y7") if name == "x" else s5G.after("x7"))
            for i in range(4):
                PN["s5", "glu", i] = rg.take()
        elif st == "moe":
            before = list(rg.uses), list(rg.landed)
            plan_ffn("moe", False)
            STRIDE["uses"] = [b - a for a, b in zip(before[0], rg.uses)]
            STRIDE["uses"][TAIL] = 1
            STRIDE["landed"] = [b - a for a, b in zip(before[1], rg.landed)]

    def slot_of(pn):
        return tail if pn.slot == TAIL else ring[:, pn.slot, :]

    def landed(pn, e=None):
        n = pn.landed if e is None else e * STRIDE["landed"][pn.slot] + pn.landed
        return ring_landed[pn.slot], n

    def panel(pn, k, w, first=0):
        return slot_of(pn)[:, first:first + k * w].rearrange("p (k w) -> p k w", w=w)

    def load_panel(sp, pn, pieces, e=None):
        if pn.before is not None:
            freed, n = pn.before
            sp.wait_ge(freed, n if e is None else e * STRIDE["uses"][pn.slot] + n)
        for dst, src in pieces:
            sp.dma_start(dst, src).then_inc(ring_landed[pn.slot], 16)

    def rows(w):
        return w.rearrange("(k p) n -> p k n", p=P)

    cols_a_at = dict(conv_w=0, conv_b=64, norm_w=80, skip=96, s5_d=112)
    cols_b_at = dict(ada_b=0, c=96, pool_scale=104, gla_ba=108)

    def start_sp(sp):
        sp.dma_start(consts[:, :], A["consts"]).then_inc(consts_landed, 16)
        sp.dma_start(x[:, :, :], A["x"].rearrange("b (t p) d -> p (b t) d", p=P)).then_inc(x_landed, 16)

    def start_act(act):
        def load(dst, src):
            act.dma_start(dst, src).then_inc(params_landed, 16)
            NPARAM[0] += 16

        load(cols_b_nat[0:96, :], A["ada_b_2"].rearrange("l (r p) -> (l r) p", p=P))
        load(cols_b_nat[96:104, :], A["c_2"].rearrange("b (r p) -> (b r) p", p=P))
        load(cols_b_nat[104:108, :], A["pool_scale"].rearrange("l (r p) -> (l r) p", p=P))
        load(cols_b_nat[108:110, :], A["gla_ba"])
        load(cols_a_nat[0:64, :], A["mlstm_conv_w_2"].rearrange("l k (r p) -> (l k r) p", p=P))
        load(cols_a_nat[64:80, :], A["mlstm_conv_b_2"].rearrange("l (r p) -> (l r) p", p=P))
        load(cols_a_nat[80:96, :], A["mlstm_norm_w_2"].rearrange("l (r p) -> (l r) p", p=P))
        load(cols_a_nat[96:112, :], A["mlstm_skip_2"].rearrange("l (r p) -> (l r) p", p=P))
        load(cols_a_nat[112:120, :], A["s5_d_2"].rearrange("l (r p) -> (l r) p", p=P))
        load(lam_nat[0:32, :], A["s5_lambda_re_2"].rearrange("l (s g) p -> (l s) (g p)", g=2))
        load(lam_nat[32:64, :], A["s5_lambda_im_2"].rearrange("l (s g) p -> (l s) (g p)", g=2))
        load(dt_nat[64:96, :], A["s5_log_dt_2"].rearrange("l (s g) -> (l s) g", g=2))
        for i in range(2):
            load(pe_nat[:, :, i, :], A["cmp_pe"].rearrange("l v j d -> j (l v) d"))
        act.wait_ge(params_clear, 2)
        for i in range(2):
            half = slice(i * HD, (i + 1) * HD)
            load(w2bd[half, :, half], A["cmp_w2"].rearrange("l v i o -> i (l v) o"))
            load(poolbd[half, :, half], A["pool_w"].rearrange("l (t h) i o -> h i (l t) o", h=2)[i])
        load(gla_wa2[:, :, :], A["gla_wa2"].rearrange("l r n -> r l n"))
        for l in range(DEPTH):
            load(gla_norm[:, l, :], A["gla_norm_g"][l].partition_broadcast(P))
        for i, name in enumerate(("mlstm_wq_2", "mlstm_wk_2", "mlstm_wv_2")):
            load(qkv_w[:, i, :, :], A[name][0].rearrange("(t n) i o -> (n i) t o", n=P // QKV_BLOCK))
        load(gate_w[:, :, :], rows(A["mlstm_w_gates_2"][0]))
        load(gate_b[:, :], A["mlstm_b_gates_2"][0].partition_broadcast(P))
        ada_b = A["ada_b_2"].rearrange("l (v r n) -> l v r n", v=6, n=CHUNK)
        for l in range(DEPTH):
            for w in range(2):
                load(ada_gb[4 * l + 2 * w:4 * l + 2 * w + 2, :], ada_b[l, 2 + 3 * w])
        load(router[:, :, :], rows(A["moe_router_2"][0]))

        act.wait_ge(param_cols, 4)
        act.copy(cols_a[:, :], psum[:, 4, 0:120]).then_inc(param_ready, 1)
        act.copy(cols_b[:, :], psum[:, 5, 0:110]).then_inc(param_ready, 1)
        act.copy(lam[:, :], psum[:, 6, 0:96]).then_inc(param_ready, 1)
        act.copy(pe_col[:, :, :], psum[:, 7, 0:4 * CMP_BLOCK].rearrange("p (v j) -> p v j", v=4)).then_inc(param_ready, 1)
        act.wait_ge(param_ready, 4)
        act.activation(cond[:, :], cols_b[:, 96:104], ACT.Silu).then_inc(param_ready, 1)

    def start_pool(pool):
        pool.memset(w2bd[:, :, :], 0.0).then_inc(params_clear, 1)
        pool.memset(poolbd[:, :, :], 0.0).then_inc(params_clear, 1)

    def start_dve(dve):
        dve.memset(eps[:, 0:1], 4.0 * LN_EPS)
        dve.memset(eps[:, 1:2], LN_EPS)
        dve.memset(eps[:, 3:4], np.pi / 2)
        dve.memset(eps[:, 2:3], RMS_EPS).then_inc(param_rows, 1)
        dve.wait_ge(params_landed, NPARAM[0])
        dve.tensor_copy(lam_nat[64:96, :].rearrange("s (g p) -> s g p", g=2),
                        dt_nat[64:96, :].unsqueeze(2).to_broadcast([32, 2, S5_P])).then_inc(param_rows, 1)

    def start_pe(pe):
        pe.wait_ge(consts_landed, 16)
        pe.wait_ge(x_landed, 16)
        turn_x(pe, 0)
        pe.wait_ge(params_landed, NPARAM[0])
        pe.wait_ge(param_rows, 2)
        pe.transpose(psum[:, 4, 0:120], cols_a_nat[0:120, :], ident[0:120, 0:120]).then_inc(param_cols, 1)
        pe.transpose(psum[:, 5, 0:110], cols_b_nat[0:110, :], ident[0:110, 0:110]).then_inc(param_cols, 1)
        pe.transpose(psum[:, 6, 0:96], lam_nat[:, :], ident[0:96, 0:96]).then_inc(param_cols, 1)
        for v in range(4):
            last = pe.transpose(psum[:, 7, v * CMP_BLOCK:(v + 1) * CMP_BLOCK],
                                pe_nat[:, v, :, :].rearrange("j a d -> j (a d)"), ident[0:CMP_BLOCK, 0:CMP_BLOCK])
        last.then_inc(param_cols, 1)

    def turn_x(pe, q):
        for t in range(NT):
            if q > 0:
                pe.wait_ge(x_ready, NT * (q - 1) + t + 1)
            for b in range(2):
                for k in range(4):
                    last = pe.transpose(psum[:, 2 * t + b, k * P:(k + 1) * P],
                                        x[:, t, (4 * b + k) * P:(4 * b + k + 1) * P], ident)
                last.then_inc(x_turned, 1)

    def copy_xT_act(act, q):
        for i in range(2 * NT):
            t, b = divmod(i, 2)
            act.wait_ge(x_turned, 4 * q + i + 1)
            act.copy(xT[:, 4 * b:4 * b + 4, t * P:(t + 1) * P],
                     psum[:, i, :].rearrange("p (k n) -> p k n", k=4)).then_inc(xT_ready, 1)

    def copy_xT_dve(dve, q):
        l, w = divmod(q - 6, 2)
        dve.wait_ge(mod_ready, 24)
        for i in range(2 * NT):
            t, b = divmod(i, 2)
            dve.wait_ge(x_turned, 4 * q + i + 1)
            for k in range(4):
                last = dve.tensor_scalar(xT[:, 4 * b + k, t * P:(t + 1) * P], psum[:, i, k * P:(k + 1) * P],
                                         mod_col[:, l, 3 * w + 1, 4 * b + k:4 * b + k + 1],
                                         mod_col[:, l, 3 * w, 4 * b + k:4 * b + k + 1], ALU.mult, ALU.add)
            last.then_inc(xT_ready, 1)

    def wait_xT(pe, q):
        pe.wait_ge(xT_ready, 4 * q + 4)

    def ln_pool(pool, m):
        if m > 0:
            pool.wait_ge(scaled, NT * m)
            pool.wait_ge(x_ready, NT * m)
        if m < 6:
            g, b = A["ln_g"][m // 3, m % 3], A["ln_b"][m // 3, m % 3]
        else:
            which = "ffn" if m % 2 else "mix"
            g, b = A[f"ln_{which}_g_2"][(m - 6) // 2], A[f"ln_{which}_b_2"][(m - 6) // 2]
        pool.dma_start(lnp[:, 0, :], g.partition_broadcast(P)).then_inc(lnp_landed, 16)
        pool.dma_start(lnp[:, 1, :], b.partition_broadcast(P)).then_inc(lnp_landed, 16)
        if m >= 6:
            pool.wait_ge(gate_stored, 16 * 8)
            pool.dma_start(lnp[:, 2, :], gate_dram[m - 6].partition_broadcast(P)).then_inc(lnp_landed, 16)

    def lnp_count(m):
        return 16 * (2 * (m + 1) + max(0, m - 5))

    def ln_pool_add(pool, m):
        pool.wait_ge(lnp_landed, lnp_count(m))
        for t in range(NT):
            pool.wait_ge(scaled, NT * m + t + 1)
            pool.wait_ge(x_turned, 4 * m + 4)
            if t == 0 and m < 6:
                pool.wait_ge(gate_stored, 16 * 2 * (1, 1, 2, 3, 3, 4)[m])
            pool.tensor_tensor(x[:, t, :], z[:, t, :], lnp[:, 1, :], ALU.add).then_inc(x_ready, 1)

    def ln_dve(dve, step, m, source, ready):
        half = m in (0, 2, 3, 5)
        dve.wait_ge(*ready)
        if m >= 6:
            dve.wait_ge(lnp_landed, lnp_count(m))
        for t in range(NT):
            y = source(t)
            if m >= 6:
                dve.tensor_tensor(z[:, t, :], y, lnp[:, 2, :], ALU.mult).then_inc(*step.one())
                dve.wait_ge(*step.now())
                y = z[:, t, :]
            dve.scalar_tensor_tensor(z[:, t, :], x[:, t, :], 2 * ALPHA if half else ALPHA, y, ALU.mult,
                                     ALU.add).then_inc(*step.one())
            dve.wait_ge(*step.now())
            for i in range(2):
                dve.bn_stats(bn[:, t, i, :], z[:, t, i * 512:(i + 1) * 512]).then_inc(*step.one())
            dve.wait_ge(*step.now())
            dve.bn_aggr(mv[:, t, :], bn[:, t, :, :].rearrange("p a b -> p (a b)")).then_inc(var_ready, 1)
        for t in range(NT):
            dve.wait_ge(std_ready, NT * m + t + 1)
            dve.reciprocal(rstd[:, t:t + 1], std[:, t:t + 1]).then_inc(*step.one())
            dve.wait_ge(*step.now())
            dve.tensor_scalar(z[:, t, :], z[:, t, :], mv[:, t, 0:1], rstd[:, t:t + 1], ALU.subtract,
                              ALU.mult).then_inc(*step.one())
            dve.wait_ge(*step.now())
            dve.wait_ge(lnp_landed, lnp_count(m))
            dve.tensor_tensor(z[:, t, :], z[:, t, :], lnp[:, 0, :], ALU.mult).then_inc(scaled, 1)

    def ln_act(act, m):
        half = m in (0, 2, 3, 5)
        if m == 0:
            act.wait_ge(param_rows, 1)
        for t in range(NT):
            act.wait_ge(var_ready, NT * m + t + 1)
            act.activation(std[:, t:t + 1], mv[:, t, 1:2], ACT.Sqrt,
                           bias=eps[:, 0:1] if half else eps[:, 1:2]).then_inc(std_ready, 1)

    def acc(t, half=None):
        if half is None:
            return psum[:, 4 + 2 * t:6 + 2 * t, :].rearrange("p b n -> p (b n)")
        return psum[:, 4 + 2 * t + half, :]

    cv = Carve()
    hT = cv.take(FT, SEQ)
    act_g = cv.take(2, CHUNK)
    h = cv.take(2, CHUNK)
    ada_acc = cv.take(CHUNK)
    y_sum = cv.take(NT, D)
    gate_row = cv.take(2, CHUNK)
    expert_gate = cv.take(NT, EXPERTS)
    route = cv.take(NT, 128)
    ARENA_FFN = cv.at

    def ffn_sp(sp, key, wg, wu, wd, e=None):
        for c, (c0, w) in enumerate(CHUNKS):
            pg, pu = PN[key, "g", c], PN[key, "u", c]
            if c < NC - 1:
                load_panel(sp, pg, [(panel(pg, KD, w), rows(wg)[:, :, c0:c0 + w])], e)
                load_panel(sp, pu, [(panel(pu, KD, w), rows(wu)[:, :, c0:c0 + w])], e)
            else:
                load_panel(sp, pg, [(panel(pg, KD, w), rows(wg)[:, :, c0:c0 + w]),
                                    (panel(pg, KD, w, KD * w), rows(wu)[:, :, c0:c0 + w])], e)
            if (key, "ada", c) in PN:
                l, a = divmod(key * NC + c, 12)
                pa = PN[key, "ada", c]
                load_panel(sp, pa, [(panel(pa, KD, CHUNK), rows(A["ada_w_2"][l])[:, :, a * CHUNK:(a + 1) * CHUNK])])
        for c in range(NC):
            f0, f1 = 4 * c, min(4 * c + 4, FT)
            pd = PN[key, "d", c]
            load_panel(sp, pd, [(panel(pd, f1 - f0, D), rows(wd)[:, f0:f1, :])], e)

    def before_group(first, g, lag=2):
        v = first + (g - lag + 1)
        return v if not isinstance(v, int) or v > 0 else None

    def ffn_pe(pe, n, first, key, e=None, tiles=NT):
        groups = NC * tiles
        src = xT if tiles == NT else xg

        def up(c, t):
            g = tiles * c + t
            b = g % 2
            w = CHUNKS[c][1]
            pg, pu = PN[key, "g", c], PN[key, "u", c]
            if t == 0:
                pe.wait_ge(*landed(pg, e))
            v = before_group(first, g)
            if v is not None:
                pe.wait_ge(h_ready, v)
            last_chunk = c == NC - 1
            for k in range(KD):
                mm = pe.matmul(psum[:, 2 * b, 0:w], src[:, k, t * P:(t + 1) * P], panel(pg, KD, w)[:, k, :],
                               start=k == 0, stop=k == KD - 1)
                if k == 0 and tiles == 1 and c > 0:
                    mm.then_inc(ring_freed[PN[key, "u", c - 1].slot], 1)
            if t == tiles - 1 and not last_chunk:
                mm.then_inc(ring_freed[pg.slot], 1)
            if t == 0 and not last_chunk:
                pe.wait_ge(*landed(pu, e))
            for k in range(KD):
                mm = pe.matmul(psum[:, 2 * b + 1, 0:w], src[:, k, t * P:(t + 1) * P],
                               panel(pu, KD, w, KD * w if last_chunk else 0)[:, k, :],
                               start=k == 0, stop=k == KD - 1)
            mm.then_inc(up_done, 1)

        def turn(c, t):
            g = tiles * c + t
            b = g % 2
            bank = 4 + b if c < NC - 1 else 2 * b
            pe.wait_ge(h_ready, first + (g + 1))
            v = before_group(first, g)
            if v is not None:
                pe.wait_ge(hT_ready, v)
            for f in range(CHUNKS[c][1] // P):
                mm = pe.transpose(psum[:, bank, f * P:(f + 1) * P], h[:, b, f * P:(f + 1) * P], ident)
                if f == 0 and tiles == NT and t == 0:
                    mm.then_inc(ring_freed[PN[key, "u", c].slot], 1)
                if f == 0 and tiles == 1 and c == NC - 2:
                    mm.then_inc(ring_freed[PN[key, "u", c + 1].slot], 1)
            mm.then_inc(h_turned, 1)

        def mod(c):
            l, a = divmod(n * NC + c, 12)
            v, part = divmod(a, 2)
            i = n * NC + c
            pe.wait_ge(ada_ready, i + 1)
            if i > 0:
                pe.wait_ge(mod_ready, i)
            if v in (2, 5):
                row = 4 * l + 2 * (v // 3) + part
                pe.matmul(psum[0:1, 6, 0:CHUNK], ones[:, 0:1], ada_acc[:, :], start=True, stop=False)
                pe.matmul(psum[0:1, 6, 0:CHUNK], ident[0:8, row:row + 1], ada_gb[:, :],
                          start=False, stop=True).then_inc(mod_done, 1)
            else:
                for f in range(4):
                    mm = pe.matmul(psum[:, 6, f:f + 1], ada_acc[:, f * P:(f + 1) * P], ones[:, 0:1],
                                   start=True, stop=True)
                mm.then_inc(mod_done, 1)

        for c in range(NC):
            if tiles == 1:
                if c == 1:
                    pe.wait_ge(moe_added, e + 1)
                up(c, 0)
                if c == 2:
                    turn_spread(pe, e)
                if c > 0:
                    turn(c - 1, 0)
                continue
            up(c, 0)
            if c > 0:
                turn(c - 1, 1)
            up(c, 1)
            if (key, "ada", c) in PN:
                mod(c)
            if c == 0 and e is not None:
                pe.wait_ge(moe_added, e + 1)
            turn(c, 0)
        if (key, "ada", 0) in PN:
            pe.wait_ge(mod_ready, (n + 1) * NC)
        if tiles == 1:
            gather_pe(pe, e + 1)
        for c in range(NC):
            pd = PN[key, "d", c]
            if c == 1:
                turn(NC - 1, tiles - 1)
            f0, f1 = 4 * c, min(4 * c + 4, FT)
            pe.wait_ge(hT_ready, first + max(tiles * (c + 1), groups - tiles))
            pe.wait_ge(*landed(pd, e))
            down = [(f, t, half) for f in range(f0, f1) for t in range(tiles) for half in range(2)]
            if tiles == 1 and c == NC - 1:
                down.sort(key=lambda fth: fth[2])
            for f, t, half in down:
                mm = pe.matmul(acc(t, half), hT[:, f, t * P:(t + 1) * P],
                               panel(pd, f1 - f0, D)[:, f - f0, half * 512:(half + 1) * 512],
                               start=f == 0, stop=f == FT - 1)
                if tiles == 1 and f == FT - 1 and half == 0:
                    mm.then_inc(half_done, 1)
            mm.then_inc(*((ring_freed[pd.slot], 1) if c < NC - 1 else (acc_done, 1)))

    def ffn_act(act, first, tiles=NT, e=None):
        for c, (_, w) in enumerate(CHUNKS):
            for t in range(tiles):
                g = tiles * c + t
                v = before_group(first, g)
                if v is not None:
                    act.wait_ge(h_ready, v)
                act.wait_ge(up_done, first + (g + 1))
                act.activation(act_g[:, g % 2, 0:w], psum[:, 2 * (g % 2), 0:w], ACT.Silu).then_inc(act_ready, 1)
                if tiles == 1 and c == 3:
                    copy_spread(act, e)
                if g > 0:
                    copy_h(act, first, g - 1, tiles)
        copy_h(act, first, NC * tiles - 1, tiles)

    def copy_h(act, first, g, tiles):
        c, t = divmod(g, tiles)
        bank = 4 + g % 2 if c < NC - 1 else 2 * (g % 2)
        nf = CHUNKS[c][1] // P
        act.wait_ge(h_turned, first + (g + 1))
        act.copy(hT[:, 4 * c:4 * c + nf, t * P:(t + 1) * P],
                 psum[:, bank, 0:nf * P].rearrange("p (f n) -> p f n", f=nf)).then_inc(hT_ready, 1)

    def ffn_dve(dve, step, n, first, key, tiles=NT):
        for c, (_, w) in enumerate(CHUNKS):
            for t in range(tiles):
                g = tiles * c + t
                b = g % 2
                v = before_group(first, g)
                if v is not None:
                    dve.wait_ge(h_turned, v)
                dve.wait_ge(act_ready, first + (g + 1))
                dve.tensor_tensor(h[:, b, 0:w], act_g[:, b, 0:w], psum[:, 2 * b + 1, 0:w], ALU.mult)\
                   .then_inc(h_ready, 1)
                if t == 0 and (key, "ada", c) in PN:
                    ada(dve, step, n, key, c)
            if (key, "ada", c) in PN:
                mod_out(dve, n, c)

    def ada(dve, step, n, key, c):
        pa = PN[key, "ada", c]
        i = n * NC + c
        if i == 0:
            dve.wait_ge(param_ready, 5)
        if i > 0:
            dve.wait_ge(mod_done, i)
        dve.wait_ge(*landed(pa))
        for k in range(KD):
            src = panel(pa, KD, CHUNK)[:, k, :]
            if k == 0:
                ins = dve.tensor_scalar(ada_acc[:, :], src, cond[:, k:k + 1], None, ALU.mult)
            else:
                ins = dve.scalar_tensor_tensor(ada_acc[:, :], src, cond[:, k:k + 1], ada_acc[:, :], ALU.mult, ALU.add)
            if k < KD - 1:
                ins.then_inc(*step.one())
                dve.wait_ge(*step.now())
            else:
                ins.then_inc(ada_ready, 1)

    def mod_out(dve, n, c):
        l, a = divmod(n * NC + c, 12)
        v, part = divmod(a, 2)
        i = n * NC + c
        dve.wait_ge(mod_done, i + 1)
        if v in (2, 5):
            j = 2 * (2 * l + v // 3) + part
            if j >= 2:
                dve.wait_ge(gate_stored, 16 * (j - 1))
            dve.tensor_scalar(gate_row[0:1, j % 2, :], psum[0:1, 6, 0:CHUNK], 1.0, None, ALU.add).then_inc(mod_ready, 1)
        else:
            bias = cols_b[:, l * 48 + a * 4:l * 48 + a * 4 + 4]
            dve.scalar_tensor_tensor(mod_col[:, l, v, part * 4:part * 4 + 4], psum[:, 6, 0:4],
                                     1.0 if v in (1, 4) else 0.0, bias, ALU.add, ALU.add).then_inc(mod_ready, 1)

    def gate_pool(pool, n):
        for c in range(NC):
            i = n * NC + c
            l, a = divmod(i, 12)
            v, part = divmod(a, 2)
            if v in (2, 5):
                j = 2 * (2 * l + v // 3) + part
                pool.wait_ge(mod_ready, i + 1)
                pool.dma_start(gate_dram[j // 2:j // 2 + 1, part * CHUNK:(part + 1) * CHUNK],
                               gate_row[0:1, j % 2, :]).then_inc(gate_stored, 16)

    cv = Carve()
    qT = cv.take(REP, SEQ)
    kT = cv.take(2, SEQ)
    vv = cv.take(2, NT, P)
    gates = cv.take(NT, 3 * HEADS)
    zc = cv.take(2, 2, SEQ)
    g1 = cv.take(2, CMP_STRIDE)
    g1rep = cv.take(HEADS, CMP_STRIDE)
    kcT = cv.take(CMP_STRIDE)
    vblk = cv.take(HEADS, HD)
    u_sb = cv.take(NT, 256)
    gqk = cv.take(2, SEQ)
    gv = cv.take(NT, GLA_H * GLA_V)
    gaT = cv.take(SEQ)
    sr = cv.take(NT, GLA_H * GLA_V)
    gl_min, gl_abs, gl_b, gl_eb, gl_enb, gl_ekd = (cv.take(SEQ) for _ in range(6))
    gl_q, gl_k, gl_kd = (cv.take(SEQ) for _ in range(3))
    kdT = cv.take(NT, P)
    s_blk = cv.take(4, GLA_H * GLA_V)
    at_sb = cv.take(GLA_H, NT, P)
    sq = cv.take(NT, GLA_H * GLA_V)
    ss = cv.take(NT, GLA_H)
    ss_std = cv.take(NT, GLA_H)
    oC = cv.take(NT, GLA_H * GLA_V)
    pooledT = cv.take(2, SEQ)
    oA = cv.take(NT, HEADS * HD)
    o_tmp = cv.take(HEADS * HD)
    pT = cv.take(2, 2 * REP, P)
    pc = cv.take(NT, HEADS, CMP_STRIDE)
    pc_max = cv.take(NT * HEADS)
    pc_sum = cv.take(NT * HEADS)
    pcT = cv.take(NT, P)
    nmax = cv.take(8, REP)
    rsum = cv.take(8, REP)
    o_w = cv.take(2, HEADS)
    p_sb = z[:, :, :]
    oT = xT

    UNITS = [(t, b, g) for t in range(NT) for b in range(2) for g in range(GROUPS)]

    def bank(i):
        return psum[:, i, :]

    def mix_sp(sp, l):
        w = rows(A["w_in"][l])
        for i, (c0, n) in enumerate(IN_PANELS):
            if i == 3:
                pn = PN["mix", l, "w1"]
                dst = slot_of(pn).rearrange("p (v j o) -> p v j o", v=2, o=HD)
                load_panel(sp, pn, [(dst[d * HD:(d + 1) * HD, v], A["cmp_w1"][l, v].rearrange("(j d) o -> d j o", d=HD))
                                    for v in range(2) for d in range(2)])
            pn = PN["mix", l, "in", i]
            if i == 0:
                dst = panel(pn, KD, n).rearrange("p k (r g d) -> p k r g d", r=REP, g=GROUPS)
                src = w[:, :, 0:n].rearrange("p k (g r d) -> p k g r d", g=GROUPS, r=REP)
                load_panel(sp, pn, [(dst[:, :, r, g, :], src[:, :, g, r, :]) for r in range(REP) for g in range(GROUPS)])
            else:
                load_panel(sp, pn, [(panel(pn, KD, n), w[:, :, c0:c0 + n])])
        for i in range(2):
            pn = PN["mix", l, "out", i]
            load_panel(sp, pn, [(panel(pn, KD, CHUNK), rows(A["w_out"][l])[:, :, i * CHUNK:(i + 1) * CHUNK])])

    def mix_pe(pe, l):
        def features(dst, pn, w, first, m):
            for k in range(KD):
                mm = pe.matmul(dst, panel(pn, KD, w)[:, k, first:first + m], xT[:, k, :], start=k == 0, stop=k == KD - 1)
            return mm

        def tokens(dst, pn, w, first, m, t):
            for k in range(KD):
                mm = pe.matmul(dst, xT[:, k, t * P:(t + 1) * P], panel(pn, KD, w)[:, k, first:first + m],
                               start=k == 0, stop=k == KD - 1)
            return mm

        pn = [PN["mix", l, "in", i] for i in range(len(IN_PANELS))]
        pe.wait_ge(*landed(pn[0]))
        for r in range(REP):
            mm = features(bank(r // 2)[:, (r % 2) * SEQ:(r % 2 + 1) * SEQ], pn[0], 512, r * P, P)
            if r % 2:
                mm.then_inc(*mixP.inc(f"q{r // 2}", l))
        pe.wait_ge(*landed(pn[1]))
        features(bank(2)[:, 0:SEQ], pn[1], 512, 0, P)
        features(bank(2)[:, SEQ:2 * SEQ], pn[1], 512, 128, P).then_inc(*mixP.inc("kcvc", l))
        features(bank(3)[:, 0:SEQ], pn[1], 512, 256, P)
        for t in range(NT):
            mm = tokens(bank(4)[:, t * P:(t + 1) * P], pn[1], 512, 384, P, t)
        mm.then_inc(*mixP.inc("vs", l))
        pe.wait_ge(*landed(pn[2]))
        features(bank(3)[:, SEQ:2 * SEQ], pn[2], 280, 0, P).then_inc(*mixP.inc("kskw", l))
        for t in range(NT):
            mm = tokens(bank(5)[:, t * 256:t * 256 + 152], pn[2], 280, 128, 152, t)
        mm.then_inc(*mixP.inc("vwgl", l))

        w1 = PN["mix", l, "w1"]
        pe.wait_ge(*landed(w1))
        pe.wait_ge(*mixV.after("zc", l))
        w1v = slot_of(w1).rearrange("p (v j o) -> p v j o", v=2, o=HD)
        for v in range(2):
            for j in range(CMP_BLOCK):
                half, pos = divmod(j, CMP_STRIDE)
                for g in range(GROUPS):
                    part = slice(g * HD, (g + 1) * HD)
                    src = zc[part, v, half, :].rearrange("p (c j) -> p c j", j=CMP_STRIDE)[:, half:half + N_CMP, pos]
                    mm = pe.matmul(bank(6 + g)[part, v * CMP_STRIDE:v * CMP_STRIDE + N_CMP], w1v[part, v, j, :], src,
                                   start=j == 0, stop=j == CMP_BLOCK - 1)
        mm.then_inc(*mixP.inc("cmp1", l))

        pe.wait_ge(*landed(pn[3]))
        pe.wait_ge(*mixA.after("q0", l))
        for t in range(NT):
            mm = tokens(bank(0)[:, t * 256:(t + 1) * 256], pn[3], 512, 0, 256, t)
        mm.then_inc(*mixP.inc("u", l))
        pe.wait_ge(*mixA.after("q1", l))
        features(bank(1)[:, 0:SEQ], pn[3], 512, 256, P)
        features(bank(1)[:, SEQ:2 * SEQ], pn[3], 512, 384, P).then_inc(*mixP.inc("gqk", l))
        pe.wait_ge(*landed(pn[4]))
        for t in range(NT):
            mm = tokens(bank(2)[:, t * 256:(t + 1) * 256], pn[4], 272, 0, 256, t)
        mm.then_inc(*mixP.inc("gv", l))
        pe.wait_ge(*mixA.after("kskw", l))
        features(bank(3)[0:16, 0:SEQ], pn[4], 272, 256, 16).then_inc(*mixP.inc("ga", l))
        pe.wait_ge(*landed(pn[5]))
        pe.wait_ge(*mixA.after("vs", l))
        for t in range(NT):
            mm = tokens(bank(4)[:, t * 256:(t + 1) * 256], pn[5], 256, 0, 256, t)
        mm.then_inc(*mixP.inc("gr", l))

        pe.wait_ge(*mixA.after("g1", l))
        pe.wait_ge(*mixA.after("ga", l))
        pe.matmul(bank(6)[:, 0:SEQ], gla_wa2[:, l, :], gaT[0:16, :], start=True, stop=True).then_inc(*mixP.inc("pre", l))
        pe.wait_ge(*mixA.after("gates", l))
        pe.matmul(bank(5)[:, 0:CMP_STRIDE], w2bd[:, 2 * l, :], g1[:, 0, :], start=True, stop=True)
        pe.wait_ge(*mixV.after("g1rep", l))
        pe.matmul(bank(5)[:, P:2 * P], g1rep[:, :, :].rearrange("p h n -> p (h n)"), w2bd[:, 2 * l + 1, :],
                  start=True, stop=True).then_inc(*mixP.inc("cmp2", l))
        pe.wait_ge(*mixV.after("u", l))
        pe.wait_ge(*mixV.after("gqk", l))
        bands = const("bands").rearrange("p (w t) -> p w t", t=SEQ + P)
        for i in range(len(POOL_WINDOWS)):
            dst = bank(i // 2)[:, (i % 2) * SEQ:(i % 2 + 1) * SEQ]
            cols = slice((i // 2) * P, (i // 2 + 1) * P)
            pe.matmul(dst[:, 0:P], u_sb[:, 0, cols], bands[:, i, 0:P], start=True, stop=True)
            pe.matmul(dst[:, P:SEQ], u_sb[:, 0, cols], bands[:, i, P:SEQ], start=True, stop=False)
            mm = pe.matmul(dst[:, P:SEQ], u_sb[:, 1, cols], bands[:, i, SEQ:SEQ + P], start=False, stop=True)
        mm.then_inc(*mixP.inc("pool1", l))

        pe.wait_ge(*mixV.after("gl_kd", l))
        for t in range(NT):
            mm = pe.transpose(bank(3)[:, t * P:(t + 1) * P], gl_kd[:, t * P:(t + 1) * P], ident)
        mm.then_inc(*mixP.inc("kdT", l))
        pe.wait_ge(*mixA.after("pool1", l))
        for i in range(2):
            mm = pe.matmul(bank(7)[:, i * SEQ:(i + 1) * SEQ], poolbd[:, 2 * l + i, :], pooledT[:, i, :],
                           start=True, stop=True)
        mm.then_inc(*mixP.inc("pool2", l))
        pe.wait_ge(*mixA.after("kdT", l))
        pe.wait_ge(*mixV.after("gv", l))
        pe.wait_ge(*mixA.after("sr", l))
        pe.wait_ge(*mixV.after("vblk", l))
        for n in range(3):
            part = slice((n % 2) * GLA_CHUNK, (n % 2 + 1) * GLA_CHUNK)
            mm = pe.matmul(bank(4 + n % 2)[:, (n // 2) * 256:(n // 2 + 1) * 256], kdT[part, n // 2, :], gv[part, n // 2, :],
                           start=True, stop=True)
        mm.then_inc(*mixP.inc("dS", l))
        for t in range(NT):
            for hh in range(GLA_H):
                part = slice(hh * GLA_K, (hh + 1) * GLA_K)
                mm = pe.matmul(bank(hh)[:, t * P:(t + 1) * P], gl_k[part, t * P:(t + 1) * P], gl_q[part, t * P:(t + 1) * P],
                               start=True, stop=True)
        mm.then_inc(*mixP.inc("at", l))
        pe.wait_ge(*mixV.after("s_blk", l))
        pe.wait_ge(*mixV.after("at", l))
        pe.wait_ge(*mixV.after("gl_v", l))
        pe.wait_ge(*mixA.after("pool2", l))
        for t in range(NT):
            for n in (2 * t, 2 * t + 1):
                part = slice((n % 2) * GLA_CHUNK, (n % 2 + 1) * GLA_CHUNK)
                pe.matmul(bank(6 + t)[part, 0:256], gl_q[:, n * GLA_CHUNK:(n + 1) * GLA_CHUNK], s_blk[:, n, :],
                          start=True, stop=True)
            for hh in range(GLA_H):
                mm = pe.matmul(bank(6 + t)[:, hh * GLA_V:(hh + 1) * GLA_V], at_sb[:, hh, t, :],
                               gv[:, t, hh * GLA_V:(hh + 1) * GLA_V], start=False, stop=True, skip_group_check=True)
            mm.then_inc(*mixP.inc(f"gla{t}", l))

        pe.wait_ge(*mixV.after("kcT", l))
        for t in range(NT):
            for r in range(REP):
                for g in range(GROUPS):
                    part = slice(g * HD, (g + 1) * HD)
                    at = (t * REP + r) * CMP_STRIDE
                    mm = pe.matmul(bank(g)[:, at:at + CMP_STRIDE], qT[part, r, t * P:(t + 1) * P], kcT[part, :],
                                   start=True, stop=True)
        mm.then_inc(*mixP.inc("sc", l))

        def scores(i):
            t, b, g = UNITS[i]
            nk = P * (t + 1)
            part = slice(g * HD, (g + 1) * HD)
            if i >= 2:
                pe.wait_ge(*mixV.after(f"p{i - 2}", l))
            else:
                pe.wait_ge(*mixV.after("pc_bias" if i == 0 else "at", l))
                pe.wait_ge(*mixV.after("pc_bias", l))
            dst = psum[:, 2 * (i % 2):2 * (i % 2) + 2, :].rearrange("p b n -> p (b n)")
            for r in range(REP):
                mm = pe.matmul(dst[:, r * nk:(r + 1) * nk], qT[part, r, t * P:(t + 1) * P], kT[part, b, 0:nk],
                               start=True, stop=True)
            mm.then_inc(*mixP.inc(f"s{i}", l))

        def turn_p(i):
            t, b, g = UNITS[i]
            pe.wait_ge(*mixA.after(f"e{i}", l))
            if i > 0:
                pe.wait_ge(*mixA.after(f"pT{i - 1}", l))
            else:
                pe.wait_ge(*mixV.after("oc1", l))
            dst = psum[:, 4:6, :].rearrange("p b n -> p (b n)")
            for j in range(REP * (t + 1)):
                mm = pe.transpose(dst[:, j * P:(j + 1) * P], p_sb[:, i % 2, j * P:(j + 1) * P], ident)
            mm.then_inc(*mixP.inc(f"t{i}", l))

        def values(i):
            t, b, g = UNITS[i]
            pe.wait_ge(*mixA.after(f"pT{i}", l))
            if g == 0:
                pe.wait_ge(*mixV.after(f"oC{b}" if t == 0 else f"oA{b}_{t - 1}", l))
            for r in range(REP):
                for kt in range(t + 1):
                    mm = pe.matmul(bank(6 + b)[:, (g * REP + r) * HD:(g * REP + r + 1) * HD], pT[:, i % 2, r * (t + 1) + kt, :],
                                   vv[:, b, kt, g * HD:(g + 1) * HD], start=kt == 0, stop=kt == t)
            mm.then_inc(*mixP.inc(f"v{i}", l))

        scores(0)
        pe.wait_ge(*mixV.after("pc", l))
        for t in range(NT):
            mm = pe.transpose(bank(3)[:, t * P:(t + 1) * P], pc[:, t, :, :].rearrange("p h n -> p (h n)"), ident)
        mm.then_inc(*mixP.inc("pcT", l))
        pe.wait_ge(*mixA.after("pcT", l))
        for t in range(NT):
            pe.matmul(bank(4 + t)[:, :], pcT[:, t, :], vblk[:, :, :].rearrange("p h d -> p (h d)"), start=True, stop=True)\
              .then_inc(*mixP.inc(f"oc{t}", l))
        scores(1)
        for i in range(len(UNITS)):
            turn_p(i)
            if i + 2 < len(UNITS):
                scores(i + 2)
            values(i)

        pe.wait_ge(*mixV.after("oA1_1", l))
        for t in range(NT):
            for j in range(4):
                mm = pe.transpose(bank(t)[:, j * P:(j + 1) * P], oA[:, t, j * P:(j + 1) * P], ident)
            mm.then_inc(*mixP.inc(f"oA{t}", l))
        for t in range(NT):
            for j in range(2):
                mm = pe.transpose(bank(2)[:, (2 * t + j) * P:(2 * t + j + 1) * P], oC[:, t, j * P:(j + 1) * P], ident)
        mm.then_inc(*mixP.inc("oC", l))
        pe.wait_ge(*mixA.after("oT", l))
        for i in range(2):
            po = PN["mix", l, "out", i]
            pe.wait_ge(*landed(po))
            for t in range(NT):
                for k in range(KD):
                    mm = pe.matmul(acc(t, i), oT[:, k, t * P:(t + 1) * P], panel(po, KD, CHUNK)[:, k, :],
                                   start=k == 0, stop=k == KD - 1)
            mm.then_inc(*(mixP.inc("wo0", l) if i == 0 else (acc_done, 1)))

    def mix_act(act, step, l):
        for i in range(2):
            act.wait_ge(*mixP.after(f"q{i}", l))
            act.mul(qT[:, 2 * i:2 * i + 2, :], bank(i).rearrange("p (r n) -> p r n", r=2), HD ** -0.5)\
               .then_inc(*mixA.inc(f"q{i}", l))
        act.wait_ge(*mixP.after("vs", l))
        act.copy(vv[:, 0], bank(4)[:, 0:256].rearrange("p (t d) -> p t d", t=NT)).then_inc(*mixA.inc("vs", l))
        act.wait_ge(*mixP.after("kskw", l))
        act.copy(kT[:, :, :], bank(3).rearrange("p (b n) -> p b n", b=2)).then_inc(*mixA.inc("kskw", l))
        act.wait_ge(*mixP.after("vwgl", l))
        vwgl = bank(5).rearrange("p (t c) -> p t c", t=NT)
        act.copy(vv[:, 1], vwgl[:, :, 0:P]).then_inc(*mixA.inc("vw", l))
        act.activation(gates[:, :, :], vwgl[:, :, P:P + 24], ACT.Sigmoid).then_inc(*mixA.inc("gates", l))
        act.wait_ge(*mixP.after("cmp1", l))
        act.wait_ge(*mixG.after("zeros", l))
        for g in range(GROUPS):
            part = slice(g * HD, (g + 1) * HD)
            ins = act.activation(g1[part, :, 0:N_CMP],
                                 bank(6 + g)[part, 0:2 * CMP_STRIDE].rearrange("p (v n) -> p v n", v=2)[:, :, 0:N_CMP],
                                 ACT.Gelu_apprx_tanh)
        ins.then_inc(*mixA.inc("g1", l))
        act.wait_ge(*mixP.after("ga", l))
        act.copy(gaT[0:16, :], bank(3)[0:16, 0:SEQ]).then_inc(*mixA.inc("ga", l))
        act.wait_ge(*mixP.after("gr", l))
        act.activation(sr[:, :, :], bank(4).rearrange("p (t c) -> p t c", t=NT), ACT.Silu).then_inc(*mixA.inc("sr", l))
        act.wait_ge(*mixV.after("gl_v", l))
        act.activation(gl_abs, gl_min, ACT.Abs).then_inc(*mixA.inc("abs", l))
        act.wait_ge(*mixA.after("abs", l))
        act.activation(gl_abs, gl_abs, ACT.Exp, scale=-1.0).then_inc(*mixA.inc("ex", l))
        act.wait_ge(*mixA.after("ex", l))
        act.activation(gl_abs, gl_abs, ACT.Ln, bias=1.0).then_inc(*mixA.inc("ln1", l))
        act.wait_ge(*mixP.after("pool1", l))
        for i in range(len(POOL_WINDOWS)):
            part = slice((i % 2) * HD, (i % 2 + 1) * HD)
            ins = act.copy(pooledT[part, i // 2, :], bank(i // 2)[part, (i % 2) * SEQ:(i % 2 + 1) * SEQ])
        ins.then_inc(*mixA.inc("pool1", l))
        act.wait_ge(*mixV.after("gl_b", l))
        act.activation(gl_eb, gl_b, ACT.Exp, scale=1.0 / GLA_TAU).then_inc(*mixA.inc("eb", l))
        act.activation(gl_enb, gl_b, ACT.Exp, scale=-1.0 / GLA_TAU).then_inc(*mixA.inc("enb", l))
        act.wait_ge(*mixV.after("gl_dd", l))
        act.activation(gl_ekd, gl_ekd, ACT.Exp, scale=1.0 / GLA_TAU).then_inc(*mixA.inc("ekd", l))
        act.wait_ge(*mixP.after("kdT", l))
        act.copy(kdT[:, :, :], bank(3)[:, 0:256].rearrange("p (t c) -> p t c", t=NT)).then_inc(*mixA.inc("kdT", l))
        act.wait_ge(*mixP.after("pool2", l))
        for i in range(2):
            ins = act.mul(oT[:, 4 + i, :], bank(7)[:, i * SEQ:(i + 1) * SEQ], cols_b[:, 104 + 2 * l + i:105 + 2 * l + i])
        ins.then_inc(*mixA.inc("pool2", l))
        for t in range(NT):
            act.wait_ge(*mixP.after(f"gla{t}", l))
            act.activation(sq[:, t, :], bank(6 + t)[:, 0:256], ACT.Square).then_inc(*mixA.inc(f"sq{t}", l))
        act.wait_ge(*mixV.after("ss", l))
        act.activation(ss_std[:, :, :], ss[:, :, :], ACT.Sqrt, bias=eps[:, 2:3], scale=1.0 / GLA_V)\
           .then_inc(*mixA.inc("ss_std", l))
        act.wait_ge(*mixV.after("pc_sub", l))
        act.activation(pc[:, :, :, :], pc[:, :, :, :], ACT.Exp).then_inc(*mixA.inc("pc_exp", l))

        def exps(i):
            t, b, g = UNITS[i]
            nk = P * (t + 1)
            act.wait_ge(*mixV.after(f"m{i}", l))
            for r in range(REP):
                ins = act.activation(p_sb[:, i % 2, r * nk:(r + 1) * nk], p_sb[:, i % 2, r * nk:(r + 1) * nk], ACT.Exp,
                                     bias=nmax[:, i, r:r + 1], accum_out=rsum[:, i, r:r + 1])
            ins.then_inc(*mixA.inc(f"e{i}", l))

        act.wait_ge(*mixP.after("pcT", l))
        act.copy(pcT[:, :, :], bank(3)[:, 0:256].rearrange("p (t c) -> p t c", t=NT)).then_inc(*mixA.inc("pcT", l))
        exps(0)
        for i in range(len(UNITS)):
            t = UNITS[i][0]
            if i + 1 < len(UNITS):
                exps(i + 1)
            act.wait_ge(*mixP.after(f"t{i}", l))
            if i >= 2:
                act.wait_ge(*mixP.after(f"v{i - 2}", l))
            n = REP * (t + 1)
            act.copy(pT[:, i % 2, 0:n, :], psum[:, 4:6, :].rearrange("p b (j n) -> p (b j) n", n=P)[:, 0:n, :])\
               .then_inc(*mixA.inc(f"pT{i}", l))
        for t in range(NT):
            act.wait_ge(*mixP.after(f"oA{t}", l))
            act.copy(oT[:, 0:4, t * P:(t + 1) * P], bank(t).rearrange("p (j n) -> p j n", j=4))
        act.wait_ge(*mixP.after("oC", l))
        act.copy(oT[:, 6:8, :].rearrange("p j (t n) -> p t j n", t=NT), bank(2).rearrange("p (t j n) -> p t j n", t=NT, j=2))\
           .then_inc(*mixA.inc("oT", l))

    def mix_dve(dve, step, l):
        def link(ins):
            ins.then_inc(*step.one())
            dve.wait_ge(*step.now())

        dve.wait_ge(*mixP.after("kcvc", l))
        for v in range(2):
            for half in range(2):
                ins = dve.tensor_tensor(
                    zc[:, v, half, :].rearrange("p (c j) -> p c j", j=CMP_STRIDE),
                    bank(2)[:, v * SEQ:(v + 1) * SEQ].rearrange("p (c j) -> p c j", j=CMP_STRIDE),
                    pe_col[:, 2 * l + v, half * CMP_STRIDE:(half + 1) * CMP_STRIDE].unsqueeze(1)
                    .to_broadcast([P, SEQ // CMP_STRIDE, CMP_STRIDE]), ALU.add)
        ins.then_inc(*mixV.inc("zc", l))
        dve.wait_ge(*mixP.after("u", l))
        dve.tensor_copy(u_sb[:, :, :], bank(0).rearrange("p (t c) -> p t c", t=NT)).then_inc(*mixV.inc("u", l))
        dve.wait_ge(*mixP.after("gqk", l))
        dve.tensor_copy(gqk[:, :, :], bank(1).rearrange("p (t c) -> p t c", t=2)).then_inc(*mixV.inc("gqk", l))
        dve.wait_ge(*mixP.after("gv", l))
        dve.tensor_copy(gv[:, :, :], bank(2).rearrange("p (t c) -> p t c", t=NT)).then_inc(*mixV.inc("gv", l))
        dve.wait_ge(*mixA.after("g1", l))
        dve.tensor_copy(g1rep[:, :, :], g1[:, 1, :].unsqueeze(1).to_broadcast([P, HEADS, CMP_STRIDE]))\
           .then_inc(*mixV.inc("g1rep", l))
        dve.wait_ge(*mixP.after("pre", l))
        dve.tensor_scalar(gl_min, bank(6)[:, 0:SEQ], cols_b[:, 108 + l:109 + l], None, ALU.add)\
           .then_inc(*mixV.inc("gl_v", l))
        dve.wait_ge(*mixV.after("gl_v", l))
        dve.wait_ge(*mixA.after("ln1", l))
        link(dve.scalar_tensor_tensor(gl_min, gl_min, 0.0, gl_abs, ALU.min, ALU.subtract))
        dve.tensor_tensor_scan(gl_b, const("gla_go"), gl_min, 0.0, ALU.mult, ALU.add).then_inc(*mixV.inc("gl_b", l))
        dve.wait_ge(*mixV.after("gl_b", l))
        b4 = gl_b.rearrange("p (n c) -> p n c", c=GLA_CHUNK)
        dve.tensor_tensor(gl_ekd.rearrange("p (n c) -> p n c", c=GLA_CHUNK),
                          b4[:, :, GLA_CHUNK - 1:GLA_CHUNK].to_broadcast([P, 4, GLA_CHUNK]), b4, ALU.subtract)\
           .then_inc(*mixV.inc("gl_dd", l))
        dve.wait_ge(*mixP.after("cmp2", l))
        dve.tensor_copy(kcT, bank(5)[:, 0:CMP_STRIDE]).then_inc(*mixV.inc("kcT", l))
        dve.tensor_tensor(vblk[:, :, :].rearrange("p (g r) d -> p g r d", g=GROUPS),
                          bank(5)[:, P:2 * P].rearrange("p (g d) -> p g d", g=GROUPS).unsqueeze(2)
                          .to_broadcast([P, GROUPS, REP, HD]),
                          const("head_rows").rearrange("p (g r) -> p g r", g=GROUPS).unsqueeze(3)
                          .to_broadcast([P, GROUPS, REP, HD]), ALU.mult).then_inc(*mixV.inc("vblk", l))
        dve.wait_ge(*mixV.after("gqk", l))
        dve.wait_ge(*mixA.after("eb", l))
        dve.scalar_tensor_tensor(gl_q, gqk[:, 0, :], GLA_K ** -0.5, gl_eb, ALU.mult, ALU.mult)
        dve.wait_ge(*mixA.after("ekd", l))
        dve.tensor_tensor(gl_k, gqk[:, 1, :], gl_enb, ALU.mult)
        dve.tensor_tensor(gl_kd, gqk[:, 1, :], gl_ekd, ALU.mult).then_inc(*mixV.inc("gl_kd", l))
        dve.wait_ge(*mixP.after("dS", l))
        dve.wait_ge(*mixG.after("zeros", l))
        for n in range(3):
            for hh in range(GLA_H):
                part, cols = slice(hh * GLA_K, (hh + 1) * GLA_K), slice(hh * GLA_V, (hh + 1) * GLA_V)
                dS = bank(4 + n % 2)[part, (n // 2) * 256:(n // 2 + 1) * 256][:, cols]
                if n == 0:
                    ins = dve.tensor_copy(s_blk[part, 1, cols], dS)
                else:
                    ins = dve.scalar_tensor_tensor(s_blk[part, n + 1, cols], s_blk[part, n, cols],
                                                   gl_eb[part, n * GLA_CHUNK + GLA_CHUNK - 1:(n + 1) * GLA_CHUNK], dS,
                                                   ALU.mult, ALU.add)
            if n < 2:
                link(ins)
            else:
                ins.then_inc(*mixV.inc("s_blk", l))
        dve.wait_ge(*mixP.after("at", l))
        keep = const("gla_keep").bitcast(U32).unsqueeze(1).to_broadcast([P, NT, P])
        for hh in range(GLA_H):
            ins = dve.copy_predicated(at_sb[:, hh, :, :], keep, bank(hh)[:, 0:256].rearrange("p (t n) -> p t n", t=NT))
        ins.then_inc(*mixV.inc("at", l))
        for t in range(NT):
            dve.wait_ge(*mixA.after(f"sq{t}", l))
            ins = dve.tensor_reduce(ss[:, t, :], sq[:, t, :].rearrange("p (h d) -> p h d", d=GLA_V), AX_X, ALU.add)
        ins.then_inc(*mixV.inc("ss", l))
        dve.wait_ge(*mixP.after("sc", l))
        for g in range(GROUPS):
            ins = dve.tensor_tensor(
                pc[:, :, g * REP:(g + 1) * REP, :],
                bank(g)[:, 0:P].rearrange("p (t r n) -> p t r n", t=NT, r=REP),
                const("cmp_bias").rearrange("p (t n) -> p t n", t=NT).unsqueeze(2).to_broadcast([P, NT, REP, CMP_STRIDE]),
                ALU.add)
        ins.then_inc(*mixV.inc("pc_bias", l))
        dve.wait_ge(*mixV.after("pc_bias", l))
        pcf = pc[:, :, :, :].rearrange("p t h n -> p (t h) n")
        link(dve.tensor_reduce(pc_max, pcf, AX_X, ALU.max))
        dve.tensor_tensor(pcf, pcf, pc_max.unsqueeze(2).to_broadcast([P, NT * HEADS, CMP_STRIDE]), ALU.subtract)\
           .then_inc(*mixV.inc("pc_sub", l))
        dve.wait_ge(*mixA.after("ss_std", l))
        link(dve.reciprocal(ss[:, :, :], ss_std[:, :, :]))
        dve.wait_ge(*mixG.after("sr", l))
        for t in range(NT):
            link(dve.tensor_tensor(oC[:, t, :].rearrange("p (h d) -> p h d", d=GLA_V),
                                   bank(6 + t)[:, 0:256].rearrange("p (h d) -> p h d", d=GLA_V),
                                   ss[:, t, :].unsqueeze(2).to_broadcast([P, GLA_H, GLA_V]), ALU.mult))
            dve.tensor_tensor(oC[:, t, :], oC[:, t, :], sr[:, t, :], ALU.mult).then_inc(*mixV.inc(f"oC{t}", l))
        dve.wait_ge(*mixA.after("pc_exp", l))
        link(dve.tensor_tensor(pc[:, :, :, :], pc[:, :, :, :],
                               const("cmp_seen").rearrange("p (t n) -> p t n", t=NT).unsqueeze(2)
                               .to_broadcast([P, NT, HEADS, CMP_STRIDE]), ALU.mult))
        link(dve.tensor_reduce(pc_sum, pcf, AX_X, ALU.add))
        link(dve.tensor_scalar(pc_sum, pc_sum, 0.5, None, ALU.max))
        link(dve.reciprocal(pc_sum, pc_sum))
        dve.tensor_tensor(pcf, pcf, pc_sum.unsqueeze(2).to_broadcast([P, NT * HEADS, CMP_STRIDE]), ALU.mult)\
           .then_inc(*mixV.inc("pc", l))

        def probs(i):
            t, b, g = UNITS[i]
            nk = P * (t + 1)
            dve.wait_ge(*mixP.after(f"s{i}", l))
            if i >= 2:
                dve.wait_ge(*mixP.after(f"t{i - 2}", l))
            src = psum[:, 2 * (i % 2):2 * (i % 2) + 2, :].rearrange("p b n -> p (b n)")[:, 0:REP * nk]
            dst = p_sb[:, i % 2, 0:REP * nk].rearrange("p (r n) -> p r n", r=REP)
            dve.tensor_tensor(dst, src.rearrange("p (r n) -> p r n", r=REP),
                              const("causal")[:, 2 * P - nk:2 * P].unsqueeze(1).to_broadcast([P, REP, nk]), ALU.add)\
               .then_inc(*mixV.inc(f"p{i}", l))
            dve.wait_ge(*mixV.after(f"p{i}", l))
            dve.tensor_reduce(nmax[:, i, :], dst, AX_X, ALU.max, negate=True).then_inc(*mixV.inc(f"m{i}", l))

        def heads(ap):
            return ap.rearrange("p (h d) -> p h d", d=HD)

        def each_head(ap):
            return ap.unsqueeze(2).to_broadcast([P, HEADS, HD])

        g3 = gates[:, :, :].rearrange("p t (h b) -> p t b h", b=3)
        probs(0)
        for t in range(NT):
            dve.wait_ge(*mixP.after(f"oc{t}", l))
            dve.tensor_tensor(heads(oA[:, t, :]), heads(bank(4 + t)), each_head(g3[:, t, 0, :]), ALU.mult)\
               .then_inc(*mixV.inc(f"oc{t}", l))
        for i in range(1, len(UNITS) + 1):
            if i < len(UNITS):
                probs(i)
            t, b, g = UNITS[i - 1]
            if g == GROUPS - 1:
                j = i - 2
                dve.wait_ge(*mixP.after(f"v{i - 1}", l))
                link(dve.reciprocal(o_w[:, b, :], rsum[:, j:j + 2, :].rearrange("p u r -> p (u r)")))
                link(dve.tensor_tensor(o_w[:, b, :], o_w[:, b, :], g3[:, t, 1 + b, :], ALU.mult))
                dve.tensor_tensor(heads(o_tmp), heads(bank(6 + b)), each_head(o_w[:, b, :]), ALU.mult)\
                   .then_inc(*mixV.inc(f"ot{b}_{t}", l))
                dve.wait_ge(*mixV.after(f"ot{b}_{t}", l))
                dve.tensor_tensor(oA[:, t, :], oA[:, t, :], o_tmp, ALU.add).then_inc(*mixV.inc(f"oA{b}_{t}", l))
                dve.wait_ge(*mixV.after(f"oA{b}_{t}", l))

    def mix_pool(pool, step, l):
        pool.memset(s_blk[:, :, :], 0.0)
        pool.memset(at_sb[:, :, :, :], 0.0)
        pool.memset(g1[:, :, :], 0.0).then_inc(*mixG.inc("zeros", l))
        pool.wait_ge(*mixA.after("sr", l))
        pool.tensor_tensor(sr[:, :, :], sr[:, :, :], gla_norm[:, l, :].unsqueeze(1).to_broadcast([P, NT, GLA_H * GLA_V]),
                           ALU.mult).then_inc(*mixG.inc("sr", l))

    cv = Carve()
    sz = cv.take(ML_T, SEQ)
    xc = cv.take(ML_T, SEQ)
    xm = cv.take(ML_T, SEQ)
    kk = xm
    vm = cv.take(NT, ML_INNER)
    gts = cv.take(NT, 2 * ML_HEADS)
    logf, ml_a, ml_f, ml_m, ml_neg, ml_den, ml_em, ml_rd = (cv.take(NT, ML_HEADS) for _ in range(8))
    ml_bn = cv.take(NT, ML_HEADS, 6)
    ml_mv = cv.take(NT, ML_HEADS, 2)
    ml_std, ml_rs = cv.take(NT, ML_HEADS), cv.take(NT, ML_HEADS)
    NP2 = ML_T // 2

    def col_a(name, i):
        return cols_a[:, cols_a_at[name] + i:cols_a_at[name] + i + 1]

    def block_diag(buf):
        return buf.rearrange("p (t n o) -> p t n o", n=P // QKV_BLOCK, o=QKV_BLOCK)

    bd_a = z[:, :, :].rearrange("p t d -> p (t d)")
    bd_b = xT[:, :, :].rearrange("p k n -> p (k n)")

    def ml_scratch():
        q = slot_of(PN["ml", "scratch_q"]).rearrange("p (t n) -> p t n", n=SEQ)
        hh = slot_of(PN["ml", "scratch_h"])
        s = slot_of(PN["ml", "scratch_s"])
        return (q, hh.rearrange("p (t n) -> p t n", n=SEQ), hh.rearrange("p (t n) -> p t n", t=NT),
                s[:, 0:1024].rearrange("p (t h n) -> p t h n", t=NT, h=ML_HEADS),
                [s[:, 1024:1536], s[:, 1536:2560]],
                [s[:, 2560:3072], s[:, 3072:4096]])

    def mlstm_sp(sp):
        w = rows(A["mlstm_w_in_2"][0])
        for i in range(8):
            pn = PN["ml", "in", i]
            load_panel(sp, pn, [(panel(pn, KD, CHUNK), w[:, :, i * CHUNK:(i + 1) * CHUNK])])
        for i in range(4):
            pn = PN["ml", "out", i]
            load_panel(sp, pn, [(panel(pn, 4, D), rows(A["mlstm_w_out_2"][0])[:, 4 * i:4 * i + 4, :])])

    def mlstm_pe(pe):
        q, vT, hn, diag, sd, sdT = ml_scratch()
        fills = ([f"in{j}" for j in range(2 * NP2)] + [f"vT{j}" for j in range(NP2)] +
                 [f"q{j}" for j in range(NP2)] + [f"k{j}" for j in range(NP2)])

        def fill_bank(name):
            n = fills.index(name)
            if n >= 4:
                pe.wait_ge(*mlA.after(fills[n - 4]))
            return bank(n % 4)

        for j in range(2 * NP2):
            pn = PN["ml", "in", j // 2]
            if j % 2 == 0:
                pe.wait_ge(*landed(pn))
            dst = fill_bank(f"in{j}")
            for i in range(2):
                cols = ((2 * j + i) % 4) * P
                for k in range(KD):
                    mm = pe.matmul(dst[:, i * SEQ:(i + 1) * SEQ], panel(pn, KD, CHUNK)[:, k, cols:cols + P], xT[:, k, :],
                                   start=k == 0, stop=k == KD - 1)
            mm.then_inc(*mlP.inc(f"in{j}"))

        bv = bd_a.rearrange("p (t c) -> p t c", c=P)
        pe.wait_ge(*mlV.after("bd_v"))
        for j in range(8):
            t, c4 = divmod(j, 4)
            if j >= 2:
                pe.wait_ge(*mlV.after(f"v{j - 2}"))
            for i in range(4):
                ct = 4 * c4 + i
                mm = pe.matmul(bank(4 + j % 2)[:, i * P:(i + 1) * P], xm[:, ct, t * P:(t + 1) * P], bv[:, ct, :],
                               start=True, stop=True)
            mm.then_inc(*mlP.inc(f"v{j}"))

        def project(name, bd, src):
            for j in range(NP2):
                dst = fill_bank(f"{name}{j}")
                for i in range(2):
                    mm = pe.matmul(dst[:, i * SEQ:(i + 1) * SEQ], bd[:, 2 * j + i, :], src[:, 2 * j + i, :],
                                   start=True, stop=True)
                mm.then_inc(*mlP.inc(f"{name}{j}"))

        def gate_part(i, src, name):
            for ct in range(ML_T):
                if ct % 2 == 0:
                    pe.wait_ge(*mlA.after(f"{name}{ct // 2}"))
                for t in range(NT):
                    mm = pe.matmul(bank(6 + t)[:, 0:2 * ML_HEADS], src[:, ct, t * P:(t + 1) * P], gate_w[:, ML_T * i + ct, :],
                                   start=i == 0 and ct == 0, stop=i == 2 and ct == ML_T - 1)
            return mm

        project("vT", bv, xm)
        pe.wait_ge(*mlV.after("bd_q"))
        pe.wait_ge(*mlA.after(f"xc{NP2 - 1}"))
        project("q", bd_b.rearrange("p (t c) -> p t c", c=P), xc)
        gate_part(0, q, "q")
        pe.wait_ge(*mlV.after("bd_k"))
        project("k", bv, xc)
        gate_part(1, kk, "k")
        gate_part(2, vT, "vT").then_inc(*mlP.inc("gates"))

        pe.wait_ge(*mlV.after("logf"))
        pe.matmul(bank(5)[:, 0:ML_HEADS], const("upto"), logf[:, 0, :], start=True, stop=True)
        pe.matmul(bank(5)[:, ML_HEADS:2 * ML_HEADS], ones, logf[:, 0, :], start=True, stop=False)
        pe.matmul(bank(5)[:, ML_HEADS:2 * ML_HEADS], const("upto"), logf[:, 1, :], start=False, stop=True)\
          .then_inc(*mlP.inc("F"))
        pe.wait_ge(*mlA.after("k7"))
        pe.wait_ge(*mlV.after("diag"))
        for t in range(NT):
            mm = pe.matmul(bank(t), ones, diag[:, t, :, :].rearrange("p h n -> p (h n)"), start=True, stop=True)
        mm.then_inc(*mlP.inc("abc"))

        def score_dst(t):
            return bank(2) if t == 0 else psum[:, 4:6, :].rearrange("p b n -> p (b n)")

        for t in range(NT):
            nk = P * (t + 1)
            for hh in range(ML_HEADS):
                for i in range(4):
                    ct = 4 * hh + i
                    mm = pe.matmul(score_dst(t)[:, hh * nk:(hh + 1) * nk], q[:, ct, t * P:(t + 1) * P], kk[:, ct, 0:nk],
                                   start=i == 0, stop=i == 3)
            mm.then_inc(*mlP.inc(f"S{t}"))
        for t in range(NT):
            pe.wait_ge(*mlV.after(f"sd{t}"))
            dst = bank(3) if t == 0 else psum[:, 6:8, :].rearrange("p b n -> p (b n)")
            for i in range(ML_HEADS * (t + 1)):
                mm = pe.transpose(dst[:, i * P:(i + 1) * P], sd[t][:, i * P:(i + 1) * P], ident)
            mm.then_inc(*mlP.inc(f"T{t}"))
            pe.wait_ge(*mlA.after(f"T{t}"))
            for hh in range(ML_HEADS):
                n = t * ML_HEADS + hh
                if n >= 4:
                    pe.wait_ge(*mlV.after(f"h{n - 4}"))
                if n == 0:
                    pe.wait_ge(*mlV.after("am1"))
                for kt in range(t + 1):
                    mm = pe.matmul(bank(n % 4), sdT[t][:, (hh * (t + 1) + kt) * P:(hh * (t + 1) + kt + 1) * P],
                                   vm[:, kt, hh * ML_HD:(hh + 1) * ML_HD], start=kt == 0, stop=kt == t)
                mm.then_inc(*mlP.inc(f"n{n}"))
        pe.wait_ge(*mlV.after("hn"))
        for j in range(NP2):
            if j >= 4:
                pe.wait_ge(*mlV.after(f"hs{j - 4}"))
            for i in range(2):
                for t in range(NT):
                    mm = pe.transpose(bank(j % 4)[:, i * SEQ + t * P:i * SEQ + (t + 1) * P],
                                      hn[:, t, (2 * j + i) * P:(2 * j + i + 1) * P], ident)
            mm.then_inc(*mlP.inc(f"h{j}"))
        for i in range(4):
            pn = PN["ml", "out", i]
            pe.wait_ge(*landed(pn))
            pe.wait_ge(*mlG.after(f"y{2 * i + 1}"))
            for k in range(4):
                for t in range(NT):
                    for half in range(2):
                        mm = pe.matmul(acc(t, half), xc[:, 4 * i + k, t * P:(t + 1) * P],
                                       panel(pn, 4, D)[:, k, half * 512:(half + 1) * 512],
                                       start=i == 0 and k == 0, stop=i == 3 and k == 3)
            mm.then_inc(*(mlP.inc(f"wo{i}") if i < 3 else (acc_done, 1)))

    def mlstm_act(act, step):
        q, vT, hn, diag, sd, sdT = ml_scratch()

        def out_of(j, name, n):
            act.wait_ge(*mlP.after(name))
            return bank(n % 4).rearrange("p (t n) -> p t n", t=2)

        for j in range(NP2):
            act.copy(xm[:, 2 * j:2 * j + 2, :], out_of(j, f"in{j}", j)).then_inc(*mlA.inc(f"in{j}"))
        for j in range(NP2):
            n = NP2 + j
            act.activation(sz[:, 2 * j:2 * j + 2, :], out_of(j, f"in{n}", n), ACT.Silu).then_inc(*mlA.inc(f"in{n}"))
            act.wait_ge(*mlV.after(f"conv{j}"))
            for i in (2 * j, 2 * j + 1):
                ins = act.activation(xc[:, i, :], xc[:, i, :], ACT.Silu, bias=col_a("conv_b", i))
            ins.then_inc(*mlA.inc(f"xc{j}"))
        act.wait_ge(*PN["ml", "scratch_h"].before)
        for j in range(NP2):
            act.copy(vT[:, 2 * j:2 * j + 2, :], out_of(j, f"vT{j}", j)).then_inc(*mlA.inc(f"vT{j}"))
        act.wait_ge(*PN["ml", "scratch_q"].before)
        for j in range(NP2):
            act.mul(q[:, 2 * j:2 * j + 2, :], out_of(j, f"q{j}", j), 1.0).then_inc(*mlA.inc(f"q{j}"))
        for j in range(NP2):
            act.copy(kk[:, 2 * j:2 * j + 2, :], out_of(j, f"k{j}", j)).then_inc(*mlA.inc(f"k{j}"))
        act.wait_ge(*mlV.after("gts"))
        act.activation(logf[:, :, :], gts[:, :, ML_HEADS:], ACT.Abs).then_inc(*mlA.inc("abs"))
        act.wait_ge(*mlA.after("abs"))
        act.activation(logf[:, :, :], logf[:, :, :], ACT.Exp, scale=-1.0).then_inc(*mlA.inc("ex"))
        act.wait_ge(*mlA.after("ex"))
        act.activation(logf[:, :, :], logf[:, :, :], ACT.Ln, bias=1.0).then_inc(*mlA.inc("ln1"))
        act.wait_ge(*mlP.after("k7"))
        for i in range(ML_T):
            ins = act.mul(xc[:, i, :], xc[:, i, :], col_a("skip", i))
        ins.then_inc(*mlA.inc("skip"))
        for t in range(NT):
            nk = P * (t + 1)
            act.wait_ge(*mlV.after(f"m{t}"))
            for hh in range(ML_HEADS):
                ins = act.activation(sd[t][:, hh * nk:(hh + 1) * nk], sd[t][:, hh * nk:(hh + 1) * nk], ACT.Exp,
                                     bias=ml_neg[:, t, hh:hh + 1])
            ins.then_inc(*mlA.inc(f"E{t}"))
        act.activation(ml_em[:, :, :], ml_em[:, :, :], ACT.Exp, scale=-1.0).then_inc(*mlA.inc("em"))
        for t in range(NT):
            act.wait_ge(*mlP.after(f"T{t}"))
            src = bank(3) if t == 0 else psum[:, 6:8, :].rearrange("p b n -> p (b n)")
            act.copy(sdT[t], src).then_inc(*mlA.inc(f"T{t}"))
        act.wait_ge(*mlV.after("h_mv"))
        act.activation(ml_std[:, :, :], ml_mv[:, :, :, 1], ACT.Sqrt, bias=eps[:, 1:2]).then_inc(*mlA.inc("hstd"))

    def mlstm_dve(dve, step):
        q, vT, hn, diag, sd, sdT = ml_scratch()

        def link(ins):
            ins.then_inc(*step.one())
            dve.wait_ge(*step.now())

        def build_bd(buf, i, name):
            dve.tensor_tensor(block_diag(buf),
                              qkv_w[:, i, :, :].unsqueeze(2).to_broadcast([P, ML_T, P // QKV_BLOCK, QKV_BLOCK]),
                              const("blk4").unsqueeze(1).unsqueeze(3).to_broadcast([P, ML_T, P // QKV_BLOCK, QKV_BLOCK]),
                              ALU.mult).then_inc(*mlV.inc(name))

        dve.wait_ge(x_ready, NT * 6)
        build_bd(bd_a, 2, "bd_v")
        for j in range(NP2):
            dve.wait_ge(*mlA.after(f"in{j}"))
            for tap in range(ML_CONV - 1, -1, -1):
                back = ML_CONV - 1 - tap
                for i in (2 * j, 2 * j + 1):
                    w = col_a("conv_w", tap * ML_T + i)
                    if back == 0:
                        ins = dve.tensor_scalar(xc[:, i, :], xm[:, i, :], w, None, ALU.mult)
                    else:
                        ins = dve.scalar_tensor_tensor(xc[:, i, back:], xm[:, i, 0:SEQ - back], w, xc[:, i, back:],
                                                       ALU.mult, ALU.add)
                if back < ML_CONV - 1:
                    link(ins)
                else:
                    ins.then_inc(*mlV.inc(f"conv{j}"))
        dve.wait_ge(*mlP.after(f"in{2 * NP2 - 1}"))
        build_bd(bd_b, 0, "bd_q")
        for j in range(8):
            t, c4 = divmod(j, 4)
            dve.wait_ge(*mlP.after(f"v{j}"))
            dve.tensor_copy(vm[:, t, c4 * 512:(c4 + 1) * 512], bank(4 + j % 2)).then_inc(*mlV.inc(f"v{j}"))
        dve.wait_ge(*mlP.after(f"vT{NP2 - 1}"))
        build_bd(bd_a, 1, "bd_k")
        dve.wait_ge(*mlP.after("gates"))
        for t in range(NT):
            ins = dve.tensor_tensor(gts[:, t, :], bank(6 + t)[:, 0:2 * ML_HEADS], gate_b[:, :], ALU.add)
        ins.then_inc(*mlV.inc("gts"))
        dve.wait_ge(*mlA.after("ln1"))
        dve.wait_ge(*mlV.after("gts"))
        dve.scalar_tensor_tensor(logf[:, :, :], gts[:, :, ML_HEADS:], 0.0, logf[:, :, :], ALU.min, ALU.subtract)\
           .then_inc(*mlV.inc("logf"))
        dve.wait_ge(*mlP.after("F"))
        f_ps = bank(5)[:, 0:NT * ML_HEADS].rearrange("p (t h) -> p t h", t=NT)
        dve.tensor_copy(ml_f[:, :, :], f_ps)
        link(dve.tensor_tensor(ml_a[:, :, :], gts[:, :, 0:ML_HEADS], f_ps, ALU.subtract))
        dve.wait_ge(*PN["ml", "scratch_s"].before)
        for t in range(NT):
            ins = dve.tensor_tensor(diag[:, t, :, :], ident.unsqueeze(1).to_broadcast([P, ML_HEADS, P]),
                                    ml_a[:, t, :].unsqueeze(2).to_broadcast([P, ML_HEADS, P]), ALU.mult)
        ins.then_inc(*mlV.inc("diag"))
        dve.wait_ge(*mlP.after("abc"))
        causal = const("causal")[:, P:2 * P].unsqueeze(1).to_broadcast([P, ML_HEADS, P])
        sdv = [sd[t].rearrange("p (h n) -> p h n", h=ML_HEADS) for t in range(NT)]
        a_all = [bank(t).rearrange("p (h n) -> p h n", h=ML_HEADS) for t in range(NT)]
        dve.tensor_tensor(sdv[0], a_all[0], causal, ALU.add).then_inc(*mlV.inc("am0"))
        dve.tensor_copy(sdv[1][:, :, 0:P], a_all[0])
        dve.tensor_tensor(sdv[1][:, :, P:2 * P], a_all[1], causal, ALU.add).then_inc(*mlV.inc("am1"))
        dve.wait_ge(*mlV.after("am1"))
        for t in range(NT):
            link(dve.tensor_reduce(ml_m[:, t, :], sdv[t], AX_X, ALU.max))
            link(dve.tensor_scalar(ml_m[:, t, :], ml_m[:, t, :], 0.0, None, ALU.max))
            if t == 1:
                link(dve.tensor_tensor(ml_em[:, :, :], ml_f[:, :, :], ml_m[:, :, :], ALU.add))
            dve.tensor_scalar(ml_neg[:, t, :], ml_m[:, t, :], -1.0, None, ALU.mult).then_inc(*mlV.inc(f"m{t}"))
        for t in range(NT):
            src = bank(2) if t == 0 else psum[:, 4:6, :].rearrange("p b n -> p (b n)")
            dve.wait_ge(*mlP.after(f"S{t}"))
            dve.wait_ge(*mlA.after(f"E{t}"))
            dve.scalar_tensor_tensor(sd[t], src, ML_HD ** -0.5, sd[t], ALU.mult, ALU.mult).then_inc(*mlV.inc(f"sd{t}"))
            dve.wait_ge(*mlV.after(f"sd{t}"))
            link(dve.tensor_reduce(ml_den[:, t, :], sdv[t], AX_X, ALU.add))
        link(dve.scalar_tensor_tensor(ml_den[:, :, :], ml_den[:, :, :], -1.0, ml_den[:, :, :], ALU.mult, ALU.max))
        dve.wait_ge(*mlA.after("em"))
        link(dve.tensor_tensor(ml_den[:, :, :], ml_den[:, :, :], ml_em[:, :, :], ALU.max))
        link(dve.reciprocal(ml_rd[:, :, :], ml_den[:, :, :]))
        dve.wait_ge(*mlP.after("gates"))
        for t in range(NT):
            for hh in range(ML_HEADS):
                n = t * ML_HEADS + hh
                part = hn[:, t, hh * ML_HD:(hh + 1) * ML_HD]
                dve.wait_ge(*mlP.after(f"n{n}"))
                dve.tensor_scalar(part, bank(n % 4), ml_rd[:, t, hh:hh + 1], None, ALU.mult).then_inc(*mlV.inc(f"h{n}"))
                dve.wait_ge(*mlV.after(f"h{n}"))
                link(dve.bn_stats(ml_bn[:, t, hh, :], part))
                ins = dve.bn_aggr(ml_mv[:, t, hh, :], ml_bn[:, t, hh, :])
        ins.then_inc(*mlV.inc("h_mv"))
        dve.wait_ge(*mlA.after("hstd"))
        link(dve.reciprocal(ml_rs[:, :, :], ml_std[:, :, :]))
        for t in range(NT):
            for hh in range(ML_HEADS):
                part = hn[:, t, hh * ML_HD:(hh + 1) * ML_HD]
                ins = dve.tensor_scalar(part, part, ml_mv[:, t, hh, 0:1], ml_rs[:, t, hh:hh + 1], ALU.subtract, ALU.mult)
        ins.then_inc(*mlV.inc("hn"))
        dve.wait_ge(*mlA.after("skip"))
        for j in range(NP2):
            dve.wait_ge(*mlP.after(f"h{j}"))
            for i in range(2):
                ct = 2 * j + i
                ins = dve.scalar_tensor_tensor(xc[:, ct, :], bank(j % 4)[:, i * SEQ:(i + 1) * SEQ], col_a("norm_w", ct),
                                               xc[:, ct, :], ALU.mult, ALU.add)
            ins.then_inc(*mlV.inc(f"hs{j}"))

    def mlstm_pool(pool, step):
        for j in range(NP2):
            pool.wait_ge(*mlV.after(f"hs{j}"))
            pool.tensor_tensor(xc[:, 2 * j:2 * j + 2, :], xc[:, 2 * j:2 * j + 2, :], sz[:, 2 * j:2 * j + 2, :], ALU.mult)\
                .then_inc(*mlG.inc(f"y{j}"))


    QUAD = 4
    ROUND = 1.5 * 2 ** 23
    TURN = 6.2831850
    cv = Carve()
    rot = cv.take(2, 2, QUAD, SEQ)
    w_in_s = cv.take(2, QUAD, SEQ)
    back_s = cv.take(2, QUAD, SEQ)
    sig = w_in_s.rearrange("p a b n -> p (a b n)").rearrange("p (i n) -> p i n", n=CHUNK)
    turned_s = y_sum[:, :, :].rearrange("p t d -> p (t d)").rearrange("p (a b n) -> p a b n", a=2, b=QUAD)
    b_wide = y_sum[:, :, :].rearrange("p t d -> p (t d)").rearrange("p (a s g h) -> p a s g h", a=2, s=S5_T, g=2)
    z_row = z[:, :, :].rearrange("p t d -> p (t d)")
    b_nat = z_row[:, 0:1024].rearrange("p (a s h) -> p a s h", a=2, s=S5_T)
    b_t1, b_t2 = [z_row[:, 1024 + 512 * i:1536 + 512 * i].rearrange("p (s h) -> p s h", s=S5_T) for i in range(2)]
    phase = z_row[:, 0:1024].rearrange("p (j n) -> p j n", j=QUAD)
    whole = gate_row[:, :, :].rearrange("p a n -> p (a n)").rearrange("p (j n) -> p j n", j=QUAD)
    cv = Carve(ARENA_FFN)
    BT = cv.take(2, KD, P)
    c_nat = cv.take(2, KD, 2 * S5_P)
    CT1 = cv.take(2, QUAD, P)
    CT = [z_row[:, 1024:2048].rearrange("p (a j n) -> p a j n", a=2, j=QUAD), CT1]
    lam_dt, turn, l_mag, l_sin, l_cos, l_abs, l_kr, l_ki, l_den, l_t1, l_t2 = (cv.take(S5_T) for _ in range(11))
    l_re, l_im, l_logdt = lam[:, 0:S5_T], lam[:, S5_T:2 * S5_T], lam[:, 2 * S5_T:3 * S5_T]

    def s5_load_pool(pool):
        pool.wait_ge(x_ready, NT * 7)
        for i, part in enumerate(("re", "im")):
            src = A[f"s5_b_{part}_2"][0].rearrange("(s g) p h -> (g p) s h", g=2)
            pool.dma_start(b_nat[:, i, :, :], src).then_inc(s5_landed, 16)
        for i, part in enumerate(("re", "im")):
            src = A[f"s5_c_{part}_2"][0].rearrange("(t g) h p -> (g h) t p", g=KD)
            for copy in range(2):
                pool.dma_start(c_nat[:, i, :, copy * S5_P:(copy + 1) * S5_P], src).then_inc(s5_landed, 16)

    def s5_discrete_act(act):
        act.activation(l_abs, l_logdt, ACT.Exp).then_inc(*s5A.inc("dt"))
        act.wait_ge(*s5V.after("lam_dt"))
        act.activation(l_mag, lam_dt, ACT.Exp).then_inc(*s5A.inc("mag"))
        act.wait_ge(*s5V.after("turn"))
        act.activation(l_sin, turn, ACT.Sin, scale=TURN)
        act.activation(l_cos, turn, ACT.Abs).then_inc(*s5A.inc("abs"))
        act.wait_ge(*s5A.after("abs"))
        act.activation(l_cos, l_cos, ACT.Sin, scale=-TURN, bias=eps[:, 3:4]).then_inc(*s5A.inc("cos"))

    def s5_discrete_dve(dve, step):
        def link(ins):
            ins.then_inc(*step.one())
            dve.wait_ge(*step.now())

        dve.wait_ge(*s5A.after("dt"))
        dve.tensor_tensor(lam_dt, l_re, l_abs, ALU.mult).then_inc(*s5V.inc("lam_dt"))
        link(dve.scalar_tensor_tensor(l_t1, l_im, 1.0 / (2.0 * np.pi), l_abs, ALU.mult, ALU.mult))
        link(dve.tensor_scalar(l_t2, l_t1, ROUND, ROUND, ALU.add, ALU.subtract))
        dve.tensor_tensor(turn, l_t1, l_t2, ALU.subtract).then_inc(*s5V.inc("turn"))
        link(dve.tensor_tensor(l_den, l_re, l_re, ALU.mult))
        link(dve.tensor_tensor(l_t1, l_im, l_im, ALU.mult))
        link(dve.tensor_tensor(l_den, l_den, l_t1, ALU.add))
        link(dve.reciprocal(l_den, l_den))
        dve.wait_ge(*s5A.after("cos"))
        link(dve.tensor_tensor(l_cos, l_cos, l_mag, ALU.mult))
        link(dve.tensor_scalar(l_cos, l_cos, 1.0, None, ALU.subtract))
        link(dve.tensor_tensor(l_sin, l_sin, l_mag, ALU.mult))
        for out_, p_, q_, op in ((l_kr, l_re, l_im, ALU.add), (l_ki, l_im, l_re, ALU.subtract)):
            dve.tensor_tensor(l_t1, l_cos, p_, ALU.mult)
            link(dve.tensor_tensor(l_t2, l_sin, q_, ALU.mult))
            if op == ALU.add:
                link(dve.tensor_tensor(out_, l_t1, l_t2, ALU.add))
            else:
                link(dve.tensor_tensor(out_, l_t2, l_t1, ALU.subtract))
            link(dve.tensor_tensor(out_, out_, l_den, ALU.mult))
        dve.wait_ge(s5_landed, 16 * 6)
        kr, ki = (v.unsqueeze(2).to_broadcast([P, S5_T, S5_H]) for v in (l_kr, l_ki))
        own = const("b_own").unsqueeze(1).unsqueeze(3).to_broadcast([P, S5_T, 2, S5_H])
        for part in range(2):
            dve.tensor_tensor(b_t1, kr, b_nat[:, part, :, :], ALU.mult)
            link(dve.tensor_tensor(b_t2, ki, b_nat[:, 1 - part, :, :], ALU.mult))
            link(dve.tensor_tensor(b_t1, b_t1, b_t2, ALU.add if part else ALU.subtract))
            ins = dve.tensor_tensor(b_wide[:, part, :, :, :], b_t1.unsqueeze(2).to_broadcast([P, S5_T, 2, S5_H]), own, ALU.mult)
            if part == 0:
                link(ins)
            else:
                ins.then_inc(*s5V.inc("b_wide"))

    def s5_states():
        return [slot_of(PN["s5", name]).rearrange("p (i a j n) -> p i a j n", i=2, a=2, j=QUAD)
                for name in ("scratch_s", "scratch_x")]

    def s5_sp(sp):
        w = rows(A["s5_w_glu_2"][0])
        for i in range(4):
            h_, gate = divmod(i, 2)
            c0 = gate * D + h_ * CHUNK
            pn = PN["s5", "glu", i]
            load_panel(sp, pn, [(panel(pn, KD, CHUNK), w[:, :, c0:c0 + CHUNK])])

    def s5_pool(pool, step):
        scanned, states = s5_states()

        def link(ins):
            ins.then_inc(*step.one())
            pool.wait_ge(*step.now())

        def angles(k):
            if k > 0:
                pool.wait_ge(*s5A.after(f"rot{k - 1}"))
            else:
                pool.wait_ge(*s5A.after("bt3"))
            link(pool.tensor_tensor(phase, turn[:, QUAD * k:QUAD * k + QUAD].unsqueeze(2).to_broadcast([P, QUAD, SEQ]),
                                    const("steps").unsqueeze(1).to_broadcast([P, QUAD, SEQ]), ALU.mult))
            link(pool.tensor_scalar(whole, phase, ROUND, ROUND, ALU.add, ALU.subtract))
            pool.tensor_tensor(phase, phase, whole, ALU.subtract).then_inc(*s5G.inc(f"angle{k}"))

        def turn_back(k):
            s, xs, r = scanned[:, k % 2, :, :, :], states[:, k % 2, :, :, :], rot[:, k % 2, :, :, :]
            cos, sin = (r[:, i, :, :].unsqueeze(1).to_broadcast([P, 2, QUAD, SEQ]) for i in range(2))
            pool.wait_ge(*s5V.after(f"scan{k}"))
            if k == 0:
                pool.wait_ge(*PN["s5", "scratch_x"].before)
            if k >= 2:
                pool.wait_ge(*s5P.after(f"y{k - 2}"))
            if k >= 1:
                pool.wait_ge(*s5G.after(f"x{k - 1}"))
            for i in range(2):
                pool.tensor_tensor(xs[:, i, :, :], s[:, i, :, :], r[:, 0, :, :], ALU.mult)
                ins = pool.tensor_tensor(back_s[:, i, :, :], s[:, i, :, :], r[:, 1, :, :], ALU.mult)
            link(ins)
            pool.tensor_tensor(xs[:, 0, :, :], xs[:, 0, :, :], back_s[:, 1, :, :], ALU.subtract)
            pool.tensor_tensor(xs[:, 1, :, :], xs[:, 1, :, :], back_s[:, 0, :, :], ALU.add).then_inc(*s5G.inc(f"x{k}"))

        angles(0)
        angles(1)
        for k in range(KD):
            turn_back(k)
            if k + 2 < KD:
                angles(k + 2)
        pool.wait_ge(*s5P.after("y7"))
        pool.dma_start(z_row[0:1, :], A["s5_b_glu_2"]).then_inc(s5_landed, 16)

    def s5_act(act, step):
        def angles(k):
            r = rot[:, k % 2, :, :, :]
            act.wait_ge(*s5G.after(f"angle{k}"))
            if k >= 2:
                act.wait_ge(*s5V.after(f"w{k - 2}"))
                act.wait_ge(*s5G.after(f"x{k - 2}"))
            act.activation(r[:, 1, :, :], phase, ACT.Sin, scale=TURN)
            act.activation(r[:, 0, :, :], phase, ACT.Abs).then_inc(*s5A.inc(f"abs{k}"))
            act.wait_ge(*s5A.after(f"abs{k}"))
            act.activation(r[:, 0, :, :], r[:, 0, :, :], ACT.Sin, scale=-TURN, bias=eps[:, 3:4]).then_inc(*s5A.inc(f"rot{k}"))

        for i in range(4):
            act.wait_ge(*s5P.after(f"bt{i}"))
            part, half = divmod(i, 2)
            act.copy(BT[:, part, 4 * half:4 * half + 4, :], bank(4 + i).rearrange("p (k n) -> p k n", n=P))\
               .then_inc(*s5A.inc(f"bt{i}"))
        for k in range(KD):
            angles(k)
            if k == KD // 2:
                gelu(act, 0)
        gelu(act, 1)
        for i in range(4):
            act.wait_ge(*s5P.after(f"glu{i}"))
            act.activation(sig[:, i, :], bank(2 * i + 1), ACT.Sigmoid).then_inc(*s5A.inc(f"sig{i}"))

    def gelu(act, half):
        k1 = KD // 2 * (half + 1)
        act.wait_ge(*s5V.after(f"y{k1 - 1}"))
        part = xT[:, k1 - KD // 2:k1, :]
        act.activation(part, part, ACT.Gelu_apprx_tanh).then_inc(*s5A.inc(f"gelu{half}"))

    def s5_dve(dve, step):
        scanned, states = s5_states()

        def link(ins):
            ins.then_inc(*step.one())
            dve.wait_ge(*step.now())

        def skip_u(k):
            dve.wait_ge(*s5P.after(f"y{k}"))
            dve.scalar_tensor_tensor(xT[:, k, :], xT[:, k, :], col_a("s5_d", k), bank(6 + k % 2)[:, 0:SEQ], ALU.mult, ALU.add)\
               .then_inc(*s5V.inc(f"y{k}"))

        for k in range(KD):
            bu = psum[:, 0:QUAD, :].rearrange("p j (a n) -> p a j n", a=2)
            r = rot[:, k % 2, :, :, :]
            dve.wait_ge(*s5P.after(f"bu{k}"))
            dve.wait_ge(*s5A.after(f"rot{k}"))
            if k >= 1:
                dve.wait_ge(*s5V.after(f"scan{k - 1}"))
            for i in range(2):
                dve.tensor_tensor(w_in_s[:, i, :, :], bu[:, i, :, :], r[:, 0, :, :], ALU.mult)
                ins = dve.tensor_tensor(turned_s[:, i, :, :], bu[:, i, :, :], r[:, 1, :, :], ALU.mult)
            ins.then_inc(*s5V.inc(f"w{k}"))
            dve.wait_ge(*s5V.after(f"w{k}"))
            dve.tensor_tensor(w_in_s[:, 0, :, :], w_in_s[:, 0, :, :], turned_s[:, 1, :, :], ALU.add)
            link(dve.tensor_tensor(w_in_s[:, 1, :, :], w_in_s[:, 1, :, :], turned_s[:, 0, :, :], ALU.subtract))
            if k == 0:
                dve.wait_ge(*PN["s5", "scratch_s"].before)
            if k >= 2:
                dve.wait_ge(*s5G.after(f"x{k - 2}"))
            for j in range(QUAD):
                mag = l_mag[:, QUAD * k + j:QUAD * k + j + 1].to_broadcast([P, SEQ])
                for i in range(2):
                    ins = dve.tensor_tensor_scan(scanned[:, k % 2, i, j, :], mag, w_in_s[:, i, j, :], 0.0, ALU.mult, ALU.add)
            ins.then_inc(*s5V.inc(f"scan{k}"))
            dve.wait_ge(*s5P.after(f"ct{k}"))
            if k >= 2:
                dve.wait_ge(*s5P.after(f"y{k - 2}"))
            own = const("c_own").rearrange("p (j n) -> p j n", j=QUAD)
            src = [bank(4 + k % 2)[:, i * P:(i + 1) * P].unsqueeze(1).to_broadcast([P, QUAD, P]) for i in range(2)]
            dve.tensor_tensor(CT[k % 2][:, 0, :, :], src[0], own, ALU.mult)
            dve.scalar_tensor_tensor(CT[k % 2][:, 1, :, :], src[1], -1.0, own, ALU.mult, ALU.mult).then_inc(*s5V.inc(f"ct{k}"))
            if k >= 1:
                skip_u(k - 1)
        skip_u(KD - 1)
        for i in range(4):
            h_, t = divmod(i, 2)
            dve.wait_ge(*s5A.after(f"sig{i}"))
            ins = dve.tensor_tensor(y_sum[:, t, h_ * CHUNK:(h_ + 1) * CHUNK], bank(2 * i), sig[:, i, :], ALU.mult)
        ins.then_inc(*step.one())

    def s5_turn_b_pe(pe):
        pe.wait_ge(*s5V.after("b_wide"))
        for i in range(4):
            part, half = divmod(i, 2)
            for k in range(4):
                s0 = QUAD * (4 * half + k)
                mm = pe.transpose(bank(4 + i)[:, k * P:(k + 1) * P],
                                  b_wide[:, part, s0:s0 + QUAD, :, :].rearrange("p s g h -> p (s g h)"), ident)
            mm.then_inc(*s5P.inc(f"bt{i}"))

    def s5_pe(pe):
        scanned, states = s5_states()

        def outputs(k):
            pe.wait_ge(*s5V.after(f"ct{k}"))
            pe.wait_ge(*s5G.after(f"x{k}"))
            if k >= 2:
                pe.wait_ge(*s5V.after(f"y{k - 2}"))
            for j in range(QUAD):
                for i in range(2):
                    mm = pe.matmul(bank(6 + k % 2)[:, 0:SEQ], CT[k % 2][:, i, j, :], states[:, k % 2, i, j, :],
                                   start=j == 0 and i == 0, stop=j == QUAD - 1 and i == 1)
            mm.then_inc(*s5P.inc(f"y{k}"))

        pe.wait_ge(*s5A.after("bt3"))
        for k in range(KD):
            if k >= 1:
                pe.wait_ge(*s5V.after(f"w{k - 1}"))
            for j in range(QUAD):
                own_rows = slice(32 * j, 32 * j + 32)
                for i in range(2):
                    mm = pe.matmul(bank(j)[:, i * SEQ:(i + 1) * SEQ], BT[own_rows, i, k, :], xT[own_rows, k, :],
                                   start=True, stop=True)
            mm.then_inc(*s5P.inc(f"bu{k}"))
            if k == 0:
                pe.wait_ge(s5_landed, 16 * 6)
            if k >= 2:
                pe.wait_ge(*s5V.after(f"ct{k - 2}"))
            for i in range(2):
                mm = pe.transpose(bank(4 + k % 2)[:, i * P:(i + 1) * P], c_nat[:, i, k, :], ident)
            mm.then_inc(*s5P.inc(f"ct{k}"))
            if k >= 1:
                outputs(k - 1)
        outputs(KD - 1)
        pe.wait_ge(*s5A.after("gelu1"))
        pe.wait_ge(s5_landed, 16 * 7)
        for h_ in range(2):
            for gate in range(2):
                pn = PN["s5", "glu", 2 * h_ + gate]
                pe.wait_ge(*landed(pn))
                for t in range(NT):
                    i = 2 * h_ + t
                    dst = bank(2 * i + gate)
                    c0 = gate * D + h_ * CHUNK
                    for k in range(KD):
                        mm = pe.matmul(dst, xT[:, k, t * P:(t + 1) * P], panel(pn, KD, CHUNK)[:, k, :],
                                       start=k == 0, stop=False)
                    if t == NT - 1:
                        mm.then_inc(ring_freed[pn.slot], 1)
                    mm = pe.matmul(dst, ones[0:1, :], z_row[0:1, c0:c0 + CHUNK], start=False, stop=True)
                    if gate:
                        mm.then_inc(*s5P.inc(f"glu{i}"))

    r_logit, r_rest, r_eq, r_one, r_two, r_sel, r_cum = (route[:, :, 8 * i:8 * i + 8] for i in range(7))
    r_v1, r_v2, r_at, r_e, r_w1, r_w2, r_total = (route[:, :, 64 + i:65 + i] for i in range(7))
    r_rank = route[:, :, 72:72 + EXPERTS + 1]
    wide = [P, NT, EXPERTS]
    DENSE_GROUPS = 5 * NG

    cv = Carve(ARENA_FFN)
    xg = cv.take(KD, P)
    scatter = cv.take(NT * P)
    pick = cv.take(NT, P)
    spread = cv.take(NT, P)
    y_part = cv.take(D)

    def route_pe(pe):
        for t in range(NT):
            for k in range(KD):
                mm = pe.matmul(bank(4 + t)[:, 0:EXPERTS], xT[:, k, t * P:(t + 1) * P], router[:, k, :],
                               start=k == 0, stop=k == KD - 1)
        mm.then_inc(route_done, 1)
        pe.wait_ge(chosen, 1)
        pe.matmul(bank(6)[:, 0:EXPERTS], const("upto"), r_sel[:, 0, :], start=True, stop=True)
        pe.matmul(bank(6)[:, EXPERTS:2 * EXPERTS], ones, r_sel[:, 0, :], start=True, stop=False)
        pe.matmul(bank(6)[:, EXPERTS:2 * EXPERTS], const("upto"), r_sel[:, 1, :], start=False, stop=True)
        for t in range(NT):
            mm = pe.matmul(bank(6)[:, 2 * EXPERTS:3 * EXPERTS], ones, r_sel[:, t, :], start=t == 0, stop=t == NT - 1)
        mm.then_inc(ranked, 1)

    def route_act(act):
        act.wait_ge(routed, 1)
        act.activation(r_e, r_e, ACT.Exp).then_inc(route_exp, 1)

    def route_dve(dve, step):
        def link(ins):
            ins.then_inc(*step.one())
            dve.wait_ge(*step.now())

        def largest(values, v, one):
            link(dve.tensor_reduce(v, values, AX_X, ALU.max))
            link(dve.tensor_tensor(r_eq, values, v.to_broadcast(wide), ALU.is_ge))
            link(dve.scalar_tensor_tensor(r_eq, numbers, -float(EXPERTS), r_eq, ALU.add, ALU.mult))
            link(dve.tensor_reduce(r_at, r_eq, AX_X, ALU.min))
            link(dve.scalar_tensor_tensor(one, numbers, -float(EXPERTS), r_at.to_broadcast(wide), ALU.add, ALU.is_equal))

        numbers = const("experts").unsqueeze(1).to_broadcast(wide)
        dve.memset(y_sum[:, :, :], 0.0)
        dve.memset(r_rank, -1.0)
        dve.wait_ge(route_done, 1)
        for t in range(NT):
            ins = dve.tensor_copy(r_logit[:, t, :], bank(4 + t)[:, 0:EXPERTS])
        link(ins)
        largest(r_logit, r_v1, r_one)
        link(dve.scalar_tensor_tensor(r_rest, r_one, -3e38, r_logit, ALU.mult, ALU.add))
        largest(r_rest, r_v2, r_two)
        dve.tensor_tensor(r_e, r_v2, r_v1, ALU.subtract).then_inc(routed, 1)
        dve.tensor_tensor(r_sel, r_one, r_two, ALU.add).then_inc(chosen, 1)
        dve.wait_ge(ranked, 1)
        dve.wait_ge(chosen, 1)
        counts = bank(6)[:, 0:2 * EXPERTS].rearrange("p (t e) -> p t e", t=NT)
        link(dve.tensor_tensor(r_cum, counts, r_sel, ALU.mult))
        link(dve.tensor_scalar(r_rank[:, :, 0:EXPERTS], r_cum, 1.0, None, ALU.subtract))
        link(dve.tensor_reduce(r_total[:, 0, :], bank(6)[:, 2 * EXPERTS:3 * EXPERTS], AX_X, ALU.max))
        dve.tensor_scalar(over[:, :], r_total[0:1, 0, :], float(P), None, ALU.is_gt).then_inc(over_ready, 1)
        pick_dve(dve, 0)
        dve.wait_ge(route_exp, 1)
        link(dve.tensor_scalar(r_w1, r_e, 1.0, None, ALU.add))
        link(dve.reciprocal(r_w1, r_w1))
        link(dve.tensor_tensor(r_w2, r_e, r_w1, ALU.mult))
        dve.tensor_tensor(r_one, r_one, r_w1.to_broadcast(wide), ALU.mult)
        link(dve.tensor_tensor(r_two, r_two, r_w2.to_broadcast(wide), ALU.mult))
        dve.tensor_tensor(expert_gate[:, :, :], r_one, r_two, ALU.add).then_inc(moe_added, 1)
        dve.wait_ge(moe_added, 1)

    def slots_used_up(eng):
        eng.wait_ge(over_ready, 1)
        return eng.value_load(over[0:1, 0:1], min_val=0, max_val=1)

    def pick_dve(dve, e):
        slots = const("steps")[:, 0:P]
        for t in range(NT):
            rank = r_rank[:, t, e:e + 1] if isinstance(e, int) else r_rank[:, t, bass.ds(e, 1)]
            ins = dve.tensor_scalar(pick[:, t, :], slots, rank, None, ALU.is_equal)
        ins.then_inc(pick_ready, 1)

    def spread_dve(dve, e):
        slots = const("steps")[:, 0:P]
        for t in range(NT):
            ins = dve.tensor_scalar(spread[:, t, :], slots, r_rank[:, t, bass.ds(e, 1)], expert_gate[:, t, bass.ds(e, 1)],
                                    ALU.is_equal, ALU.mult)
        ins.then_inc(spread_ready, 1)

    def gather_pe(pe, e):
        pe.wait_ge(pick_ready, e + 1)
        if not isinstance(e, int):
            pe.wait_ge(spread_copied, e)
        for k in range(KD):
            for t in range(NT):
                mm = pe.matmul(bank(6 + k // 4)[:, (k % 4) * P:(k % 4 + 1) * P], x[:, t, k * P:(k + 1) * P], pick[:, t, :],
                               start=t == 0, stop=t == NT - 1)
        mm.then_inc(gathered, 1)

    def gathered_dve(dve, e):
        dve.wait_ge(gathered, e + 1)
        for k in range(KD):
            ins = dve.tensor_scalar(xg[:, k, :], bank(6 + k // 4)[:, (k % 4) * P:(k % 4 + 1) * P],
                                    mod_col[:, 1, 4, k:k + 1], mod_col[:, 1, 3, k:k + 1], ALU.mult, ALU.add)
        ins.then_inc(xg_ready, 1)

    def turn_spread(pe, e):
        pe.wait_ge(spread_ready, e + 1)
        for t in range(NT):
            mm = pe.transpose(bank(6)[:, t * P:(t + 1) * P], spread[:, t, :], ident)
        mm.then_inc(spread_turned, 1)

    def copy_spread(act, e):
        act.wait_ge(spread_turned, e + 1)
        act.copy(scatter, bank(6)[:, 0:NT * P]).then_inc(spread_copied, 1)

    def expert_pe(pe, e):
        pe.wait_ge(xg_ready, e + 1)
        ffn_pe(pe, None, DENSE_GROUPS + e * NC, "moe", e, 1)
        pe.wait_ge(xg_ready, e + 2)
        for half in range(2):
            pe.wait_ge(half_copied, 2 * e + (half + 1))
            for t in range(NT):
                mm = pe.matmul(bank((6, 2)[half] + t), scatter[:, t * P:(t + 1) * P], y_part[:, half * 512:(half + 1) * 512],
                               start=True, stop=True)
            mm.then_inc(scattered, 1)

    def expert_act(act, e):
        ffn_act(act, DENSE_GROUPS + e * NC, 1, e)
        for half in range(2):
            act.wait_ge(*((half_done, e + 1) if half == 0 else (acc_done, e + 9)))
            act.copy(y_part[:, half * 512:(half + 1) * 512], acc(0, half)).then_inc(half_copied, 1)

    def expert_dve(dve, step, e):
        spread_dve(dve, e)
        dve.wait_ge(gathered, e + 1)
        pick_dve(dve, e + 1)
        ffn_dve(dve, step, None, DENSE_GROUPS + e * NC, "moe", 1)
        gathered_dve(dve, e + 1)
        for half in range(2):
            dve.wait_ge(scattered, 2 * e + (half + 1))
            for t in range(NT):
                part = y_sum[:, t, half * 512:(half + 1) * 512]
                ins = dve.tensor_tensor(part, part, bank((6, 2)[half] + t), ALU.add)
        ins.then_inc(moe_added, 1)
        dve.wait_ge(moe_added, e + 2)

    def moe_add(dve, e):
        dve.wait_ge(acc_done, e + 9)
        for t in range(NT):
            ins = dve.scalar_tensor_tensor(y_sum[:, t, :], acc(t), expert_gate[:, t, bass.ds(e, 1)], y_sum[:, t, :],
                                           ALU.mult, ALU.add)
        ins.then_inc(moe_added, 1)
        dve.wait_ge(moe_added, e + 2)


    ACC_READY = {m: (acc_done, v) for m, v in {0: 1, 1: 2, 2: 3, 3: 4, 4: 5, 5: 6, 6: 7, 7: 8}.items()}
    LAST_Q = max([int(s[2:]) + 1 for s in stages if s.startswith("ln")], default=0)

    def ffn_weights(n):
        if n < 4:
            return A["ffn_wg"][n // 2, n % 2], A["ffn_wu"][n // 2, n % 2], A["ffn_wd"][n // 2, n % 2]
        return A["ffn_w13_2"][0][:, 0:D_FF], A["ffn_w13_2"][0][:, D_FF:2 * D_FF], A["ffn_w2_2"][0]

    block = ctx.enter_context(nc.Block())

    @block.sync
    def _(sp):
        start_sp(sp)
        for st in stages:
            if st.startswith("ffn"):
                ffn_sp(sp, int(st[3:]), *ffn_weights(int(st[3:])))
            elif st.startswith("mix"):
                mix_sp(sp, int(st[3:]))
            elif st == "mlstm":
                mlstm_sp(sp)
            elif st == "s5":
                s5_sp(sp)
            elif st == "moe":
                with sp.Fori(0, EXPERTS) as e:
                    w13 = A["moe_w13_2"][0, e]
                    ffn_sp(sp, "moe", w13[:, 0:D_FF], w13[:, D_FF:2 * D_FF], A["moe_w2_2"][0, e], e)
        sp.wait_ge(x_ready, NT * LAST_Q)
        sp.dma_start(out.rearrange("b (t p) d -> p (b t) d", p=P), x[:, :, :]).then_inc(out_stored, 16)
        sp.wait_ge(out_stored, 16)

    @block.gpsimd
    def _(pool):
        step = Count(pool_step)
        start_pool(pool)
        for st in stages:
            if st.startswith("ffn") and int(st[3:]) < 4:
                if int(st[3:]) == 0:
                    ln_pool(pool, 0)
                gate_pool(pool, int(st[3:]))
            elif st.startswith("ln"):
                m = int(st[2:])
                ln_pool_add(pool, m)
                if f"ln{m + 1}" in stages:
                    ln_pool(pool, m + 1)
                if m == 6 and "s5" in stages:
                    s5_load_pool(pool)
            elif st.startswith("mix"):
                mix_pool(pool, step, int(st[3:]))
            elif st == "mlstm":
                mlstm_pool(pool, step)
            elif st == "s5":
                s5_pool(pool, step)

    @block.scalar
    def _(act):
        step = Count(act_step)
        start_act(act)
        copy_xT_act(act, 0)
        for st in stages:
            if st.startswith("ffn"):
                ffn_act(act, int(st[3:]) * NG)
                if st == "ffn4" and "s5" in stages:
                    s5_discrete_act(act)
            elif st.startswith("ln"):
                m = int(st[2:])
                ln_act(act, m)
                if m < 5:
                    copy_xT_act(act, m + 1)
            elif st.startswith("mix"):
                mix_act(act, step, int(st[3:]))
            elif st == "mlstm":
                mlstm_act(act, step)
            elif st == "s5":
                s5_act(act, step)
            elif st == "moe":
                route_act(act)
                with act.If(slots_used_up(act) < 1):
                    with act.Fori(0, EXPERTS) as e:
                        expert_act(act, e)
                with act.Else():
                    with act.Fori(0, EXPERTS) as e:
                        ffn_act(act, DENSE_GROUPS + e * NG)

    @block.vector
    def _(dve):
        step = Count(dve_step)
        start_dve(dve)
        for st in stages:
            if st.startswith("ffn"):
                ffn_dve(dve, step, int(st[3:]), int(st[3:]) * NG, int(st[3:]))
                if st == "ffn4" and "s5" in stages:
                    s5_discrete_dve(dve, step)
            elif st.startswith("ln"):
                m = int(st[2:])
                if m in ACC_READY:
                    ln_dve(dve, step, m, acc, ACC_READY[m])
                elif m == 8:
                    ln_dve(dve, step, m, lambda t: y_sum[:, t, :], step.now())
                else:
                    ln_dve(dve, step, m, lambda t: y_sum[:, t, :], (moe_added, EXPERTS + 1))
                if 5 <= m < 9:
                    copy_xT_dve(dve, m + 1)
            elif st.startswith("mix"):
                mix_dve(dve, step, int(st[3:]))
            elif st == "mlstm":
                mlstm_dve(dve, step)
            elif st == "s5":
                s5_dve(dve, step)
            elif st == "moe":
                route_dve(dve, step)
                with dve.If(slots_used_up(dve) < 1):
                    gathered_dve(dve, 0)
                    with dve.Fori(0, EXPERTS) as e:
                        expert_dve(dve, step, e)
                with dve.Else():
                    with dve.Fori(0, EXPERTS) as e:
                        ffn_dve(dve, step, None, DENSE_GROUPS + e * NG, "moe")
                        moe_add(dve, e)

    @block.tensor
    def _(pe):
        start_pe(pe)
        q = 0
        for st in stages:
            if st.startswith("ffn"):
                wait_xT(pe, q)
                ffn_pe(pe, int(st[3:]), int(st[3:]) * NG, int(st[3:]))
            elif st.startswith("ln"):
                q = int(st[2:]) + 1
                if q < 10:
                    turn_x(pe, q)
                if q == 8 and "s5" in stages:
                    s5_turn_b_pe(pe)
            elif st.startswith("mix"):
                wait_xT(pe, q)
                mix_pe(pe, int(st[3:]))
            elif st == "mlstm":
                wait_xT(pe, q)
                mlstm_pe(pe)
            elif st == "s5":
                wait_xT(pe, q)
                s5_pe(pe)
            elif st == "moe":
                wait_xT(pe, q)
                route_pe(pe)
                with pe.If(slots_used_up(pe) < 1):
                    pe.wait_ge(over_ready, 1)
                    gather_pe(pe, 0)
                    with pe.Fori(0, EXPERTS) as e:
                        expert_pe(pe, e)
                with pe.Else():
                    with pe.Fori(0, EXPERTS) as e:
                        ffn_pe(pe, None, DENSE_GROUPS + e * NG, "moe", e)


INPUTS = ["x", "ln_g", "ln_b", "ffn_wg", "ffn_wu", "ffn_wd", "w_in", "w_out", "cmp_pe", "cmp_w1", "cmp_w2", "pool_w",
          "pool_scale", "gla_wa2", "gla_ba", "gla_norm_g", "c_2", "ada_w_2", "ada_b_2", "ln_mix_g_2", "ln_mix_b_2",
          "ln_ffn_g_2", "ln_ffn_b_2", "mlstm_w_in_2", "mlstm_conv_w_2", "mlstm_conv_b_2", "mlstm_wq_2", "mlstm_wk_2",
          "mlstm_wv_2", "mlstm_w_gates_2", "mlstm_b_gates_2", "mlstm_norm_w_2", "mlstm_skip_2", "mlstm_w_out_2",
          "ffn_w13_2", "ffn_w2_2", "s5_lambda_re_2", "s5_lambda_im_2", "s5_b_re_2", "s5_b_im_2", "s5_c_re_2",
          "s5_c_im_2", "s5_d_2", "s5_log_dt_2", "s5_w_glu_2", "s5_b_glu_2", "moe_router_2", "moe_w13_2", "moe_w2_2"]


def prepare(nc, inputs, upto=None):
    const_at, consts = shape_constants()
    arrays = {"in_" + name: np.ascontiguousarray(inputs[name]) for name in INPUTS}
    arrays["in_consts"] = consts
    A = {name[3:]: nc.dram_tensor(name, a.shape, mybir.dt.from_np(a.dtype), kind="ExternalInput").ap()
         for name, a in arrays.items()}
    out = nc.dram_tensor("out", (1, SEQ, D), F32, kind="ExternalOutput").ap()
    build_program(nc, A, out, const_at, upto)
    return arrays


def kernel(**inputs):
    import concourse.bacc as bacc
    from concourse.bass_utils import run_bass_kernel_spmd

    nc = bacc.Bacc("TRN2", target_bir_lowering=False, num_devices=1)
    arrays = prepare(nc, inputs)
    result = run_bass_kernel_spmd(nc, [arrays], core_ids=[0])
    return result.results[0]["out"]
```

```python
from contextlib import ExitStack

import numpy as np

import concourse.bass as bass
from concourse import mybir

F32 = mybir.dt.float32
F32R = mybir.dt.float32r
U32 = mybir.dt.uint32
ALU = mybir.AluOpType
ACT = mybir.ActivationFunctionType
AX_X = mybir.AxisListType.X

P = 128
SEQ = 256
NT = SEQ // P
D = 1024
KD = D // P
DEPTH = 2
D_FF = 2816
CHUNK = 512
CHUNKS = [(c, min(CHUNK, D_FF - c)) for c in range(0, D_FF, CHUNK)]
NC = len(CHUNKS)
NG = NC * NT
FT = D_FF // P
ALPHA = (2.0 * DEPTH) ** 0.25
LN_EPS = 1e-5
RMS_EPS = 1e-6
NEG = -1e30

HEADS, HD, GROUPS = 8, 64, 2
REP = HEADS // GROUPS
CMP_BLOCK, CMP_STRIDE = 32, 16
N_CMP = SEQ // CMP_STRIDE - 1
POOL_WINDOWS = (2, 4, 8, 16)
GLA_H, GLA_K, GLA_V, GLA_CHUNK, GLA_TAU = 4, 32, 64, 64, 16.0
IN_SIZES = [("nq", 512), ("kc", 128), ("vc", 128), ("ks", 128), ("vs", 128), ("kw", 128), ("vw", 128),
            ("gl", 24), ("u", 256), ("gq", 128), ("gk", 128), ("gv", 256), ("ga", 16), ("gr", 256)]
D_IN = sum(n for _, n in IN_SIZES)
IN_PANELS = [(0, 512), (512, 512), (1024, 280), (1304, 512), (1816, 272), (2088, 256)]

ML_INNER, ML_HEADS, ML_CONV, QKV_BLOCK = 2 * D, 4, 4, 4
ML_HD = ML_INNER // ML_HEADS
ML_T = ML_INNER // P
S5_G, S5_H, S5_P = 64, 16, 64
S5_T = S5_G * S5_P // P
EXPERTS = 8

ROUND = 1.5 * 2 ** 23

SLOTS = 4
SLOT = KD * CHUNK


def shape_constants():
    p = np.arange(P)[:, None]
    f = np.arange(P)[None, :]
    t = np.arange(SEQ)
    parts = {}
    parts["ident"] = (p == f)
    parts["ones"] = np.ones((P, P))
    parts["upto"] = (p <= f)
    causal = np.where(f <= p, 0.0, NEG)
    parts["causal"] = np.concatenate([np.zeros((P, P)), causal], 1)
    n = np.arange(CMP_STRIDE)
    end = n * CMP_STRIDE + CMP_BLOCK - 1
    seen = np.stack([(end[None, :] <= p + P * i) & (n[None, :] < N_CMP) for i in range(NT)], 1)
    parts["cmp_seen"] = seen.reshape(P, -1)
    parts["cmp_bias"] = np.where(seen, 0.0, NEG).reshape(P, -1)
    parts["head_rows"] = (p // CMP_STRIDE == np.arange(HEADS)[None, :])
    parts["blk4"] = (p // QKV_BLOCK == np.arange(P // QKV_BLOCK)[None, :])
    bands = []
    for w in POOL_WINDOWS:
        s = np.arange(SEQ)[:, None]
        band = ((s <= t) & (s > t - w)) / np.minimum(w, t + 1.0)[None, :] - (s == t)
        bands += [band[0:P, :], band[P:, P:]]
    parts["bands"] = np.concatenate(bands, 1)
    parts["gla_keep"] = ((p <= f) & (p // GLA_CHUNK == f // GLA_CHUNK))
    parts["gla_go"] = np.tile((t % GLA_CHUNK != 0)[None, :], (P, 1))
    parts["steps"] = np.tile(t[None, :], (P, 1))
    parts["b_own"] = (p // S5_P == np.arange(2)[None, :])
    grp = np.arange(P)[None, None, :] // S5_H
    parts["c_own"] = (grp == 2 * np.arange(4)[None, :, None] + (np.arange(P) // S5_P)[:, None, None]).reshape(P, -1)
    parts["experts"] = np.tile(np.arange(EXPERTS)[None, :], (P, 1))
    at, cols, start = {}, [], 0
    for name, a in parts.items():
        a = np.asarray(a, np.float32)
        at[name] = (start, a.shape[1])
        cols.append(a)
        start += a.shape[1]
    return at, np.ascontiguousarray(np.concatenate(cols, 1))


class Count:

    def __init__(self, sem):
        self.sem, self.value = sem, 0

    def one(self):
        self.value += 1
        return self.sem, 1

    def now(self):
        return self.sem, self.value


class Events:

    def __init__(self, sem, names):
        self.sem, self.names = sem, list(names)
        self.at = {n: i + 1 for i, n in enumerate(self.names)}
        assert len(self.at) == len(self.names)
        self.made = 0

    def inc(self, name, rep=0):
        assert self.at[name] + rep * len(self.names) == self.made + 1, (name, self.names[self.made % len(self.names)])
        self.made += 1
        return self.sem, 1

    def after(self, name, rep=0):
        return self.sem, rep * len(self.names) + self.at[name]


class Panel:

    def __init__(self, slot, landed, over, before):
        self.slot, self.landed, self.over, self.before = slot, landed, over, before


class Ring:

    def __init__(self, freed):
        self.freed, self.uses, self.landed = freed, [0] * (SLOTS + 1), [0] * (SLOTS + 1)
        self.over, self.next = [None] * (SLOTS + 1), 0

    def take(self, slot=None, dmas=1, over=None):
        if slot is None:
            slot = self.next
            self.next = (slot + 1) % SLOTS
        self.landed[slot] += 16 * dmas
        if over is None:
            self.uses[slot] += 1
            over = self.freed[slot], self.uses[slot]
        before, self.over[slot] = self.over[slot], over
        return Panel(slot, self.landed[slot], over, before)


TAIL = SLOTS

FFN_PANELS = []
for _c in range(NC - 1):
    FFN_PANELS += [("g", _c, 4 * _c, 2), ("u", _c, 4 * _c + 2, 2)]
FFN_PANELS += [("g", NC - 1, 4 * NC - 4, 2)]
UP_HALVES = 4 * NC - 2
MOD_LATE = {UP_HALVES - 1: NC - 2, UP_HALVES + 1: NC - 1}
for _f in range(0, FT, 4):
    if _f + 6 < FT:
        FFN_PANELS += [("d", _f, UP_HALVES + _f // 2, 2)]
    else:
        FFN_PANELS += [("d", _g, UP_HALVES + _g // 2, 1) for _g in range(_f, min(_f + 4, FT), 2)]
FFN_HALVES = UP_HALVES + FT // 2
GATE_END = {(4 * c + 1 if c < NC - 1 else UP_HALVES - 2): c for c in range(NC)}
UP_END = {(4 * c + 3 if c < NC - 1 else UP_HALVES - 1): c for c in range(NC)}
HALF = SLOT // 2
UPPERS = 3
STAGES = ["ffn0", "ln0", "mix0", "ln1", "ffn1", "ln2", "ffn2", "ln3", "mix1", "ln4", "ffn3", "ln5",
          "mlstm", "ln6", "ffn4", "ln7", "s5", "ln8", "moe", "ln9"]


def build_program(nc, A, out, const_at, upto=None):
    stages = STAGES if upto is None else STAGES[:STAGES.index(upto) + 1]
    with ExitStack() as ctx:
        program(nc, A, out, const_at, stages, ctx)


def program(nc, A, out, const_at, stages, ctx):
    def sb(name, shape, dt=F32):
        return ctx.enter_context(nc.sbuf_tensor(name, shape, dt))

    def sem(name):
        return ctx.enter_context(nc.semaphore(name))

    psum = ctx.enter_context(nc.psum_tensor("psum", [P, 8, 512], F32))
    n_const = sum(n for _, n in const_at.values())
    consts = sb("consts", [P, n_const])

    def const(name):
        start, n = const_at[name]
        return consts[:, start:start + n]

    ident, ones = const("ident"), const("ones")
    x = sb("x", [P, NT, D])
    lnp = sb("lnp", [P, 3, D])
    bn = sb("bn", [P, NT, 2, 6])
    mv = sb("mv", [P, NT, 2])
    std = sb("std", [P, NT])
    rstd = sb("rstd", [P, NT])
    eps = sb("eps", [P, 5])

    cols_a = sb("cols_a", [P, 120])
    cols_b = sb("cols_b", [P, 110])
    lam = sb("lam", [P, 96])
    pe_col = sb("pe_col", [P, DEPTH * 2, CMP_BLOCK])
    cond = sb("cond", [P, KD])
    w2bd = sb("w2bd", [P, DEPTH * 2, P])
    poolbd = sb("poolbd", [P, DEPTH * 2, P])
    gla_wa2 = sb("gla_wa2", [16, DEPTH, P])
    gla_norm = sb("gla_norm", [P, DEPTH, GLA_H * GLA_V])
    qkv_w = sb("qkv_w", [P, 3, ML_T, QKV_BLOCK])
    gate_w = sb("gate_w", [P, 3 * ML_T, 2 * ML_HEADS])
    gate_b = sb("gate_b", [P, 2 * ML_HEADS])
    ada_gb = sb("ada_gb", [8, CHUNK])
    over = sb("over", [1, 1], mybir.dt.int32)
    router = sb("router", [P, KD, EXPERTS])
    mod_col = sb("mod_col", [P, DEPTH, 6, KD])
    gate_dram = nc.dram_tensor("gate_rows", [4, D], F32, kind="Internal").ap()

    ARENA = 18480
    places = (("ring", [P, SLOTS, SLOT]), ("tail", [P, HALF]), ("xT", [P, KD, SEQ]), ("z", [P, NT, D]), ("arena", [P, ARENA]))
    with ExitStack() as named:
        ring, tail, xT, z, arena = (named.enter_context(nc.sbuf_tensor(n, shape, F32)) for n, shape in places)
    ring_r, tail_r, xT_r, z_r, arena_r = (sb(n + "_r", shape, F32R) for n, shape in places)

    class Carve:

        def __init__(self, start=0, end=ARENA, of=None):
            self.at, self.end, self.of = start, end, arena if of is None else of

        def take(self, *dims, parts=P):
            n = int(np.prod(dims))
            v = self.of[0:parts, self.at:self.at + n]
            self.at += n
            assert self.at <= self.end, (self.at, self.end)
            if len(dims) == 1:
                return v
            names = "abcd"[:len(dims)]
            return v.rearrange(f"p ({' '.join(names)}) -> p {' '.join(names)}", **dict(zip(names[1:], dims[1:])))

    cv = Carve()
    cols_a_nat = cv.take(P)
    cols_b_nat = cv.take(P)
    lam_nat = cv.take(P, parts=96)
    dt_nat = cv.take(2, parts=96)
    pe_nat = cv.take(DEPTH * 2, 2, HD, parts=CMP_BLOCK)

    ring_landed = [sem(f"ring_landed{i}") for i in range(SLOTS + 1)]
    ring_freed = [sem(f"ring_freed{i}") for i in range(SLOTS + 1)]
    x_landed, consts_landed, params_landed = sem("x_landed"), sem("consts_landed"), sem("params_landed")
    params_clear = sem("params_clear")
    param_rows = sem("param_rows")
    param_cols = sem("param_cols")
    param_ready = sem("param_ready")
    dve_step, act_step, pool_step = sem("dve_step"), sem("act_step"), sem("pool_step")
    lnp_landed = sem("lnp_landed")
    first_tile_done = sem("first_tile_done")
    acc_done = sem("acc_done")
    var_ready, std_ready = sem("var_ready"), sem("std_ready")
    x_ready = sem("x_ready")
    x_turned, xT_ready = sem("x_turned"), sem("xT_ready")
    upper_ready, lower_ready, halves_used = sem("upper_ready"), sem("lower_ready"), sem("halves_used")
    xh_ready, xl_ready = sem("xh_ready"), sem("xl_ready")
    act_ready, h_ready = sem("act_ready"), sem("h_ready")
    h_turned, hT_ready, hL_ready = sem("h_turned"), sem("hT_ready"), sem("hL_ready")
    ada_landed = [sem(f"ada_landed{j}") for j in range(2)]
    ada_ready, mod_done, mod_ready, gate_row_ready, gate_stored = (
        sem("ada_ready"), sem("mod_done"), sem("mod_ready"), sem("gate_row_ready"), sem("gate_stored"))
    b_landed, c_landed, bias_landed = sem("b_landed"), sem("c_landed"), sem("bias_landed")
    route_done, routed, route_exp = sem("route_done"), sem("routed"), sem("route_exp")
    chosen, ranked, over_ready = sem("chosen"), sem("ranked"), sem("over_ready")
    pick_ready, gathered, xg_ready = sem("pick_ready"), sem("gathered"), sem("xg_ready")
    xu_ready, xgh_ready = sem("xu_ready"), sem("xgh_ready")
    spread_ready, spread_turned, spread_copied = sem("spread_ready"), sem("spread_turned"), sem("spread_copied")
    half_done, half_copied, scattered = sem("half_done"), sem("half_copied"), sem("scattered")
    moe_added = sem("moe_added")
    out_stored = sem("out_stored")
    NPARAM = [0]

    mixP = Events(sem("mix_pe"), ["q0", "q1", "kcvc", "vs", "kskw", "vwgl", "cmp1", "u", "gqk", "gv", "ga", "gr", "pre",
                                  "cmp2", "pool1", "kdT", "pool2", "dS", "at", "gla0", "gla1", "sc", "s0", "pcT", "oc0",
                                  "oc1", "s1", "t0", "s2", "v0", "t1", "s3", "v1", "t2", "s4", "v2", "t3", "s5", "v3",
                                  "t4", "s6", "v4", "t5", "s7", "v5", "t6", "v6", "t7", "v7", "oA0", "oA1", "oC", "wo0"])
    mixA = Events(sem("mix_act"), ["q0", "q1", "vs", "kskw", "vw", "gates", "g1", "ga", "sr", "abs", "ex", "ln1", "pool1",
                                   "eb", "enb", "ekd", "kdT", "pool2", "sq0", "sq1", "ss_std", "pc_exp", "pcT", "e0", "e1",
                                   "pT0", "e2", "pT1", "e3", "pT2", "e4", "pT3", "e5", "pT4", "e6", "pT5", "e7", "pT6",
                                   "pT7", "oT"])
    mixV = Events(sem("mix_dve"), ["zc", "u", "gqk", "gv", "g1rep", "gl_v", "gl_b", "gl_dd", "kcT", "vblk", "gl_kd",
                                   "s_blk", "at", "ss", "pc_bias", "pc_sub", "oC0", "oC1", "pc", "p0", "m0", "oc0", "oc1",
                                   "p1", "m1", "p2", "m2", "ot0_0", "oA0_0", "p3", "m3", "p4", "m4", "ot1_0", "oA1_0",
                                   "p5", "m5", "p6", "m6", "ot0_1", "oA0_1", "p7", "m7", "ot1_1", "oA1_1"])
    mixG = Events(sem("mix_pool"), ["zeros", "sr"])

    eight = range(8)
    mlP = Events(sem("ml_pe"), [f"in{j}" for j in range(16)] + [f"v{j}" for j in eight] + [f"vT{j}" for j in eight] +
                 [f"q{j}" for j in eight] + [f"k{j}" for j in eight] +
                 ["gates", "F", "abc", "S0", "S1", "T0", "n0", "n1", "n2", "n3", "T1", "n4", "n5", "n6", "n7"] +
                 [f"h{j}" for j in eight] + ["wo0", "wo1", "wo2"])
    mlA = Events(sem("ml_act"), ["up0", "up1", "xh0", "xh1"] + [n for j in eight for n in (f"up{j + 2}", f"in{j}")] +
                 [n for j in range(8, 16) for n in (f"up{j + 2}", f"in{j}", f"xc{j - 8}") if n not in ("up16", "up17")] +
                 [f"{n}{j}" for n in ("vT", "q", "k") for j in eight] +
                 ["abs", "ex", "ln1", "skip", "E0", "E1", "em", "T0", "T1", "hstd"])
    mlV = Events(sem("ml_dve"), ["lo0", "xl0", "xl1", "lo1", "bd_v"] + [n for j in eight for n in (f"lo{j + 2}", f"conv{j}")] +
                 [f"lo{j}" for j in range(10, 16)] + ["bd_q"] + [f"v{j}" for j in eight] +
                 ["bd_k", "gts", "logf", "diag", "am0", "am1", "m0", "m1", "sd0", "sd1"] + [f"h{j}" for j in eight] +
                 ["h_mv", "hn"] + [f"hs{j}" for j in eight])
    mlG = Events(sem("ml_pool"), [f"y{j}" for j in eight])

    def s5_order(*names):
        return [f"{n}{k - lag}" for k in range(KD + 2) for n, lag in names if max(0, -lag) <= k - lag < KD]

    s5P = Events(sem("s5_pe"), [f"bt{i}" for i in range(4)] + s5_order(("bu", 0), ("ct", 1), ("y", 2)) +
                 [f"glu{i}" for i in range(4)])
    s5A = Events(sem("s5_act"), ["dt", "mag", "abs", "cos"] + [f"bt{i}" for i in range(4)] +
                 s5_order(("phase", 0), ("abs", 0), ("rot", 0)) + ["gelu0", "gelu1"] + [f"sig{i}" for i in range(4)])
    s5V = Events(sem("s5_dve"), ["lam_dt", "turn", "b_wide", "angle0"] +
                 s5_order(("w", 0), ("angle", -1), ("scan", 0), ("ct", 1), ("y", 2)))
    s5G = Events(sem("s5_pool"), [f"x{k}" for k in eight])

    rg = Ring(ring_freed)
    PN = {}

    def plan_ffn(key):
        base = FFN_HALVES * (5 if key == "moe" else key)
        for p, (kind, c, first_half, n) in enumerate(FFN_PANELS):
            PN[key, kind, c] = rg.take(p % 3, dmas=2 if (kind, c) == ("g", NC - 1) else 1,
                                       over=(halves_used, base + first_half + n))
        PN[key, "u", NC - 1] = PN[key, "g", NC - 1]
        PN[key, "upper"] = [rg.take(slot, dmas=0, over=(halves_used, base + FFN_HALVES)) for slot in (3, TAIL)]
        rg.next = 2

    STRIDE = {}
    for st in stages:
        if st.startswith("ffn"):
            plan_ffn(int(st[3:]))
        elif st.startswith("mix"):
            l = int(st[3:])
            for i in range(len(IN_PANELS)):
                if i == 3:
                    PN["mix", l, "w1"] = rg.take(dmas=4, over=mixP.after("cmp1", l))
                last_use = ("q1", "vs", "vwgl", "gqk", "ga", "gr")[i]
                PN["mix", l, "in", i] = rg.take(dmas=HEADS if i == 0 else 1, over=mixP.after(last_use, l))
            PN["mix", l, "out", 0] = rg.take(over=mixP.after("wo0", l))
            PN["mix", l, "out", 1] = rg.take(over=(acc_done, 1 + l))
        elif st == "mlstm":
            for i in range(8):
                PN["ml", "in", i] = rg.take(i % 3, over=mlP.after(f"in{2 * i + 1}"))
            PN["ml", "upper"] = [rg.take(slot, dmas=0, over=mlP.after("in15")) for slot in (3, TAIL)]
            rg.next = 0
            for name, last_use in (("q", "S1"), ("h", "h7"), ("s", "n7")):
                PN["ml", "scratch_" + name] = rg.take(dmas=0, over=mlP.after(last_use))
            for i in range(4):
                PN["ml", "out", i] = rg.take(over=mlP.after(f"wo{i}") if i < 3 else (acc_done, 3))
        elif st == "s5":
            for name in "sx":
                PN["s5", "scratch_" + name] = rg.take(dmas=0, over=s5P.after("y7") if name == "x" else s5G.after("x7"))
            for i in range(4):
                PN["s5", "glu", i] = rg.take()
        elif st == "moe":
            MOE_BEFORE = list(rg.over)
            before = list(rg.landed)
            plan_ffn("moe")
            STRIDE["landed"] = [b - a for a, b in zip(before, rg.landed)]
            for p in range(3):
                sem_, n = rg.over[p]
                PN[("moe",) + FFN_PANELS[p][:2]].before = sem_, n - FFN_HALVES

    def slot_of(pn):
        return tail if pn.slot == TAIL else ring[:, pn.slot, :]

    def landed(pn, e=None):
        n = pn.landed if e is None else e * STRIDE["landed"][pn.slot] + pn.landed
        return ring_landed[pn.slot], n

    def panel(pn, k, w, first=0):
        return slot_of(pn)[:, first:first + k * w].rearrange("p (k w) -> p k w", w=w)

    def load_panel(sp, pn, pieces, e=None):
        if pn.before is not None:
            freed, n = pn.before
            sp.wait_ge(freed, n if e is None else e * FFN_HALVES + n)
        for dst, src in pieces:
            sp.dma_start(dst, src).then_inc(ring_landed[pn.slot], 16)

    def rows(w):
        return w.rearrange("(k p) n -> p k n", p=P)

    cols_a_at = dict(conv_w=0, conv_b=64, norm_w=80, skip=96, s5_d=112)
    cols_b_at = dict(ada_b=0, c=96, pool_scale=104, gla_ba=108)

    def start_sp(sp):
        sp.dma_start(ident, A["consts"][:, 0:P]).then_inc(consts_landed, 16)
        sp.dma_start(x[:, :, :], A["x"].rearrange("b (t p) d -> p (b t) d", p=P)).then_inc(x_landed, 16)

    def start_act(act):
        def load(dst, src):
            act.dma_start(dst, src).then_inc(params_landed, 16)
            NPARAM[0] += 16

        load(consts[:, P:], A["consts"][:, P:])
        load(cols_b_nat[0:96, :], A["ada_b_2"].rearrange("l (r p) -> (l r) p", p=P))
        load(cols_b_nat[96:104, :], A["c_2"].rearrange("b (r p) -> (b r) p", p=P))
        load(cols_b_nat[104:108, :], A["pool_scale"].rearrange("l (r p) -> (l r) p", p=P))
        load(cols_b_nat[108:110, :], A["gla_ba"])
        load(cols_a_nat[0:64, :], A["mlstm_conv_w_2"].rearrange("l k (r p) -> (l k r) p", p=P))
        load(cols_a_nat[64:80, :], A["mlstm_conv_b_2"].rearrange("l (r p) -> (l r) p", p=P))
        load(cols_a_nat[80:96, :], A["mlstm_norm_w_2"].rearrange("l (r p) -> (l r) p", p=P))
        load(cols_a_nat[96:112, :], A["mlstm_skip_2"].rearrange("l (r p) -> (l r) p", p=P))
        load(cols_a_nat[112:120, :], A["s5_d_2"].rearrange("l (r p) -> (l r) p", p=P))
        load(lam_nat[0:32, :], A["s5_lambda_re_2"].rearrange("l (s g) p -> (l s) (g p)", g=2))
        load(lam_nat[32:64, :], A["s5_lambda_im_2"].rearrange("l (s g) p -> (l s) (g p)", g=2))
        load(dt_nat[64:96, :], A["s5_log_dt_2"].rearrange("l (s g) -> (l s) g", g=2))
        for i in range(2):
            load(pe_nat[:, :, i, :], A["cmp_pe"].rearrange("l v j d -> j (l v) d"))
        act.wait_ge(params_clear, 2)
        for i in range(2):
            half = slice(i * HD, (i + 1) * HD)
            load(w2bd[half, :, half], A["cmp_w2"].rearrange("l v i o -> i (l v) o"))
            load(poolbd[half, :, half], A["pool_w"].rearrange("l (t h) i o -> h i (l t) o", h=2)[i])
        load(gla_wa2[:, :, :], A["gla_wa2"].rearrange("l r n -> r l n"))
        for l in range(DEPTH):
            load(gla_norm[:, l, :], A["gla_norm_g"][l].partition_broadcast(P))
        for i, name in enumerate(("mlstm_wq_2", "mlstm_wk_2", "mlstm_wv_2")):
            load(qkv_w[:, i, :, :], A[name][0].rearrange("(t n) i o -> (n i) t o", n=P // QKV_BLOCK))
        load(gate_w[:, :, :], rows(A["mlstm_w_gates_2"][0]))
        load(gate_b[:, :], A["mlstm_b_gates_2"][0].partition_broadcast(P))
        ada_b = A["ada_b_2"].rearrange("l (v r n) -> l v r n", v=6, n=CHUNK)
        for l in range(DEPTH):
            for w in range(2):
                load(ada_gb[4 * l + 2 * w:4 * l + 2 * w + 2, :], ada_b[l, 2 + 3 * w])
        load(router[:, :, :], rows(A["moe_router_2"][0]))

    def columns_act(act):
        act.wait_ge(param_cols, 4)
        act.copy(cols_a[:, :], psum[:, 0, 0:120]).then_inc(param_ready, 1)
        act.copy(cols_b[:, :], psum[:, 1, 0:110]).then_inc(param_ready, 1)
        act.copy(lam[:, :], psum[:, 2, 0:96]).then_inc(param_ready, 1)
        act.copy(pe_col[:, :, :], psum[:, 3, 0:4 * CMP_BLOCK].rearrange("p (v j) -> p v j", v=4)).then_inc(param_ready, 1)
        act.wait_ge(param_ready, 4)
        act.activation(cond[:, :], cols_b[:, 96:104], ACT.Silu).then_inc(param_ready, 1)

    def start_pool(pool):
        pool.memset(w2bd[:, :, :], 0.0).then_inc(params_clear, 1)
        pool.memset(poolbd[:, :, :], 0.0).then_inc(params_clear, 1)

    def start_dve(dve):
        dve.memset(eps[:, 0:1], 4.0 * LN_EPS)
        dve.memset(eps[:, 1:2], LN_EPS)
        dve.memset(eps[:, 3:4], np.pi / 2)
        dve.memset(eps[:, 4:5], ROUND)
        dve.memset(eps[:, 2:3], RMS_EPS).then_inc(param_rows, 1)

    def columns_dve(dve):
        dve.wait_ge(params_landed, NPARAM[0])
        dve.tensor_copy(lam_nat[64:96, :].rearrange("s (g p) -> s g p", g=2),
                        dt_nat[64:96, :].unsqueeze(2).to_broadcast([32, 2, S5_P])).then_inc(param_rows, 1)

    def start_pe(pe):
        pe.wait_ge(consts_landed, 16)
        pe.wait_ge(x_landed, 16)
        turn_x(pe, 0)

    def columns_pe(pe):
        pe.wait_ge(params_landed, NPARAM[0])
        pe.wait_ge(param_rows, 2)
        pe.transpose(psum[:, 0, 0:120], cols_a_nat[0:120, :], ident[0:120, 0:120]).then_inc(param_cols, 1)
        pe.transpose(psum[:, 1, 0:110], cols_b_nat[0:110, :], ident[0:110, 0:110]).then_inc(param_cols, 1)
        pe.transpose(psum[:, 2, 0:96], lam_nat[:, :], ident[0:96, 0:96]).then_inc(param_cols, 1)
        for v in range(4):
            last = pe.transpose(psum[:, 3, v * CMP_BLOCK:(v + 1) * CMP_BLOCK],
                                pe_nat[:, v, :, :].rearrange("j a d -> j (a d)"), ident[0:CMP_BLOCK, 0:CMP_BLOCK])
        last.then_inc(param_cols, 1)

    def turn_x(pe, q):
        for t in range(NT):
            if q > 0:
                pe.wait_ge(x_ready, NT * (q - 1) + t + 1)
            for b in range(2):
                for k in range(4):
                    last = pe.transpose(psum[:, 2 * t + b, k * P:(k + 1) * P],
                                        x[:, t, (4 * b + k) * P:(4 * b + k + 1) * P], ident)
                last.then_inc(x_turned, 1)

    def copy_xT_act(act, q):
        for i in range(2 * NT):
            t, b = divmod(i, 2)
            act.wait_ge(x_turned, 4 * q + i + 1)
            dst = xh[:, t, 4 * b:4 * b + 4, :] if q in FFN_OF else \
                xT[:, 4 * b:4 * b + 4, t * P:(t + 1) * P]
            act.copy(dst, psum[:, i, :].rearrange("p (k n) -> p k n", k=4)).then_inc(xT_ready, 1)

    def modulate(eng, q, i):
        l, w = divmod(q - 6, 2)
        t, b = divmod(i, 2)
        eng.wait_ge(x_turned, 4 * q + i + 1)
        for k in range(4):
            dst, src = xT[:, 4 * b + k, t * P:(t + 1) * P], psum[:, i, k * P:(k + 1) * P]
            scale, shift = (mod_col[:, l, 3 * w + v, 4 * b + k:4 * b + k + 1] for v in (1, 0))
            if eng is nc.scalar:
                last = eng.activation(dst, src, ACT.Identity, scale=scale, bias=shift)
            else:
                last = eng.tensor_scalar(dst, src, scale, shift, ALU.mult, ALU.add)
        last.then_inc(xT_ready, 1)

    def modulate_act(act, q):
        act.wait_ge(mod_ready, 24)
        for i in range(3):
            modulate(nc.scalar, q, i)

    def modulate_dve(dve, q):
        modulate(nc.vector, q, 3)

    def split_xT_dve(dve, q):
        for i in range(2 * NT):
            t, b = divmod(i, 2)
            part = slice(4 * b, 4 * b + 4), slice(t * P, (t + 1) * P)
            dve.wait_ge(xT_ready, 4 * q + i + 1)
            dve.tensor_tensor(xT_r[:, part[0], part[1]], psum[:, i, :].rearrange("p (k n) -> p k n", k=4),
                              xh[:, t, part[0], :], ALU.subtract).then_inc(xl_ready, 1)

    def split_u_act(act, n):
        act.wait_ge(xT_ready, 4 * (8 if n == 0 else 10))
        for t in range(NT):
            ins = act.copy(xh[:, t, :, :], xT[:, :, t * P:(t + 1) * P])
        ins.then_inc(xh_ready, 1)

    def split_u_dve(dve, n):
        dve.wait_ge(xh_ready, n + 1)
        for t in range(NT):
            part = slice(t * P, (t + 1) * P)
            ins = dve.tensor_tensor(xT_r[:, :, part], xT[:, :, part], xh[:, t, :, :], ALU.subtract)
        ins.then_inc(xl_ready, 4)

    def wait_xT(pe, q):
        pe.wait_ge(xT_ready, 4 * q + 4)

    def ln_pool(pool, m):
        if m > 0:
            pool.wait_ge(x_ready, NT * m)
        if m < 6:
            g, b = A["ln_g"][m // 3, m % 3], A["ln_b"][m // 3, m % 3]
        else:
            which = "ffn" if m % 2 else "mix"
            g, b = A[f"ln_{which}_g_2"][(m - 6) // 2], A[f"ln_{which}_b_2"][(m - 6) // 2]
        pool.dma_start(lnp[:, 0, :], g.partition_broadcast(P)).then_inc(lnp_landed, 16)
        pool.dma_start(lnp[:, 1, :], b.partition_broadcast(P)).then_inc(lnp_landed, 16)
        if m >= 6:
            pool.wait_ge(gate_stored, 16 * 8)
            pool.dma_start(lnp[:, 2, :], gate_dram[m - 6].partition_broadcast(P)).then_inc(lnp_landed, 16)

    def lnp_count(m):
        return 16 * (2 * (m + 1) + max(0, m - 5))

    def ln_dve(dve, step, m, source, ready):
        half = m in (0, 2, 3, 5)
        dve.wait_ge(*ready[0])
        if m >= 6:
            dve.wait_ge(lnp_landed, lnp_count(m))
        def residual(t):
            y = source(t)
            if m >= 6:
                dve.tensor_tensor(z[:, t, :], y, lnp[:, 2, :], ALU.mult).then_inc(*step.one())
                dve.wait_ge(*step.now())
                y = z[:, t, :]
            dve.scalar_tensor_tensor(z[:, t, :], x[:, t, :], 2 * ALPHA if half else ALPHA, y, ALU.mult,
                                     ALU.add).then_inc(*step.one())
            dve.wait_ge(*step.now())

        def statistics(t):
            for i in range(2):
                dve.bn_stats(bn[:, t, i, :], z[:, t, i * 512:(i + 1) * 512]).then_inc(*step.one())
            dve.wait_ge(*step.now())
            dve.bn_aggr(mv[:, t, :], bn[:, t, :, :].rearrange("p a b -> p (a b)")).then_inc(var_ready, 1)

        def center(t):
            dve.scalar_tensor_tensor(z[:, t, :], z[:, t, :], mv[:, t, 0:1], lnp[:, 0, :], ALU.subtract,
                                     ALU.mult).then_inc(*step.one())

        def scale(t):
            dve.wait_ge(std_ready, NT * m + t + 1)
            dve.reciprocal(rstd[:, t:t + 1], std[:, t:t + 1]).then_inc(*step.one())
            dve.wait_ge(*step.now())
            dve.wait_ge(x_turned, 4 * m + 4)
            dve.scalar_tensor_tensor(x[:, t, :], z[:, t, :], rstd[:, t:t + 1], lnp[:, 1, :], ALU.mult,
                                     ALU.add).then_inc(x_ready, 1)

        residual(0)
        statistics(0)
        dve.wait_ge(lnp_landed, lnp_count(m))
        dve.wait_ge(var_ready, NT * m + 1)
        center(0)
        scale(0)
        dve.wait_ge(*ready[1])
        residual(1)
        statistics(1)
        dve.wait_ge(var_ready, NT * m + 2)
        center(1)
        scale(1)

    def ln_act(act, m):
        half = m in (0, 2, 3, 5)
        if m == 0:
            act.wait_ge(param_rows, 1)
        for t in range(NT):
            act.wait_ge(var_ready, NT * m + t + 1)
            act.activation(std[:, t:t + 1], mv[:, t, 1:2], ACT.Sqrt,
                           bias=eps[:, 0:1] if half else eps[:, 1:2]).then_inc(std_ready, 1)

    def acc(t, half=None):
        if half is None:
            return psum[:, 4 + 2 * t:6 + 2 * t, :].rearrange("p b n -> p (b n)")
        return psum[:, 4 + 2 * t + half, :]

    FFN_OF = {0: 0, 2: 1, 3: 2, 5: 3, 7: 4}
    cv = Carve(of=arena_r)
    hT = cv.take(FT, SEQ)
    hTl = cv.take(FT, SEQ)
    cv = Carve(cv.at)
    act_g = cv.take(2, CHUNK)
    h = cv.take(2, CHUNK)
    ada_acc = cv.take(CHUNK)
    ada_w = cv.take(2, KD, CHUNK // 2)
    ada_w_end = cv.at
    cv = Carve(ada_w_end - 2 * HALF)
    y_sum = cv.take(NT, D)
    y_end = cv.at
    expert_gate = cv.take(NT, EXPERTS)
    route = cv.take(NT, 128)
    gate_row = lnp[0:1, 2, :].rearrange("p (a n) -> p a n", a=2)
    xh = z_r[:, :, :].rearrange("p t (k n) -> p t k n", k=KD)
    upper = [ring_r[:, 3, 0:HALF], ring_r[:, 3, HALF:], tail_r[:, :]]
    cv = Carve(of=arena_r)
    hT_slots, hTl_slots = cv.take(FT, P), cv.take(FT, P)
    xg = cv.take(KD, P)
    xu = Carve(cv.at).take(KD, P)
    xgl = cv.take(KD, P)
    cv = Carve(cv.at)
    scatter = cv.take(NT * P)
    pick = cv.take(NT, P)
    spread = cv.take(NT, P)
    y_part = cv.take(D)

    class Pass:

        def __init__(self, key, tiles=NT, e=None):
            self.key, self.tiles, self.e = key, tiles, e
            self.n = key if isinstance(key, int) else None
            runs = key if e is None else e + 5
            self.halves = runs * FFN_HALVES
            self.first = key * NG if e is None else e * (NC * tiles) + 5 * NG
            self.hT, self.hTl = (hT, hTl) if tiles == NT else (hT_slots, hTl_slots)

        def next(self):
            return Pass(self.key, self.tiles, self.e + 1)

        def x_parts(self, k, t):
            if self.tiles == 1:
                return xg[:, k, :], xgl[:, k, :]
            return xh[:, t, k, :], xT_r[:, k, t * P:(t + 1) * P]

        def h_parts(self, f, t):
            return self.hT[:, f, t * P:(t + 1) * P], self.hTl[:, f, t * P:(t + 1) * P]

        def banks(self, c, t):
            b = 2 * self.tiles * ((c + 1) % 2) + 2 * t
            return psum[:, b, :], psum[:, b + 1, :]

        def groups(self, c):
            return self.first + self.tiles * (c + 1)

        def before(self, g, lag=2):
            v = self.first + (g - lag + 1)
            return v if not isinstance(v, int) or v > 0 else None

    def half_of(key, i):
        for kind, c, first_half, n in FFN_PANELS:
            if first_half <= i < first_half + n:
                pn = PN[key, kind, c]
                cols = slice(HALF * (i - first_half), HALF * (i - first_half + 1))
                return pn, kind, c, i - first_half, ring[:, pn.slot, cols], ring_r[:, pn.slot, cols]

    def ffn_sp(sp, key, wg, wu, wd, e=None):
        for kind, c, _, n in FFN_PANELS:
            pn = PN[key, kind, c]
            c0, w = CHUNKS[c] if kind != "d" else (0, 0)
            if kind == "d":
                load_panel(sp, pn, [(panel(pn, 2 * n, D), rows(wd)[:, c:c + 2 * n, :])], e)
            elif c < NC - 1:
                load_panel(sp, pn, [(panel(pn, KD, w), rows(wg if kind == "g" else wu)[:, :, c0:c0 + w])], e)
            else:
                load_panel(sp, pn, [(panel(pn, KD, w), rows(wg)[:, :, c0:c0 + w]),
                                    (panel(pn, KD, w, KD * w), rows(wu)[:, :, c0:c0 + w])], e)

    def ffn_pe(pe, r):
        key, e, tiles = r.key, r.e, r.tiles

        def three(dst, parts, rhs, rhs_low, start, stop):
            lhs, lhs_low = parts
            pe.matmul(dst, lhs_low, rhs, start=start, stop=False)
            pe.matmul(dst, lhs, rhs, start=False, stop=False)
            return pe.matmul(dst, lhs, rhs_low, start=False, stop=stop)

        def half_up(i):
            pn, kind, c, j, _, low = half_of(key, i)
            w = CHUNKS[c][1]
            k0, nk = (4 * j, 4) if c < NC - 1 else (0, KD)
            is_gate = kind == "g" and not (c == NC - 1 and j == 1)
            pe.wait_ge(lower_ready, r.halves + (i + 1))
            up_ = upper[i % UPPERS].rearrange("p (k n) -> p k n", n=w)
            low = low.rearrange("p (k n) -> p k n", n=w)
            if i == 0 and r.n is not None:
                if r.n == 4:
                    pe.wait_ge(xh_ready, 1)
                else:
                    wait_xT(pe, [q for q in FFN_OF if FFN_OF[q] == r.n][0])
                for t in range(tiles):
                    for k in range(nk):
                        for w_part in (up_, low):
                            pe.matmul(r.banks(c, t)[0][:, 0:w], r.x_parts(k, t)[0], w_part[:, k, :],
                                      start=k == 0 and w_part is up_, stop=False)
                for t in range(tiles):
                    pe.wait_ge(xl_ready, 4 * r.n + 2 * (t + 1))
                    for k in range(nk):
                        mm = pe.matmul(r.banks(c, t)[0][:, 0:w], r.x_parts(k, t)[1], up_[:, k, :], start=False, stop=False)
                mm.then_inc(halves_used, 1)
                return
            for t in range(tiles):
                dst = r.banks(c, t)[0 if is_gate else 1][:, 0:w]
                for k in range(nk):
                    mm = three(dst, r.x_parts(k0 + k, t), up_[:, k, :], low[:, k, :],
                               k0 + k == 0, k0 + k == KD - 1)
            mm.then_inc(halves_used, 1)

        def half_down(i):
            pn, kind, c, j, _, low = half_of(key, i)
            f0 = c + 2 * j
            pe.wait_ge(lower_ready, r.halves + (i + 1))
            up_ = upper[i % UPPERS].rearrange("p (f n) -> p f n", n=D)
            low = low.rearrange("p (f n) -> p f n", n=D)
            products = [(f, t, half) for f in (f0, f0 + 1) for t in range(tiles) for half in range(2)]
            if tiles == 1 and i == FFN_HALVES - 1:
                products.sort(key=lambda fth: fth[2])
            if tiles == NT and i == FFN_HALVES - 1:
                products.sort(key=lambda fth: fth[1])
            for f, t, half in products:
                cols = slice(half * CHUNK, (half + 1) * CHUNK)
                mm = three(acc(t, half), r.h_parts(f, t), up_[:, f - f0, cols],
                           low[:, f - f0, cols], f == 0, f == FT - 1)
                if tiles == 1 and f == FT - 1 and half == 0:
                    mm.then_inc(half_done, 1)
                if e is None and (f, t, half) == (FT - 1, 0, 1):
                    mm.then_inc(first_tile_done, 1)
            mm.then_inc(halves_used, 1)

        def turn(c):
            for t in range(tiles):
                g = tiles * c + t
                pe.wait_ge(h_ready, r.first + (g + 1))
                for f in range(CHUNKS[c][1] // P):
                    mm = pe.transpose(r.banks(c, t)[0][:, f * P:(f + 1) * P], h[:, g % 2, f * P:(f + 1) * P], ident)
                mm.then_inc(h_turned, 1)

        def mod(c):
            l, a = divmod(r.n * NC + c, 12)
            v, part = divmod(a, 2)
            dst = r.banks(c, 0)[1]
            pe.wait_ge(ada_ready, 2 * (r.n * NC + c + 1))
            if v in (2, 5):
                row = 4 * l + 2 * (v // 3) + part
                pe.matmul(dst[0:1, :], ones[:, 0:1], ada_acc[:, :], start=True, stop=False)
                pe.matmul(dst[0:1, :], ident[0:8, row:row + 1], ada_gb[:, :], start=False, stop=True).then_inc(mod_done, 1)
            else:
                for f in range(4):
                    mm = pe.matmul(dst[:, f:f + 1], ada_acc[:, f * P:(f + 1) * P], ones[:, 0:1], start=True, stop=True)
                mm.then_inc(mod_done, 1)

        has_mod = r.n is not None and r.n < 4
        for i in range(FFN_HALVES):
            if i < UP_HALVES and i % 4 == 0:
                c = i // 4
                if e is not None and c == (0 if tiles == NT else 1):
                    pe.wait_ge(moe_added, e + 1)
                if c >= 2:
                    pe.wait_ge(hL_ready, r.groups(c - 2))
                    if has_mod:
                        pe.wait_ge(mod_ready, r.n * NC + c - 1)
            if i >= UP_HALVES:
                c = (i - UP_HALVES) // 2
                pe.wait_ge(hL_ready, r.groups(max(c, NC - 2)) if c < NC - 1 else r.groups(c))
                if i == UP_HALVES and has_mod:
                    pe.wait_ge(mod_ready, r.n * NC + NC - 1)
            (half_up if i < UP_HALVES else half_down)(i)
            if i in GATE_END and GATE_END[i] > 0 or i == UP_HALVES:
                c = GATE_END[i] - 1 if i in GATE_END else NC - 1
                turn(c)
                if has_mod and c < NC - 2:
                    mod(c)
            if has_mod and i in MOD_LATE:
                mod(MOD_LATE[i])
            if i == 3 and r.n == 0:
                columns_pe(pe)
                pe.wait_ge(param_ready, 4)
            if i == 4 * 2 + 3 and tiles == 1:
                turn_spread(pe, e)
            if i == UP_HALVES - 1 and tiles == 1:
                gather_pe(pe, e + 1)
        if has_mod:
            pe.wait_ge(mod_ready, (r.n + 1) * NC)

    def upper_act(act, r, i):
        pn, _, _, j, raw, _ = half_of(r.key, i)
        if j == 0:
            act.wait_ge(*landed(pn, r.e))
        before = PN[r.key, "upper"][i // 2].before if r.e is None and i < UPPERS else None
        if before is not None and before[0] is not halves_used:
            act.wait_ge(*before)
        elif r.e is not None or r.key * FFN_HALVES + i >= UPPERS:
            act.wait_ge(halves_used, r.halves + (i - UPPERS + 1))
        act.copy(upper[i % UPPERS], raw).then_inc(upper_ready, 1)

    def lower_dve(dve, r, i):
        raw, low = half_of(r.key, i)[4:]
        dve.wait_ge(upper_ready, r.halves + (i + 1))
        dve.tensor_tensor(low, raw, upper[i % UPPERS], ALU.subtract).then_inc(lower_ready, 1)

    def ffn_begin_act(act, r):
        for i in range(2):
            upper_act(act, r, i)

    def ffn_begin_dve(dve, r):
        for i in range(2):
            lower_dve(dve, r, i)

    def ffn_act(act, r):
        tiles = r.tiles

        def silu(c):
            w = CHUNKS[c][1]
            for t in range(tiles):
                g = tiles * c + t
                v = r.before(g)
                if v is not None:
                    act.wait_ge(h_ready, v)
                last = [i for i in GATE_END if GATE_END[i] == c][0]
                act.wait_ge(halves_used, r.halves + (last + 1))
                act.activation(act_g[:, g % 2, 0:w], r.banks(c, t)[0][:, 0:w], ACT.Silu).then_inc(act_ready, 1)

        def copy_h(c):
            nf = CHUNKS[c][1] // P
            for t in range(tiles):
                act.wait_ge(h_turned, r.first + (tiles * c + t + 1))
                act.copy(r.hT[:, 4 * c:4 * c + nf, t * P:(t + 1) * P],
                         r.banks(c, t)[0][:, 0:nf * P].rearrange("p (f n) -> p f n", f=nf)).then_inc(hT_ready, 1)

        for i in range(FFN_HALVES):
            if i + 2 < FFN_HALVES:
                upper_act(act, r, i + 2)
            elif r.e is not None:
                with act.If(r.e < EXPERTS - 1):
                    upper_act(act, r.next(), i + 2 - FFN_HALVES)
            if i in GATE_END:
                silu(GATE_END[i])
            if i - 1 in GATE_END and GATE_END[i - 1] > 0:
                copy_h(GATE_END[i - 1] - 1)
            if i == UP_HALVES + 1:
                copy_h(NC - 1)
            if i == 3 and r.n == 0:
                columns_act(act)
            if i == 4 * 3 and tiles == 1:
                copy_spread(act, r.e)
            if i == UP_HALVES + 2 and tiles == 1:
                gathered_act(act, r.e + 1)

    def ffn_dve(dve, step, r):
        tiles = r.tiles

        def hidden(c):
            w = CHUNKS[c][1]
            last = [i for i in UP_END if UP_END[i] == c][0]
            dve.wait_ge(halves_used, r.halves + (last + 1))
            for t in range(tiles):
                g = tiles * c + t
                v = r.before(g)
                if v is not None:
                    dve.wait_ge(h_turned, v)
                dve.wait_ge(act_ready, r.first + (g + 1))
                dve.tensor_tensor(h[:, g % 2, 0:w], act_g[:, g % 2, 0:w], r.banks(c, t)[1][:, 0:w], ALU.mult)\
                   .then_inc(h_ready, 1)

        def lower_h(c):
            nf = CHUNKS[c][1] // P
            for t in range(tiles):
                part = slice(4 * c, 4 * c + nf), slice(t * P, (t + 1) * P)
                dve.wait_ge(hT_ready, r.first + (tiles * c + t + 1))
                dve.tensor_tensor(r.hTl[:, part[0], part[1]],
                                  r.banks(c, t)[0][:, 0:nf * P].rearrange("p (f n) -> p f n", f=nf),
                                  r.hT[:, part[0], part[1]], ALU.subtract).then_inc(hL_ready, 1)

        has_mod = r.n is not None and r.n < 4
        for i in range(FFN_HALVES):
            if i == UP_HALVES - 1 and r.e is None:
                lower_h(NC - 2)
            if i + 2 < FFN_HALVES:
                lower_dve(dve, r, i + 2)
            elif r.e is not None:
                with dve.If(r.e < EXPERTS - 1):
                    lower_dve(dve, r.next(), i + 2 - FFN_HALVES)
            if i - 1 in GATE_END and GATE_END[i - 1] > 0 or i == UP_HALVES + 1:
                c = GATE_END[i - 1] - 1 if i - 1 in GATE_END else NC - 1
                if i != UP_HALVES - 1 or r.e is not None:
                    lower_h(c)
                if has_mod and c < NC - 2:
                    mod_out(dve, r.n, c, r.banks(c, 0)[1])
            if has_mod and i - 1 in MOD_LATE and MOD_LATE[i - 1] == NC - 1:
                mod_out(dve, r.n, NC - 1, r.banks(NC - 1, 0)[1])
            if i in UP_END:
                if has_mod and i in MOD_LATE:
                    mod_out(dve, r.n, MOD_LATE[i], r.banks(MOD_LATE[i], 0)[1])
                hidden(UP_END[i])
                if i == 3 and r.n == 0:
                    columns_dve(dve)
                if has_mod:
                    ada(dve, step, r.n, UP_END[i], 0)
                    ada(dve, step, r.n, UP_END[i], 1)
            if i == UP_HALVES + 1 and tiles == 1:
                gathered_dve(dve, r.e + 1)
            if i == UP_HALVES + 4 and tiles == 1:
                gathered_lower_dve(dve, r.e + 1)

    def ada(dve, step, n, c, j):
        i = n * NC + c
        if i == 0 and j == 0:
            dve.wait_ge(param_ready, 5)
        if i > 0 and j == 0:
            dve.wait_ge(mod_done, i)
        dve.wait_ge(ada_landed[j], 16 * (i + 1))
        sums = ada_acc[:, j * (CHUNK // 2):(j + 1) * (CHUNK // 2)]
        for k in range(KD):
            src = ada_w[:, j, k, :]
            if k == 0:
                ins = dve.tensor_scalar(sums, src, cond[:, k:k + 1], None, ALU.mult)
            else:
                ins = dve.scalar_tensor_tensor(sums, src, cond[:, k:k + 1], sums, ALU.mult, ALU.add)
            if k < KD - 1:
                ins.then_inc(*step.one())
                dve.wait_ge(*step.now())
            else:
                ins.then_inc(ada_ready, 1)

    def mod_out(dve, n, c, sums):
        l, a = divmod(n * NC + c, 12)
        v, part = divmod(a, 2)
        i = n * NC + c
        dve.wait_ge(mod_done, i + 1)
        if v in (2, 5):
            j = 2 * (2 * l + v // 3) + part
            if j >= 2:
                dve.wait_ge(gate_stored, 16 * (j - 1))
            dve.tensor_scalar(gate_row[0:1, j % 2, :], sums[0:1, :], 1.0, None, ALU.add).then_inc(mod_ready, 1)
        else:
            bias = cols_b[:, l * 48 + a * 4:l * 48 + a * 4 + 4]
            dve.scalar_tensor_tensor(mod_col[:, l, v, part * 4:part * 4 + 4], sums[:, 0:4],
                                     1.0 if v in (1, 4) else 0.0, bias, ALU.add, ALU.add).then_inc(mod_ready, 1)

    def load_ada(pool, i):
        l, a = divmod(i, 12)
        for j in range(2):
            if i > 0:
                pool.wait_ge(ada_ready, 2 * i - 1 + j)
            c0 = a * CHUNK + j * (CHUNK // 2)
            pool.dma_start(ada_w[:, j, :, :], rows(A["ada_w_2"][l])[:, :, c0:c0 + CHUNK // 2]).then_inc(ada_landed[j], 16)

    def gate_pool(pool, n):
        for c in range(NC):
            i = n * NC + c
            if c == 0:
                load_ada(pool, i)
            if c < NC - 1:
                load_ada(pool, i + 1)
            l, a = divmod(i, 12)
            v, part = divmod(a, 2)
            if v in (2, 5):
                j = 2 * (2 * l + v // 3) + part
                pool.wait_ge(mod_ready, i + 1)
                pool.dma_start(gate_dram[j // 2:j // 2 + 1, part * CHUNK:(part + 1) * CHUNK],
                               gate_row[0:1, j % 2, :]).then_inc(gate_stored, 16)

    cv = Carve()
    qT = cv.take(REP, SEQ)
    kT = cv.take(2, SEQ)
    vv = cv.take(2, NT, P)
    gates = cv.take(NT, 3 * HEADS)
    zc = cv.take(2, 2, SEQ)
    g1 = cv.take(2, CMP_STRIDE)
    g1rep = cv.take(HEADS, CMP_STRIDE)
    kcT = cv.take(CMP_STRIDE)
    vblk = cv.take(HEADS, HD)
    u_sb = cv.take(NT, 256)
    gqk = cv.take(2, SEQ)
    gv = cv.take(NT, GLA_H * GLA_V)
    gaT = cv.take(SEQ)
    sr = cv.take(NT, GLA_H * GLA_V)
    gl_min, gl_abs, gl_b, gl_eb, gl_enb, gl_ekd = (cv.take(SEQ) for _ in range(6))
    gl_q, gl_k, gl_kd = (cv.take(SEQ) for _ in range(3))
    kdT = cv.take(NT, P)
    s_blk = cv.take(4, GLA_H * GLA_V)
    at_sb = cv.take(GLA_H, NT, P)
    sq = cv.take(NT, GLA_H * GLA_V)
    ss = cv.take(NT, GLA_H)
    ss_std = cv.take(NT, GLA_H)
    oC = cv.take(NT, GLA_H * GLA_V)
    pooledT = cv.take(2, SEQ)
    oA = cv.take(NT, HEADS * HD)
    o_tmp = cv.take(HEADS * HD)
    pT = cv.take(2, 2 * REP, P)
    pc = cv.take(NT, HEADS, CMP_STRIDE)
    pc_max = cv.take(NT * HEADS)
    pc_sum = cv.take(NT * HEADS)
    pcT = cv.take(NT, P)
    nmax = cv.take(8, REP)
    rsum = cv.take(8, REP)
    o_w = cv.take(2, HEADS)
    p_sb = z[:, :, :]
    oT = xT

    UNITS = [(t, b, g) for t in range(NT) for b in range(2) for g in range(GROUPS)]

    def bank(i):
        return psum[:, i, :]

    def mix_sp(sp, l):
        w = rows(A["w_in"][l])
        for i, (c0, n) in enumerate(IN_PANELS):
            if i == 3:
                pn = PN["mix", l, "w1"]
                dst = slot_of(pn).rearrange("p (v j o) -> p v j o", v=2, o=HD)
                load_panel(sp, pn, [(dst[d * HD:(d + 1) * HD, v], A["cmp_w1"][l, v].rearrange("(j d) o -> d j o", d=HD))
                                    for v in range(2) for d in range(2)])
            pn = PN["mix", l, "in", i]
            if i == 0:
                dst = panel(pn, KD, n).rearrange("p k (r g d) -> p k r g d", r=REP, g=GROUPS)
                src = w[:, :, 0:n].rearrange("p k (g r d) -> p k g r d", g=GROUPS, r=REP)
                load_panel(sp, pn, [(dst[:, :, r, g, :], src[:, :, g, r, :]) for r in range(REP) for g in range(GROUPS)])
            else:
                load_panel(sp, pn, [(panel(pn, KD, n), w[:, :, c0:c0 + n])])
        for i in range(2):
            pn = PN["mix", l, "out", i]
            load_panel(sp, pn, [(panel(pn, KD, CHUNK), rows(A["w_out"][l])[:, :, i * CHUNK:(i + 1) * CHUNK])])

    def mix_pe(pe, l):
        def features(dst, pn, w, first, m):
            for k in range(KD):
                mm = pe.matmul(dst, panel(pn, KD, w)[:, k, first:first + m], xT[:, k, :], start=k == 0, stop=k == KD - 1)
            return mm

        def tokens(dst, pn, w, first, m, t):
            for k in range(KD):
                mm = pe.matmul(dst, xT[:, k, t * P:(t + 1) * P], panel(pn, KD, w)[:, k, first:first + m],
                               start=k == 0, stop=k == KD - 1)
            return mm

        pn = [PN["mix", l, "in", i] for i in range(len(IN_PANELS))]
        pe.wait_ge(*landed(pn[0]))
        for r in range(REP):
            mm = features(bank(r // 2)[:, (r % 2) * SEQ:(r % 2 + 1) * SEQ], pn[0], 512, r * P, P)
            if r % 2:
                mm.then_inc(*mixP.inc(f"q{r // 2}", l))
        pe.wait_ge(*landed(pn[1]))
        features(bank(2)[:, 0:SEQ], pn[1], 512, 0, P)
        features(bank(2)[:, SEQ:2 * SEQ], pn[1], 512, 128, P).then_inc(*mixP.inc("kcvc", l))
        features(bank(3)[:, 0:SEQ], pn[1], 512, 256, P)
        for t in range(NT):
            mm = tokens(bank(4)[:, t * P:(t + 1) * P], pn[1], 512, 384, P, t)
        mm.then_inc(*mixP.inc("vs", l))
        pe.wait_ge(*landed(pn[2]))
        features(bank(3)[:, SEQ:2 * SEQ], pn[2], 280, 0, P).then_inc(*mixP.inc("kskw", l))
        for t in range(NT):
            mm = tokens(bank(5)[:, t * 256:t * 256 + 152], pn[2], 280, 128, 152, t)
        mm.then_inc(*mixP.inc("vwgl", l))

        w1 = PN["mix", l, "w1"]
        pe.wait_ge(*landed(w1))
        pe.wait_ge(*mixV.after("zc", l))
        w1v = slot_of(w1).rearrange("p (v j o) -> p v j o", v=2, o=HD)
        for v in range(2):
            for j in range(CMP_BLOCK):
                half, pos = divmod(j, CMP_STRIDE)
                for g in range(GROUPS):
                    part = slice(g * HD, (g + 1) * HD)
                    src = zc[part, v, half, :].rearrange("p (c j) -> p c j", j=CMP_STRIDE)[:, half:half + N_CMP, pos]
                    mm = pe.matmul(bank(6 + g)[part, v * CMP_STRIDE:v * CMP_STRIDE + N_CMP], w1v[part, v, j, :], src,
                                   start=j == 0, stop=j == CMP_BLOCK - 1)
        mm.then_inc(*mixP.inc("cmp1", l))

        pe.wait_ge(*landed(pn[3]))
        pe.wait_ge(*mixA.after("q0", l))
        for t in range(NT):
            mm = tokens(bank(0)[:, t * 256:(t + 1) * 256], pn[3], 512, 0, 256, t)
        mm.then_inc(*mixP.inc("u", l))
        pe.wait_ge(*mixA.after("q1", l))
        features(bank(1)[:, 0:SEQ], pn[3], 512, 256, P)
        features(bank(1)[:, SEQ:2 * SEQ], pn[3], 512, 384, P).then_inc(*mixP.inc("gqk", l))
        pe.wait_ge(*landed(pn[4]))
        for t in range(NT):
            mm = tokens(bank(2)[:, t * 256:(t + 1) * 256], pn[4], 272, 0, 256, t)
        mm.then_inc(*mixP.inc("gv", l))
        pe.wait_ge(*mixA.after("kskw", l))
        features(bank(3)[0:16, 0:SEQ], pn[4], 272, 256, 16).then_inc(*mixP.inc("ga", l))
        pe.wait_ge(*landed(pn[5]))
        pe.wait_ge(*mixA.after("vs", l))
        for t in range(NT):
            mm = tokens(bank(4)[:, t * 256:(t + 1) * 256], pn[5], 256, 0, 256, t)
        mm.then_inc(*mixP.inc("gr", l))

        pe.wait_ge(*mixA.after("g1", l))
        pe.wait_ge(*mixA.after("ga", l))
        pe.matmul(bank(6)[:, 0:SEQ], gla_wa2[:, l, :], gaT[0:16, :], start=True, stop=True).then_inc(*mixP.inc("pre", l))
        pe.wait_ge(*mixA.after("gates", l))
        pe.matmul(bank(5)[:, 0:CMP_STRIDE], w2bd[:, 2 * l, :], g1[:, 0, :], start=True, stop=True)
        pe.wait_ge(*mixV.after("g1rep", l))
        pe.matmul(bank(5)[:, P:2 * P], g1rep[:, :, :].rearrange("p h n -> p (h n)"), w2bd[:, 2 * l + 1, :],
                  start=True, stop=True).then_inc(*mixP.inc("cmp2", l))
        pe.wait_ge(*mixV.after("u", l))
        pe.wait_ge(*mixV.after("gqk", l))
        bands = const("bands").rearrange("p (w t) -> p w t", t=SEQ + P)
        for i in range(len(POOL_WINDOWS)):
            dst = bank(i // 2)[:, (i % 2) * SEQ:(i % 2 + 1) * SEQ]
            cols = slice((i // 2) * P, (i // 2 + 1) * P)
            pe.matmul(dst[:, 0:P], u_sb[:, 0, cols], bands[:, i, 0:P], start=True, stop=True)
            pe.matmul(dst[:, P:SEQ], u_sb[:, 0, cols], bands[:, i, P:SEQ], start=True, stop=False)
            mm = pe.matmul(dst[:, P:SEQ], u_sb[:, 1, cols], bands[:, i, SEQ:SEQ + P], start=False, stop=True)
        mm.then_inc(*mixP.inc("pool1", l))

        pe.wait_ge(*mixV.after("gl_kd", l))
        for t in range(NT):
            mm = pe.transpose(bank(3)[:, t * P:(t + 1) * P], gl_kd[:, t * P:(t + 1) * P], ident)
        mm.then_inc(*mixP.inc("kdT", l))
        pe.wait_ge(*mixA.after("pool1", l))
        for i in range(2):
            mm = pe.matmul(bank(7)[:, i * SEQ:(i + 1) * SEQ], poolbd[:, 2 * l + i, :], pooledT[:, i, :],
                           start=True, stop=True)
        mm.then_inc(*mixP.inc("pool2", l))
        pe.wait_ge(*mixA.after("kdT", l))
        pe.wait_ge(*mixV.after("gv", l))
        pe.wait_ge(*mixA.after("sr", l))
        pe.wait_ge(*mixV.after("vblk", l))
        for n in range(3):
            part = slice((n % 2) * GLA_CHUNK, (n % 2 + 1) * GLA_CHUNK)
            mm = pe.matmul(bank(4 + n % 2)[:, (n // 2) * 256:(n // 2 + 1) * 256], kdT[part, n // 2, :], gv[part, n // 2, :],
                           start=True, stop=True)
        mm.then_inc(*mixP.inc("dS", l))
        for t in range(NT):
            for hh in range(GLA_H):
                part = slice(hh * GLA_K, (hh + 1) * GLA_K)
                mm = pe.matmul(bank(hh)[:, t * P:(t + 1) * P], gl_k[part, t * P:(t + 1) * P], gl_q[part, t * P:(t + 1) * P],
                               start=True, stop=True)
        mm.then_inc(*mixP.inc("at", l))
        pe.wait_ge(*mixV.after("s_blk", l))
        pe.wait_ge(*mixV.after("at", l))
        pe.wait_ge(*mixV.after("gl_v", l))
        pe.wait_ge(*mixA.after("pool2", l))
        for t in range(NT):
            for n in (2 * t, 2 * t + 1):
                part = slice((n % 2) * GLA_CHUNK, (n % 2 + 1) * GLA_CHUNK)
                pe.matmul(bank(6 + t)[part, 0:256], gl_q[:, n * GLA_CHUNK:(n + 1) * GLA_CHUNK], s_blk[:, n, :],
                          start=True, stop=True)
            for hh in range(GLA_H):
                mm = pe.matmul(bank(6 + t)[:, hh * GLA_V:(hh + 1) * GLA_V], at_sb[:, hh, t, :],
                               gv[:, t, hh * GLA_V:(hh + 1) * GLA_V], start=False, stop=True, skip_group_check=True)
            mm.then_inc(*mixP.inc(f"gla{t}", l))

        pe.wait_ge(*mixV.after("kcT", l))
        for t in range(NT):
            for r in range(REP):
                for g in range(GROUPS):
                    part = slice(g * HD, (g + 1) * HD)
                    at = (t * REP + r) * CMP_STRIDE
                    mm = pe.matmul(bank(g)[:, at:at + CMP_STRIDE], qT[part, r, t * P:(t + 1) * P], kcT[part, :],
                                   start=True, stop=True)
        mm.then_inc(*mixP.inc("sc", l))

        def scores(i):
            t, b, g = UNITS[i]
            nk = P * (t + 1)
            part = slice(g * HD, (g + 1) * HD)
            if i >= 2:
                pe.wait_ge(*mixV.after(f"p{i - 2}", l))
            else:
                pe.wait_ge(*mixV.after("pc_bias" if i == 0 else "at", l))
                pe.wait_ge(*mixV.after("pc_bias", l))
            dst = psum[:, 2 * (i % 2):2 * (i % 2) + 2, :].rearrange("p b n -> p (b n)")
            for r in range(REP):
                mm = pe.matmul(dst[:, r * nk:(r + 1) * nk], qT[part, r, t * P:(t + 1) * P], kT[part, b, 0:nk],
                               start=True, stop=True)
            mm.then_inc(*mixP.inc(f"s{i}", l))

        def turn_p(i):
            t, b, g = UNITS[i]
            pe.wait_ge(*mixA.after(f"e{i}", l))
            if i > 0:
                pe.wait_ge(*mixA.after(f"pT{i - 1}", l))
            else:
                pe.wait_ge(*mixV.after("oc1", l))
            dst = psum[:, 4:6, :].rearrange("p b n -> p (b n)")
            for j in range(REP * (t + 1)):
                mm = pe.transpose(dst[:, j * P:(j + 1) * P], p_sb[:, i % 2, j * P:(j + 1) * P], ident)
            mm.then_inc(*mixP.inc(f"t{i}", l))

        def values(i):
            t, b, g = UNITS[i]
            pe.wait_ge(*mixA.after(f"pT{i}", l))
            if g == 0:
                pe.wait_ge(*mixV.after(f"oC{b}" if t == 0 else f"oA{b}_{t - 1}", l))
            for r in range(REP):
                for kt in range(t + 1):
                    mm = pe.matmul(bank(6 + b)[:, (g * REP + r) * HD:(g * REP + r + 1) * HD], pT[:, i % 2, r * (t + 1) + kt, :],
                                   vv[:, b, kt, g * HD:(g + 1) * HD], start=kt == 0, stop=kt == t)
            mm.then_inc(*mixP.inc(f"v{i}", l))

        scores(0)
        pe.wait_ge(*mixV.after("pc", l))
        for t in range(NT):
            mm = pe.transpose(bank(3)[:, t * P:(t + 1) * P], pc[:, t, :, :].rearrange("p h n -> p (h n)"), ident)
        mm.then_inc(*mixP.inc("pcT", l))
        pe.wait_ge(*mixA.after("pcT", l))
        for t in range(NT):
            pe.matmul(bank(4 + t)[:, :], pcT[:, t, :], vblk[:, :, :].rearrange("p h d -> p (h d)"), start=True, stop=True)\
              .then_inc(*mixP.inc(f"oc{t}", l))
        scores(1)
        for i in range(len(UNITS)):
            turn_p(i)
            if i + 2 < len(UNITS):
                scores(i + 2)
            values(i)

        pe.wait_ge(*mixV.after("oA1_1", l))
        for t in range(NT):
            for j in range(4):
                mm = pe.transpose(bank(t)[:, j * P:(j + 1) * P], oA[:, t, j * P:(j + 1) * P], ident)
            mm.then_inc(*mixP.inc(f"oA{t}", l))
        for t in range(NT):
            for j in range(2):
                mm = pe.transpose(bank(2)[:, (2 * t + j) * P:(2 * t + j + 1) * P], oC[:, t, j * P:(j + 1) * P], ident)
        mm.then_inc(*mixP.inc("oC", l))
        pe.wait_ge(*mixA.after("oT", l))
        for i in range(2):
            po = PN["mix", l, "out", i]
            pe.wait_ge(*landed(po))
            for t in range(NT):
                for k in range(KD):
                    mm = pe.matmul(acc(t, i), oT[:, k, t * P:(t + 1) * P], panel(po, KD, CHUNK)[:, k, :],
                                   start=k == 0, stop=k == KD - 1)
                if i == 1 and t == 0:
                    mm.then_inc(first_tile_done, 1)
            mm.then_inc(*(mixP.inc("wo0", l) if i == 0 else (acc_done, 1)))

    def mix_act(act, step, l):
        for i in range(2):
            act.wait_ge(*mixP.after(f"q{i}", l))
            act.mul(qT[:, 2 * i:2 * i + 2, :], bank(i).rearrange("p (r n) -> p r n", r=2), HD ** -0.5)\
               .then_inc(*mixA.inc(f"q{i}", l))
        act.wait_ge(*mixP.after("vs", l))
        act.copy(vv[:, 0], bank(4)[:, 0:256].rearrange("p (t d) -> p t d", t=NT)).then_inc(*mixA.inc("vs", l))
        act.wait_ge(*mixP.after("kskw", l))
        act.copy(kT[:, :, :], bank(3).rearrange("p (b n) -> p b n", b=2)).then_inc(*mixA.inc("kskw", l))
        act.wait_ge(*mixP.after("vwgl", l))
        vwgl = bank(5).rearrange("p (t c) -> p t c", t=NT)
        act.copy(vv[:, 1], vwgl[:, :, 0:P]).then_inc(*mixA.inc("vw", l))
        act.activation(gates[:, :, :], vwgl[:, :, P:P + 24], ACT.Sigmoid).then_inc(*mixA.inc("gates", l))
        act.wait_ge(*mixP.after("cmp1", l))
        act.wait_ge(*mixG.after("zeros", l))
        for g in range(GROUPS):
            part = slice(g * HD, (g + 1) * HD)
            ins = act.activation(g1[part, :, 0:N_CMP],
                                 bank(6 + g)[part, 0:2 * CMP_STRIDE].rearrange("p (v n) -> p v n", v=2)[:, :, 0:N_CMP],
                                 ACT.Gelu_apprx_tanh)
        ins.then_inc(*mixA.inc("g1", l))
        act.wait_ge(*mixP.after("ga", l))
        act.copy(gaT[0:16, :], bank(3)[0:16, 0:SEQ]).then_inc(*mixA.inc("ga", l))
        act.wait_ge(*mixP.after("gr", l))
        act.activation(sr[:, :, :], bank(4).rearrange("p (t c) -> p t c", t=NT), ACT.Silu).then_inc(*mixA.inc("sr", l))
        act.wait_ge(*mixV.after("gl_v", l))
        act.activation(gl_abs, gl_min, ACT.Abs).then_inc(*mixA.inc("abs", l))
        act.wait_ge(*mixA.after("abs", l))
        act.activation(gl_abs, gl_abs, ACT.Exp, scale=-1.0).then_inc(*mixA.inc("ex", l))
        act.wait_ge(*mixA.after("ex", l))
        act.activation(gl_abs, gl_abs, ACT.Ln, bias=1.0).then_inc(*mixA.inc("ln1", l))
        act.wait_ge(*mixP.after("pool1", l))
        for i in range(len(POOL_WINDOWS)):
            part = slice((i % 2) * HD, (i % 2 + 1) * HD)
            ins = act.copy(pooledT[part, i // 2, :], bank(i // 2)[part, (i % 2) * SEQ:(i % 2 + 1) * SEQ])
        ins.then_inc(*mixA.inc("pool1", l))
        act.wait_ge(*mixV.after("gl_b", l))
        act.activation(gl_eb, gl_b, ACT.Exp, scale=1.0 / GLA_TAU).then_inc(*mixA.inc("eb", l))
        act.activation(gl_enb, gl_b, ACT.Exp, scale=-1.0 / GLA_TAU).then_inc(*mixA.inc("enb", l))
        act.wait_ge(*mixV.after("gl_dd", l))
        act.activation(gl_ekd, gl_ekd, ACT.Exp, scale=1.0 / GLA_TAU).then_inc(*mixA.inc("ekd", l))
        act.wait_ge(*mixP.after("kdT", l))
        act.copy(kdT[:, :, :], bank(3)[:, 0:256].rearrange("p (t c) -> p t c", t=NT)).then_inc(*mixA.inc("kdT", l))
        act.wait_ge(*mixP.after("pool2", l))
        for i in range(2):
            ins = act.mul(oT[:, 4 + i, :], bank(7)[:, i * SEQ:(i + 1) * SEQ], cols_b[:, 104 + 2 * l + i:105 + 2 * l + i])
        ins.then_inc(*mixA.inc("pool2", l))
        for t in range(NT):
            act.wait_ge(*mixP.after(f"gla{t}", l))
            act.activation(sq[:, t, :], bank(6 + t)[:, 0:256], ACT.Square).then_inc(*mixA.inc(f"sq{t}", l))
        act.wait_ge(*mixV.after("ss", l))
        act.activation(ss_std[:, :, :], ss[:, :, :], ACT.Sqrt, bias=eps[:, 2:3], scale=1.0 / GLA_V)\
           .then_inc(*mixA.inc("ss_std", l))
        act.wait_ge(*mixV.after("pc_sub", l))
        act.activation(pc[:, :, :, :], pc[:, :, :, :], ACT.Exp).then_inc(*mixA.inc("pc_exp", l))

        def exps(i):
            t, b, g = UNITS[i]
            nk = P * (t + 1)
            act.wait_ge(*mixV.after(f"m{i}", l))
            for r in range(REP):
                ins = act.activation(p_sb[:, i % 2, r * nk:(r + 1) * nk], p_sb[:, i % 2, r * nk:(r + 1) * nk], ACT.Exp,
                                     bias=nmax[:, i, r:r + 1], accum_out=rsum[:, i, r:r + 1])
            ins.then_inc(*mixA.inc(f"e{i}", l))

        act.wait_ge(*mixP.after("pcT", l))
        act.copy(pcT[:, :, :], bank(3)[:, 0:256].rearrange("p (t c) -> p t c", t=NT)).then_inc(*mixA.inc("pcT", l))
        exps(0)
        for i in range(len(UNITS)):
            t = UNITS[i][0]
            if i + 1 < len(UNITS):
                exps(i + 1)
            act.wait_ge(*mixP.after(f"t{i}", l))
            if i >= 2:
                act.wait_ge(*mixP.after(f"v{i - 2}", l))
            n = REP * (t + 1)
            act.copy(pT[:, i % 2, 0:n, :], psum[:, 4:6, :].rearrange("p b (j n) -> p (b j) n", n=P)[:, 0:n, :])\
               .then_inc(*mixA.inc(f"pT{i}", l))
        for t in range(NT):
            act.wait_ge(*mixP.after(f"oA{t}", l))
            act.copy(oT[:, 0:4, t * P:(t + 1) * P], bank(t).rearrange("p (j n) -> p j n", j=4))
        act.wait_ge(*mixP.after("oC", l))
        act.copy(oT[:, 6:8, :].rearrange("p j (t n) -> p t j n", t=NT), bank(2).rearrange("p (t j n) -> p t j n", t=NT, j=2))\
           .then_inc(*mixA.inc("oT", l))

    def mix_dve(dve, step, l):
        def link(ins):
            ins.then_inc(*step.one())
            dve.wait_ge(*step.now())

        dve.wait_ge(*mixP.after("kcvc", l))
        for v in range(2):
            for half in range(2):
                ins = dve.tensor_tensor(
                    zc[:, v, half, :].rearrange("p (c j) -> p c j", j=CMP_STRIDE),
                    bank(2)[:, v * SEQ:(v + 1) * SEQ].rearrange("p (c j) -> p c j", j=CMP_STRIDE),
                    pe_col[:, 2 * l + v, half * CMP_STRIDE:(half + 1) * CMP_STRIDE].unsqueeze(1)
                    .to_broadcast([P, SEQ // CMP_STRIDE, CMP_STRIDE]), ALU.add)
        ins.then_inc(*mixV.inc("zc", l))
        dve.wait_ge(*mixP.after("u", l))
        dve.tensor_copy(u_sb[:, :, :], bank(0).rearrange("p (t c) -> p t c", t=NT)).then_inc(*mixV.inc("u", l))
        dve.wait_ge(*mixP.after("gqk", l))
        dve.tensor_copy(gqk[:, :, :], bank(1).rearrange("p (t c) -> p t c", t=2)).then_inc(*mixV.inc("gqk", l))
        dve.wait_ge(*mixP.after("gv", l))
        dve.tensor_copy(gv[:, :, :], bank(2).rearrange("p (t c) -> p t c", t=NT)).then_inc(*mixV.inc("gv", l))
        dve.wait_ge(*mixA.after("g1", l))
        dve.tensor_copy(g1rep[:, :, :], g1[:, 1, :].unsqueeze(1).to_broadcast([P, HEADS, CMP_STRIDE]))\
           .then_inc(*mixV.inc("g1rep", l))
        dve.wait_ge(*mixP.after("pre", l))
        dve.tensor_scalar(gl_min, bank(6)[:, 0:SEQ], cols_b[:, 108 + l:109 + l], None, ALU.add)\
           .then_inc(*mixV.inc("gl_v", l))
        dve.wait_ge(*mixV.after("gl_v", l))
        dve.wait_ge(*mixA.after("ln1", l))
        link(dve.scalar_tensor_tensor(gl_min, gl_min, 0.0, gl_abs, ALU.min, ALU.subtract))
        dve.tensor_tensor_scan(gl_b, const("gla_go"), gl_min, 0.0, ALU.mult, ALU.add).then_inc(*mixV.inc("gl_b", l))
        dve.wait_ge(*mixV.after("gl_b", l))
        b4 = gl_b.rearrange("p (n c) -> p n c", c=GLA_CHUNK)
        dve.tensor_tensor(gl_ekd.rearrange("p (n c) -> p n c", c=GLA_CHUNK),
                          b4[:, :, GLA_CHUNK - 1:GLA_CHUNK].to_broadcast([P, 4, GLA_CHUNK]), b4, ALU.subtract)\
           .then_inc(*mixV.inc("gl_dd", l))
        dve.wait_ge(*mixP.after("cmp2", l))
        dve.tensor_copy(kcT, bank(5)[:, 0:CMP_STRIDE]).then_inc(*mixV.inc("kcT", l))
        dve.tensor_tensor(vblk[:, :, :].rearrange("p (g r) d -> p g r d", g=GROUPS),
                          bank(5)[:, P:2 * P].rearrange("p (g d) -> p g d", g=GROUPS).unsqueeze(2)
                          .to_broadcast([P, GROUPS, REP, HD]),
                          const("head_rows").rearrange("p (g r) -> p g r", g=GROUPS).unsqueeze(3)
                          .to_broadcast([P, GROUPS, REP, HD]), ALU.mult).then_inc(*mixV.inc("vblk", l))
        dve.wait_ge(*mixV.after("gqk", l))
        dve.wait_ge(*mixA.after("eb", l))
        dve.scalar_tensor_tensor(gl_q, gqk[:, 0, :], GLA_K ** -0.5, gl_eb, ALU.mult, ALU.mult)
        dve.wait_ge(*mixA.after("ekd", l))
        dve.tensor_tensor(gl_k, gqk[:, 1, :], gl_enb, ALU.mult)
        dve.tensor_tensor(gl_kd, gqk[:, 1, :], gl_ekd, ALU.mult).then_inc(*mixV.inc("gl_kd", l))
        dve.wait_ge(*mixP.after("dS", l))
        dve.wait_ge(*mixG.after("zeros", l))
        for n in range(3):
            for hh in range(GLA_H):
                part, cols = slice(hh * GLA_K, (hh + 1) * GLA_K), slice(hh * GLA_V, (hh + 1) * GLA_V)
                dS = bank(4 + n % 2)[part, (n // 2) * 256:(n // 2 + 1) * 256][:, cols]
                if n == 0:
                    ins = dve.tensor_copy(s_blk[part, 1, cols], dS)
                else:
                    ins = dve.scalar_tensor_tensor(s_blk[part, n + 1, cols], s_blk[part, n, cols],
                                                   gl_eb[part, n * GLA_CHUNK + GLA_CHUNK - 1:(n + 1) * GLA_CHUNK], dS,
                                                   ALU.mult, ALU.add)
            if n < 2:
                link(ins)
            else:
                ins.then_inc(*mixV.inc("s_blk", l))
        dve.wait_ge(*mixP.after("at", l))
        keep = const("gla_keep").bitcast(U32).unsqueeze(1).to_broadcast([P, NT, P])
        for hh in range(GLA_H):
            ins = dve.copy_predicated(at_sb[:, hh, :, :], keep, bank(hh)[:, 0:256].rearrange("p (t n) -> p t n", t=NT))
        ins.then_inc(*mixV.inc("at", l))
        for t in range(NT):
            dve.wait_ge(*mixA.after(f"sq{t}", l))
            ins = dve.tensor_reduce(ss[:, t, :], sq[:, t, :].rearrange("p (h d) -> p h d", d=GLA_V), AX_X, ALU.add)
        ins.then_inc(*mixV.inc("ss", l))
        dve.wait_ge(*mixP.after("sc", l))
        for g in range(GROUPS):
            ins = dve.tensor_tensor(
                pc[:, :, g * REP:(g + 1) * REP, :],
                bank(g)[:, 0:P].rearrange("p (t r n) -> p t r n", t=NT, r=REP),
                const("cmp_bias").rearrange("p (t n) -> p t n", t=NT).unsqueeze(2).to_broadcast([P, NT, REP, CMP_STRIDE]),
                ALU.add)
        ins.then_inc(*mixV.inc("pc_bias", l))
        dve.wait_ge(*mixV.after("pc_bias", l))
        pcf = pc[:, :, :, :].rearrange("p t h n -> p (t h) n")
        link(dve.tensor_reduce(pc_max, pcf, AX_X, ALU.max))
        dve.tensor_tensor(pcf, pcf, pc_max.unsqueeze(2).to_broadcast([P, NT * HEADS, CMP_STRIDE]), ALU.subtract)\
           .then_inc(*mixV.inc("pc_sub", l))
        dve.wait_ge(*mixA.after("ss_std", l))
        link(dve.reciprocal(ss[:, :, :], ss_std[:, :, :]))
        dve.wait_ge(*mixG.after("sr", l))
        for t in range(NT):
            link(dve.tensor_tensor(oC[:, t, :].rearrange("p (h d) -> p h d", d=GLA_V),
                                   bank(6 + t)[:, 0:256].rearrange("p (h d) -> p h d", d=GLA_V),
                                   ss[:, t, :].unsqueeze(2).to_broadcast([P, GLA_H, GLA_V]), ALU.mult))
            dve.tensor_tensor(oC[:, t, :], oC[:, t, :], sr[:, t, :], ALU.mult).then_inc(*mixV.inc(f"oC{t}", l))
        dve.wait_ge(*mixA.after("pc_exp", l))
        link(dve.tensor_tensor(pc[:, :, :, :], pc[:, :, :, :],
                               const("cmp_seen").rearrange("p (t n) -> p t n", t=NT).unsqueeze(2)
                               .to_broadcast([P, NT, HEADS, CMP_STRIDE]), ALU.mult))
        link(dve.tensor_reduce(pc_sum, pcf, AX_X, ALU.add))
        link(dve.tensor_scalar(pc_sum, pc_sum, 0.5, None, ALU.max))
        link(dve.reciprocal(pc_sum, pc_sum))
        dve.tensor_tensor(pcf, pcf, pc_sum.unsqueeze(2).to_broadcast([P, NT * HEADS, CMP_STRIDE]), ALU.mult)\
           .then_inc(*mixV.inc("pc", l))

        def probs(i):
            t, b, g = UNITS[i]
            nk = P * (t + 1)
            dve.wait_ge(*mixP.after(f"s{i}", l))
            if i >= 2:
                dve.wait_ge(*mixP.after(f"t{i - 2}", l))
            src = psum[:, 2 * (i % 2):2 * (i % 2) + 2, :].rearrange("p b n -> p (b n)")[:, 0:REP * nk]
            dst = p_sb[:, i % 2, 0:REP * nk].rearrange("p (r n) -> p r n", r=REP)
            dve.tensor_tensor(dst, src.rearrange("p (r n) -> p r n", r=REP),
                              const("causal")[:, 2 * P - nk:2 * P].unsqueeze(1).to_broadcast([P, REP, nk]), ALU.add)\
               .then_inc(*mixV.inc(f"p{i}", l))
            dve.wait_ge(*mixV.after(f"p{i}", l))
            dve.tensor_reduce(nmax[:, i, :], dst, AX_X, ALU.max, negate=True).then_inc(*mixV.inc(f"m{i}", l))

        def heads(ap):
            return ap.rearrange("p (h d) -> p h d", d=HD)

        def each_head(ap):
            return ap.unsqueeze(2).to_broadcast([P, HEADS, HD])

        g3 = gates[:, :, :].rearrange("p t (h b) -> p t b h", b=3)
        probs(0)
        for t in range(NT):
            dve.wait_ge(*mixP.after(f"oc{t}", l))
            dve.tensor_tensor(heads(oA[:, t, :]), heads(bank(4 + t)), each_head(g3[:, t, 0, :]), ALU.mult)\
               .then_inc(*mixV.inc(f"oc{t}", l))
        for i in range(1, len(UNITS) + 1):
            if i < len(UNITS):
                probs(i)
            t, b, g = UNITS[i - 1]
            if g == GROUPS - 1:
                j = i - 2
                dve.wait_ge(*mixP.after(f"v{i - 1}", l))
                link(dve.reciprocal(o_w[:, b, :], rsum[:, j:j + 2, :].rearrange("p u r -> p (u r)")))
                link(dve.tensor_tensor(o_w[:, b, :], o_w[:, b, :], g3[:, t, 1 + b, :], ALU.mult))
                dve.tensor_tensor(heads(o_tmp), heads(bank(6 + b)), each_head(o_w[:, b, :]), ALU.mult)\
                   .then_inc(*mixV.inc(f"ot{b}_{t}", l))
                dve.wait_ge(*mixV.after(f"ot{b}_{t}", l))
                dve.tensor_tensor(oA[:, t, :], oA[:, t, :], o_tmp, ALU.add).then_inc(*mixV.inc(f"oA{b}_{t}", l))
                dve.wait_ge(*mixV.after(f"oA{b}_{t}", l))

    def mix_pool(pool, step, l):
        pool.memset(s_blk[:, :, :], 0.0)
        pool.memset(at_sb[:, :, :, :], 0.0)
        pool.memset(g1[:, :, :], 0.0).then_inc(*mixG.inc("zeros", l))
        pool.wait_ge(*mixA.after("sr", l))
        pool.tensor_tensor(sr[:, :, :], sr[:, :, :], gla_norm[:, l, :].unsqueeze(1).to_broadcast([P, NT, GLA_H * GLA_V]),
                           ALU.mult).then_inc(*mixG.inc("sr", l))

    cv = Carve()
    sz = cv.take(ML_T, SEQ)
    xc = cv.take(ML_T, SEQ)
    xm = cv.take(ML_T, SEQ)
    kk = xm
    vm = cv.take(NT, ML_INNER)
    gts = cv.take(NT, 2 * ML_HEADS)
    logf, ml_a, ml_f, ml_m, ml_neg, ml_den, ml_em, ml_rd = (cv.take(NT, ML_HEADS) for _ in range(8))
    ml_bn = cv.take(NT, ML_HEADS, 6)
    ml_mv = cv.take(NT, ML_HEADS, 2)
    ml_std, ml_rs = cv.take(NT, ML_HEADS), cv.take(NT, ML_HEADS)
    NP2 = ML_T // 2

    def col_a(name, i):
        return cols_a[:, cols_a_at[name] + i:cols_a_at[name] + i + 1]

    def block_diag(buf):
        return buf.rearrange("p (t n o) -> p t n o", n=P // QKV_BLOCK, o=QKV_BLOCK)

    bd_a = z[:, :, :].rearrange("p t d -> p (t d)")
    bd_b = xT[:, :, :].rearrange("p k n -> p (k n)")

    def ml_scratch():
        q = slot_of(PN["ml", "scratch_q"]).rearrange("p (t n) -> p t n", n=SEQ)
        hh = slot_of(PN["ml", "scratch_h"])
        s = slot_of(PN["ml", "scratch_s"])
        return (q, hh.rearrange("p (t n) -> p t n", n=SEQ), hh.rearrange("p (t n) -> p t n", t=NT),
                s[:, 0:1024].rearrange("p (t h n) -> p t h n", t=NT, h=ML_HEADS),
                [s[:, 1024:1536], s[:, 1536:2560]],
                [s[:, 2560:3072], s[:, 3072:4096]])

    def mlstm_sp(sp):
        w = rows(A["mlstm_w_in_2"][0])
        for i in range(8):
            pn = PN["ml", "in", i]
            load_panel(sp, pn, [(panel(pn, KD, CHUNK), w[:, :, i * CHUNK:(i + 1) * CHUNK])])
        for i in range(4):
            pn = PN["ml", "out", i]
            load_panel(sp, pn, [(panel(pn, 4, D), rows(A["mlstm_w_out_2"][0])[:, 4 * i:4 * i + 4, :])])

    ml_upper = [ring_r[:, 3, c0:c0 + HALF].rearrange("p (k n) -> p k n", k=KD) for c0 in (0, HALF)]
    ml_xh = tail_r[:, :].rearrange("p (k n) -> p k n", k=KD)

    def ml_half(j, of=None):
        w = (ring if of is None else of)[:, PN["ml", "in", j // 2].slot, :].rearrange("p (k n) -> p k n", k=KD)
        return w[:, :, (j % 2) * 2 * P:(j % 2 + 1) * 2 * P]

    def ml_upper_act(act, j):
        if j % 2 == 0:
            act.wait_ge(*landed(PN["ml", "in", j // 2]))
        if j < 2:
            act.wait_ge(*PN["ml", "upper"][0].before)
        else:
            act.wait_ge(*mlP.after(f"in{j - 2}"))
        act.copy(ml_upper[j % 2], ml_half(j)).then_inc(*mlA.inc(f"up{j}"))

    def ml_lower_dve(dve, j):
        dve.wait_ge(*mlA.after(f"up{j}"))
        dve.tensor_tensor(ml_half(j, ring_r), ml_half(j), ml_upper[j % 2], ALU.subtract).then_inc(*mlV.inc(f"lo{j}"))

    def ml_split_act(act):
        act.wait_ge(xT_ready, 4 * (6 + 1))
        act.wait_ge(*PN["ml", "upper"][1].before)
        for b in range(2):
            part = slice(4 * b, 4 * b + 4)
            act.copy(ml_xh[:, part, :], xT[:, part, :]).then_inc(*mlA.inc(f"xh{b}"))

    def ml_split_dve(dve):
        for b in range(2):
            part = slice(4 * b, 4 * b + 4)
            dve.wait_ge(*mlA.after(f"xh{b}"))
            dve.tensor_tensor(xT_r[:, part, :], xT[:, part, :], ml_xh[:, part, :], ALU.subtract)\
               .then_inc(*mlV.inc(f"xl{b}"))

    def mlstm_pe(pe):
        q, vT, hn, diag, sd, sdT = ml_scratch()
        fills = ([f"in{j}" for j in range(2 * NP2)] + [f"vT{j}" for j in range(NP2)] +
                 [f"q{j}" for j in range(NP2)] + [f"k{j}" for j in range(NP2)])

        def fill_bank(name):
            n = fills.index(name)
            if n >= 4:
                pe.wait_ge(*mlA.after(fills[n - 4]))
            return bank(n % 4)

        for j in range(2 * NP2):
            dst = fill_bank(f"in{j}")
            pe.wait_ge(*mlV.after(f"lo{j}"))
            low = ml_half(j, ring_r)
            for i in range(2):
                cols, dst_i = slice(i * P, (i + 1) * P), dst[:, i * SEQ:(i + 1) * SEQ]
                for k in range(KD):
                    if j == 0 and i == 0 and k % 4 == 0:
                        pe.wait_ge(*mlA.after(f"xh{k // 4}"))
                    pe.matmul(dst_i, low[:, k, cols], ml_xh[:, k, :], start=k == 0, stop=False)
                    pe.matmul(dst_i, ml_upper[j % 2][:, k, cols], ml_xh[:, k, :], start=False, stop=False)
                for k in range(KD):
                    if j == 0 and i == 0 and k % 4 == 0:
                        pe.wait_ge(*mlV.after(f"xl{k // 4}"))
                    mm = pe.matmul(dst_i, ml_upper[j % 2][:, k, cols], xT_r[:, k, :], start=False, stop=k == KD - 1)
            mm.then_inc(*mlP.inc(f"in{j}"))

        bv = bd_a.rearrange("p (t c) -> p t c", c=P)
        pe.wait_ge(*mlV.after("bd_v"))
        for j in range(8):
            t, c4 = divmod(j, 4)
            if j >= 2:
                pe.wait_ge(*mlV.after(f"v{j - 2}"))
            for i in range(4):
                ct = 4 * c4 + i
                mm = pe.matmul(bank(4 + j % 2)[:, i * P:(i + 1) * P], xm[:, ct, t * P:(t + 1) * P], bv[:, ct, :],
                               start=True, stop=True)
            mm.then_inc(*mlP.inc(f"v{j}"))

        def project(name, bd, src):
            for j in range(NP2):
                dst = fill_bank(f"{name}{j}")
                for i in range(2):
                    mm = pe.matmul(dst[:, i * SEQ:(i + 1) * SEQ], bd[:, 2 * j + i, :], src[:, 2 * j + i, :],
                                   start=True, stop=True)
                mm.then_inc(*mlP.inc(f"{name}{j}"))

        def gate_part(i, src, name):
            for ct in range(ML_T):
                if ct % 2 == 0:
                    pe.wait_ge(*mlA.after(f"{name}{ct // 2}"))
                for t in range(NT):
                    mm = pe.matmul(bank(6 + t)[:, 0:2 * ML_HEADS], src[:, ct, t * P:(t + 1) * P], gate_w[:, ML_T * i + ct, :],
                                   start=i == 0 and ct == 0, stop=i == 2 and ct == ML_T - 1)
            return mm

        project("vT", bv, xm)
        pe.wait_ge(*mlV.after("bd_q"))
        pe.wait_ge(*mlA.after(f"xc{NP2 - 1}"))
        project("q", bd_b.rearrange("p (t c) -> p t c", c=P), xc)
        gate_part(0, q, "q")
        pe.wait_ge(*mlV.after("bd_k"))
        project("k", bv, xc)
        gate_part(1, kk, "k")
        gate_part(2, vT, "vT").then_inc(*mlP.inc("gates"))

        pe.wait_ge(*mlV.after("logf"))
        pe.matmul(bank(5)[:, 0:ML_HEADS], const("upto"), logf[:, 0, :], start=True, stop=True)
        pe.matmul(bank(5)[:, ML_HEADS:2 * ML_HEADS], ones, logf[:, 0, :], start=True, stop=False)
        pe.matmul(bank(5)[:, ML_HEADS:2 * ML_HEADS], const("upto"), logf[:, 1, :], start=False, stop=True)\
          .then_inc(*mlP.inc("F"))
        pe.wait_ge(*mlA.after("k7"))
        pe.wait_ge(*mlV.after("diag"))
        for t in range(NT):
            mm = pe.matmul(bank(t), ones, diag[:, t, :, :].rearrange("p h n -> p (h n)"), start=True, stop=True)
        mm.then_inc(*mlP.inc("abc"))

        def score_dst(t):
            return bank(2) if t == 0 else psum[:, 4:6, :].rearrange("p b n -> p (b n)")

        for t in range(NT):
            nk = P * (t + 1)
            for hh in range(ML_HEADS):
                for i in range(4):
                    ct = 4 * hh + i
                    mm = pe.matmul(score_dst(t)[:, hh * nk:(hh + 1) * nk], q[:, ct, t * P:(t + 1) * P], kk[:, ct, 0:nk],
                                   start=i == 0, stop=i == 3)
            mm.then_inc(*mlP.inc(f"S{t}"))
        for t in range(NT):
            pe.wait_ge(*mlV.after(f"sd{t}"))
            dst = bank(3) if t == 0 else psum[:, 6:8, :].rearrange("p b n -> p (b n)")
            for i in range(ML_HEADS * (t + 1)):
                mm = pe.transpose(dst[:, i * P:(i + 1) * P], sd[t][:, i * P:(i + 1) * P], ident)
            mm.then_inc(*mlP.inc(f"T{t}"))
            pe.wait_ge(*mlA.after(f"T{t}"))
            for hh in range(ML_HEADS):
                n = t * ML_HEADS + hh
                if n >= 4:
                    pe.wait_ge(*mlV.after(f"h{n - 4}"))
                if n == 0:
                    pe.wait_ge(*mlV.after("am1"))
                for kt in range(t + 1):
                    mm = pe.matmul(bank(n % 4), sdT[t][:, (hh * (t + 1) + kt) * P:(hh * (t + 1) + kt + 1) * P],
                                   vm[:, kt, hh * ML_HD:(hh + 1) * ML_HD], start=kt == 0, stop=kt == t)
                mm.then_inc(*mlP.inc(f"n{n}"))
        pe.wait_ge(*mlV.after("hn"))
        for j in range(NP2):
            if j >= 4:
                pe.wait_ge(*mlV.after(f"hs{j - 4}"))
            for i in range(2):
                for t in range(NT):
                    mm = pe.transpose(bank(j % 4)[:, i * SEQ + t * P:i * SEQ + (t + 1) * P],
                                      hn[:, t, (2 * j + i) * P:(2 * j + i + 1) * P], ident)
            mm.then_inc(*mlP.inc(f"h{j}"))
        for i in range(4):
            pn = PN["ml", "out", i]
            pe.wait_ge(*landed(pn))
            pe.wait_ge(*mlG.after(f"y{2 * i + 1}"))
            for t in range(NT):
                for k in range(4):
                    for half in range(2):
                        mm = pe.matmul(acc(t, half), xc[:, 4 * i + k, t * P:(t + 1) * P],
                                       panel(pn, 4, D)[:, k, half * 512:(half + 1) * 512],
                                       start=i == 0 and k == 0, stop=i == 3 and k == 3)
                if i == 3 and t == 0:
                    mm.then_inc(first_tile_done, 1)
            mm.then_inc(*(mlP.inc(f"wo{i}") if i < 3 else (acc_done, 1)))

    def mlstm_act(act, step):
        q, vT, hn, diag, sd, sdT = ml_scratch()

        def out_of(j, name, n):
            act.wait_ge(*mlP.after(name))
            return bank(n % 4).rearrange("p (t n) -> p t n", t=2)

        for j in range(NP2):
            ml_upper_act(act, j + 2)
            act.copy(xm[:, 2 * j:2 * j + 2, :], out_of(j, f"in{j}", j)).then_inc(*mlA.inc(f"in{j}"))
        for j in range(NP2):
            n = NP2 + j
            if n + 2 < 2 * NP2:
                ml_upper_act(act, n + 2)
            act.activation(sz[:, 2 * j:2 * j + 2, :], out_of(j, f"in{n}", n), ACT.Silu).then_inc(*mlA.inc(f"in{n}"))
            act.wait_ge(*mlV.after(f"conv{j}"))
            for i in (2 * j, 2 * j + 1):
                ins = act.activation(xc[:, i, :], xc[:, i, :], ACT.Silu, bias=col_a("conv_b", i))
            ins.then_inc(*mlA.inc(f"xc{j}"))
        act.wait_ge(*PN["ml", "scratch_h"].before)
        for j in range(NP2):
            act.copy(vT[:, 2 * j:2 * j + 2, :], out_of(j, f"vT{j}", j)).then_inc(*mlA.inc(f"vT{j}"))
        act.wait_ge(*PN["ml", "scratch_q"].before)
        for j in range(NP2):
            act.mul(q[:, 2 * j:2 * j + 2, :], out_of(j, f"q{j}", j), 1.0).then_inc(*mlA.inc(f"q{j}"))
        for j in range(NP2):
            act.copy(kk[:, 2 * j:2 * j + 2, :], out_of(j, f"k{j}", j)).then_inc(*mlA.inc(f"k{j}"))
        act.wait_ge(*mlV.after("gts"))
        act.activation(logf[:, :, :], gts[:, :, ML_HEADS:], ACT.Abs).then_inc(*mlA.inc("abs"))
        act.wait_ge(*mlA.after("abs"))
        act.activation(logf[:, :, :], logf[:, :, :], ACT.Exp, scale=-1.0).then_inc(*mlA.inc("ex"))
        act.wait_ge(*mlA.after("ex"))
        act.activation(logf[:, :, :], logf[:, :, :], ACT.Ln, bias=1.0).then_inc(*mlA.inc("ln1"))
        act.wait_ge(*mlP.after("k7"))
        for i in range(ML_T):
            ins = act.mul(xc[:, i, :], xc[:, i, :], col_a("skip", i))
        ins.then_inc(*mlA.inc("skip"))
        for t in range(NT):
            nk = P * (t + 1)
            act.wait_ge(*mlV.after(f"m{t}"))
            for hh in range(ML_HEADS):
                ins = act.activation(sd[t][:, hh * nk:(hh + 1) * nk], sd[t][:, hh * nk:(hh + 1) * nk], ACT.Exp,
                                     bias=ml_neg[:, t, hh:hh + 1])
            ins.then_inc(*mlA.inc(f"E{t}"))
        act.activation(ml_em[:, :, :], ml_em[:, :, :], ACT.Exp, scale=-1.0).then_inc(*mlA.inc("em"))
        for t in range(NT):
            act.wait_ge(*mlP.after(f"T{t}"))
            src = bank(3) if t == 0 else psum[:, 6:8, :].rearrange("p b n -> p (b n)")
            act.copy(sdT[t], src).then_inc(*mlA.inc(f"T{t}"))
        act.wait_ge(*mlV.after("h_mv"))
        act.activation(ml_std[:, :, :], ml_mv[:, :, :, 1], ACT.Sqrt, bias=eps[:, 1:2]).then_inc(*mlA.inc("hstd"))

    def mlstm_dve(dve, step):
        q, vT, hn, diag, sd, sdT = ml_scratch()

        def link(ins):
            ins.then_inc(*step.one())
            dve.wait_ge(*step.now())

        def build_bd(buf, i, name):
            dve.tensor_tensor(block_diag(buf),
                              qkv_w[:, i, :, :].unsqueeze(2).to_broadcast([P, ML_T, P // QKV_BLOCK, QKV_BLOCK]),
                              const("blk4").unsqueeze(1).unsqueeze(3).to_broadcast([P, ML_T, P // QKV_BLOCK, QKV_BLOCK]),
                              ALU.mult).then_inc(*mlV.inc(name))

        dve.wait_ge(x_ready, NT * 6)
        build_bd(bd_a, 2, "bd_v")
        for j in range(NP2):
            ml_lower_dve(dve, j + 2)
            dve.wait_ge(*mlA.after(f"in{j}"))
            for tap in range(ML_CONV - 1, -1, -1):
                back = ML_CONV - 1 - tap
                for i in (2 * j, 2 * j + 1):
                    w = col_a("conv_w", tap * ML_T + i)
                    if back == 0:
                        ins = dve.tensor_scalar(xc[:, i, :], xm[:, i, :], w, None, ALU.mult)
                    else:
                        ins = dve.scalar_tensor_tensor(xc[:, i, back:], xm[:, i, 0:SEQ - back], w, xc[:, i, back:],
                                                       ALU.mult, ALU.add)
                if back < ML_CONV - 1:
                    link(ins)
                else:
                    ins.then_inc(*mlV.inc(f"conv{j}"))
        for j in range(NP2 + 2, 2 * NP2):
            ml_lower_dve(dve, j)
        dve.wait_ge(*mlP.after(f"in{2 * NP2 - 1}"))
        build_bd(bd_b, 0, "bd_q")
        for j in range(8):
            t, c4 = divmod(j, 4)
            dve.wait_ge(*mlP.after(f"v{j}"))
            dve.tensor_copy(vm[:, t, c4 * 512:(c4 + 1) * 512], bank(4 + j % 2)).then_inc(*mlV.inc(f"v{j}"))
        dve.wait_ge(*mlP.after(f"vT{NP2 - 1}"))
        build_bd(bd_a, 1, "bd_k")
        dve.wait_ge(*mlP.after("gates"))
        for t in range(NT):
            ins = dve.tensor_tensor(gts[:, t, :], bank(6 + t)[:, 0:2 * ML_HEADS], gate_b[:, :], ALU.add)
        ins.then_inc(*mlV.inc("gts"))
        dve.wait_ge(*mlA.after("ln1"))
        dve.wait_ge(*mlV.after("gts"))
        dve.scalar_tensor_tensor(logf[:, :, :], gts[:, :, ML_HEADS:], 0.0, logf[:, :, :], ALU.min, ALU.subtract)\
           .then_inc(*mlV.inc("logf"))
        dve.wait_ge(*mlP.after("F"))
        f_ps = bank(5)[:, 0:NT * ML_HEADS].rearrange("p (t h) -> p t h", t=NT)
        dve.tensor_copy(ml_f[:, :, :], f_ps)
        link(dve.tensor_tensor(ml_a[:, :, :], gts[:, :, 0:ML_HEADS], f_ps, ALU.subtract))
        dve.wait_ge(*PN["ml", "scratch_s"].before)
        for t in range(NT):
            ins = dve.tensor_tensor(diag[:, t, :, :], ident.unsqueeze(1).to_broadcast([P, ML_HEADS, P]),
                                    ml_a[:, t, :].unsqueeze(2).to_broadcast([P, ML_HEADS, P]), ALU.mult)
        ins.then_inc(*mlV.inc("diag"))
        dve.wait_ge(*mlP.after("abc"))
        causal = const("causal")[:, P:2 * P].unsqueeze(1).to_broadcast([P, ML_HEADS, P])
        sdv = [sd[t].rearrange("p (h n) -> p h n", h=ML_HEADS) for t in range(NT)]
        a_all = [bank(t).rearrange("p (h n) -> p h n", h=ML_HEADS) for t in range(NT)]
        dve.tensor_tensor(sdv[0], a_all[0], causal, ALU.add).then_inc(*mlV.inc("am0"))
        dve.tensor_copy(sdv[1][:, :, 0:P], a_all[0])
        dve.tensor_tensor(sdv[1][:, :, P:2 * P], a_all[1], causal, ALU.add).then_inc(*mlV.inc("am1"))
        dve.wait_ge(*mlV.after("am1"))
        for t in range(NT):
            link(dve.tensor_reduce(ml_m[:, t, :], sdv[t], AX_X, ALU.max))
            link(dve.tensor_scalar(ml_m[:, t, :], ml_m[:, t, :], 0.0, None, ALU.max))
            if t == 1:
                link(dve.tensor_tensor(ml_em[:, :, :], ml_f[:, :, :], ml_m[:, :, :], ALU.add))
            dve.tensor_scalar(ml_neg[:, t, :], ml_m[:, t, :], -1.0, None, ALU.mult).then_inc(*mlV.inc(f"m{t}"))
        for t in range(NT):
            src = bank(2) if t == 0 else psum[:, 4:6, :].rearrange("p b n -> p (b n)")
            dve.wait_ge(*mlP.after(f"S{t}"))
            dve.wait_ge(*mlA.after(f"E{t}"))
            dve.scalar_tensor_tensor(sd[t], src, ML_HD ** -0.5, sd[t], ALU.mult, ALU.mult).then_inc(*mlV.inc(f"sd{t}"))
            dve.wait_ge(*mlV.after(f"sd{t}"))
            link(dve.tensor_reduce(ml_den[:, t, :], sdv[t], AX_X, ALU.add))
        link(dve.scalar_tensor_tensor(ml_den[:, :, :], ml_den[:, :, :], -1.0, ml_den[:, :, :], ALU.mult, ALU.max))
        dve.wait_ge(*mlA.after("em"))
        link(dve.tensor_tensor(ml_den[:, :, :], ml_den[:, :, :], ml_em[:, :, :], ALU.max))
        link(dve.reciprocal(ml_rd[:, :, :], ml_den[:, :, :]))
        dve.wait_ge(*mlP.after("gates"))
        for t in range(NT):
            for hh in range(ML_HEADS):
                n = t * ML_HEADS + hh
                part = hn[:, t, hh * ML_HD:(hh + 1) * ML_HD]
                dve.wait_ge(*mlP.after(f"n{n}"))
                dve.tensor_scalar(part, bank(n % 4), ml_rd[:, t, hh:hh + 1], None, ALU.mult).then_inc(*mlV.inc(f"h{n}"))
                dve.wait_ge(*mlV.after(f"h{n}"))
                link(dve.bn_stats(ml_bn[:, t, hh, :], part))
                ins = dve.bn_aggr(ml_mv[:, t, hh, :], ml_bn[:, t, hh, :])
        ins.then_inc(*mlV.inc("h_mv"))
        dve.wait_ge(*mlA.after("hstd"))
        link(dve.reciprocal(ml_rs[:, :, :], ml_std[:, :, :]))
        for t in range(NT):
            for hh in range(ML_HEADS):
                part = hn[:, t, hh * ML_HD:(hh + 1) * ML_HD]
                ins = dve.tensor_scalar(part, part, ml_mv[:, t, hh, 0:1], ml_rs[:, t, hh:hh + 1], ALU.subtract, ALU.mult)
        ins.then_inc(*mlV.inc("hn"))
        dve.wait_ge(*mlA.after("skip"))
        for j in range(NP2):
            dve.wait_ge(*mlP.after(f"h{j}"))
            for i in range(2):
                ct = 2 * j + i
                ins = dve.scalar_tensor_tensor(xc[:, ct, :], bank(j % 4)[:, i * SEQ:(i + 1) * SEQ], col_a("norm_w", ct),
                                               xc[:, ct, :], ALU.mult, ALU.add)
            ins.then_inc(*mlV.inc(f"hs{j}"))

    def mlstm_pool(pool, step):
        for j in range(NP2):
            pool.wait_ge(*mlV.after(f"hs{j}"))
            pool.tensor_tensor(xc[:, 2 * j:2 * j + 2, :], xc[:, 2 * j:2 * j + 2, :], sz[:, 2 * j:2 * j + 2, :], ALU.mult)\
                .then_inc(*mlG.inc(f"y{j}"))


    QUAD = 4
    TURN = 6.2831850
    cv = Carve()
    rot = cv.take(2, 2, QUAD, SEQ)
    w_in_s = cv.take(2, QUAD, SEQ)
    turned_s = cv.take(2, QUAD, SEQ)
    back_s = cv.take(2, QUAD, SEQ)
    BT = cv.take(2, KD, P)
    CT1 = cv.take(2, QUAD, P)
    phase, whole = Carve(y_end).take(QUAD, SEQ), z[:, 0, :].rearrange("p (j n) -> p j n", j=QUAD)
    sig = w_in_s.rearrange("p a b n -> p (a b n)").rearrange("p (i n) -> p i n", n=CHUNK)
    y_row = y_sum[:, :, :].rearrange("p t d -> p (t d)")
    b_wide = y_row.rearrange("p (a s g h) -> p a s g h", a=2, s=S5_T, g=2)
    c_nat = y_row.rearrange("p (a k n) -> p a k n", a=2, k=KD)
    z_row = z[:, :, :].rearrange("p t d -> p (t d)")
    b_nat = z_row[:, 0:1024].rearrange("p (a s h) -> p a s h", a=2, s=S5_T)
    b_t1, b_t2 = [z_row[:, 1024 + 512 * i:1536 + 512 * i].rearrange("p (s h) -> p s h", s=S5_T) for i in range(2)]
    CT = [z_row[:, 1024:2048].rearrange("p (a j n) -> p a j n", a=2, j=QUAD), CT1]
    cv = Carve(ada_w_end)
    lam_dt, turn, l_mag, l_sin, l_cos, l_abs, l_kr, l_ki, l_den, l_t1, l_t2 = (cv.take(S5_T) for _ in range(11))
    l_re, l_im, l_logdt = lam[:, 0:S5_T], lam[:, S5_T:2 * S5_T], lam[:, 2 * S5_T:3 * S5_T]

    def s5_load_b(pool):
        pool.wait_ge(halves_used, 4 * FFN_HALVES + UP_HALVES)
        for i, part in enumerate(("re", "im")):
            src = A[f"s5_b_{part}_2"][0].rearrange("(s g) p h -> (g p) s h", g=2)
            pool.dma_start(b_nat[:, i, :, :], src).then_inc(b_landed, 16)

    def s5_discrete_act(act):
        act.activation(l_abs, l_logdt, ACT.Exp).then_inc(*s5A.inc("dt"))
        act.wait_ge(*s5V.after("lam_dt"))
        act.activation(l_mag, lam_dt, ACT.Exp).then_inc(*s5A.inc("mag"))
        act.wait_ge(*s5V.after("turn"))
        act.activation(l_sin, turn, ACT.Sin, scale=TURN)
        act.activation(l_cos, turn, ACT.Abs).then_inc(*s5A.inc("abs"))
        act.wait_ge(*s5A.after("abs"))
        act.activation(l_cos, l_cos, ACT.Sin, scale=-TURN, bias=eps[:, 3:4]).then_inc(*s5A.inc("cos"))

    def s5_discrete_dve(dve, step):
        def link(ins):
            ins.then_inc(*step.one())
            dve.wait_ge(*step.now())

        dve.wait_ge(*s5A.after("dt"))
        dve.tensor_tensor(lam_dt, l_re, l_abs, ALU.mult).then_inc(*s5V.inc("lam_dt"))
        link(dve.scalar_tensor_tensor(l_t1, l_im, 1.0 / (2.0 * np.pi), l_abs, ALU.mult, ALU.mult))
        link(dve.tensor_scalar(l_t2, l_t1, ROUND, ROUND, ALU.add, ALU.subtract))
        dve.tensor_tensor(turn, l_t1, l_t2, ALU.subtract).then_inc(*s5V.inc("turn"))
        link(dve.tensor_tensor(l_den, l_re, l_re, ALU.mult))
        link(dve.tensor_tensor(l_t1, l_im, l_im, ALU.mult))
        link(dve.tensor_tensor(l_den, l_den, l_t1, ALU.add))
        link(dve.reciprocal(l_den, l_den))
        dve.wait_ge(*s5A.after("cos"))
        link(dve.tensor_tensor(l_cos, l_cos, l_mag, ALU.mult))
        link(dve.tensor_scalar(l_cos, l_cos, 1.0, None, ALU.subtract))
        link(dve.tensor_tensor(l_sin, l_sin, l_mag, ALU.mult))
        for out_, p_, q_, op in ((l_kr, l_re, l_im, ALU.add), (l_ki, l_im, l_re, ALU.subtract)):
            dve.tensor_tensor(l_t1, l_cos, p_, ALU.mult)
            link(dve.tensor_tensor(l_t2, l_sin, q_, ALU.mult))
            if op == ALU.add:
                link(dve.tensor_tensor(out_, l_t1, l_t2, ALU.add))
            else:
                link(dve.tensor_tensor(out_, l_t2, l_t1, ALU.subtract))
            link(dve.tensor_tensor(out_, out_, l_den, ALU.mult))

    def s5_scale_b_dve(dve, step):
        def link(ins):
            ins.then_inc(*step.one())
            dve.wait_ge(*step.now())

        dve.wait_ge(b_landed, 16 * 2)
        kr, ki = (v.unsqueeze(2).to_broadcast([P, S5_T, S5_H]) for v in (l_kr, l_ki))
        own = const("b_own").unsqueeze(1).unsqueeze(3).to_broadcast([P, S5_T, 2, S5_H])
        for part in range(2):
            dve.tensor_tensor(b_t1, kr, b_nat[:, part, :, :], ALU.mult)
            link(dve.tensor_tensor(b_t2, ki, b_nat[:, 1 - part, :, :], ALU.mult))
            link(dve.tensor_tensor(b_t1, b_t1, b_t2, ALU.add if part else ALU.subtract))
            ins = dve.tensor_tensor(b_wide[:, part, :, :, :], b_t1.unsqueeze(2).to_broadcast([P, S5_T, 2, S5_H]), own, ALU.mult)
            if part == 0:
                link(ins)
            else:
                ins.then_inc(*s5V.inc("b_wide"))

    def s5_states():
        return [slot_of(PN["s5", name]).rearrange("p (i a j n) -> p i a j n", i=2, a=2, j=QUAD)
                for name in ("scratch_s", "scratch_x")]

    def s5_sp(sp):
        sp.wait_ge(*s5P.after("bt3"))
        for i, part in enumerate(("re", "im")):
            src = A[f"s5_c_{part}_2"][0].rearrange("(t g) h p -> (g h) t p", g=KD)
            for copy in range(2):
                sp.dma_start(c_nat[:, i, :, copy * S5_P:(copy + 1) * S5_P], src).then_inc(c_landed, 16)
        w = rows(A["s5_w_glu_2"][0])
        for i in range(4):
            h_, gate = divmod(i, 2)
            c0 = gate * D + h_ * CHUNK
            pn = PN["s5", "glu", i]
            load_panel(sp, pn, [(panel(pn, KD, CHUNK), w[:, :, c0:c0 + CHUNK])])

    def s5_pool(pool, step):
        scanned, states = s5_states()

        def link(ins):
            ins.then_inc(*step.one())
            pool.wait_ge(*step.now())

        def turn_back(k):
            s, xs, r = scanned[:, k % 2, :, :, :], states[:, k % 2, :, :, :], rot[:, k % 2, :, :, :]
            cos, sin = (r[:, i, :, :].unsqueeze(1).to_broadcast([P, 2, QUAD, SEQ]) for i in range(2))
            pool.wait_ge(*s5V.after(f"scan{k}"))
            if k == 0:
                pool.wait_ge(*PN["s5", "scratch_x"].before)
            if k >= 2:
                pool.wait_ge(*s5P.after(f"y{k - 2}"))
            if k >= 1:
                pool.wait_ge(*s5G.after(f"x{k - 1}"))
            for i in range(2):
                pool.tensor_tensor(xs[:, i, :, :], s[:, i, :, :], r[:, 0, :, :], ALU.mult)
                ins = pool.tensor_tensor(back_s[:, i, :, :], s[:, i, :, :], r[:, 1, :, :], ALU.mult)
            link(ins)
            pool.tensor_tensor(xs[:, 0, :, :], xs[:, 0, :, :], back_s[:, 1, :, :], ALU.subtract)
            pool.tensor_tensor(xs[:, 1, :, :], xs[:, 1, :, :], back_s[:, 0, :, :], ALU.add).then_inc(*s5G.inc(f"x{k}"))

        for k in range(KD):
            turn_back(k)
        pool.wait_ge(*s5P.after("y7"))
        pool.dma_start(z_row[0:1, :], A["s5_b_glu_2"]).then_inc(bias_landed, 16)

    def s5_act(act, step):
        def angles(k):
            if k > 0:
                act.wait_ge(*s5A.after(f"rot{k - 1}"))
            for j in range(QUAD):
                turns = turn[:, QUAD * k + j:QUAD * k + j + 1]
                act.activation(phase[:, j, :], const("steps"), ACT.Identity, scale=turns)
                ins = act.activation(whole[:, j, :], const("steps"), ACT.Identity, scale=turns, bias=eps[:, 4:5])
            ins.then_inc(*s5A.inc(f"phase{k}"))

        def rotations(k):
            r = rot[:, k % 2, :, :, :]
            act.wait_ge(*s5V.after(f"angle{k}"))
            if k >= 2:
                act.wait_ge(*s5V.after(f"w{k - 2}"))
                act.wait_ge(*s5G.after(f"x{k - 2}"))
            act.activation(r[:, 1, :, :], phase, ACT.Sin, scale=-TURN)
            act.activation(r[:, 0, :, :], phase, ACT.Abs).then_inc(*s5A.inc(f"abs{k}"))
            act.wait_ge(*s5A.after(f"abs{k}"))
            act.activation(r[:, 0, :, :], r[:, 0, :, :], ACT.Sin, scale=-TURN, bias=eps[:, 3:4]).then_inc(*s5A.inc(f"rot{k}"))

        for i in range(4):
            act.wait_ge(*s5P.after(f"bt{i}"))
            part, half = divmod(i, 2)
            act.copy(BT[:, part, 4 * half:4 * half + 4, :], bank(4 + i).rearrange("p (k n) -> p k n", n=P))\
               .then_inc(*s5A.inc(f"bt{i}"))
        for k in range(KD):
            angles(k)
            rotations(k)
        gelu(act, 0)
        gelu(act, 1)
        for i in range(4):
            act.wait_ge(*s5P.after(f"glu{i}"))
            act.activation(sig[:, i, :], bank(2 * i + 1), ACT.Sigmoid).then_inc(*s5A.inc(f"sig{i}"))

    def gelu(act, half):
        k1 = KD // 2 * (half + 1)
        act.wait_ge(*s5V.after(f"y{k1 - 1}"))
        part = xT[:, k1 - KD // 2:k1, :]
        act.activation(part, part, ACT.Gelu_apprx_tanh).then_inc(*s5A.inc(f"gelu{half}"))

    def s5_dve(dve, step):
        scanned, states = s5_states()

        def link(ins):
            ins.then_inc(*step.one())
            dve.wait_ge(*step.now())

        def skip_u(k):
            dve.wait_ge(*s5P.after(f"y{k}"))
            dve.scalar_tensor_tensor(xT[:, k, :], xT[:, k, :], col_a("s5_d", k), bank(6 + k % 2)[:, 0:SEQ], ALU.mult, ALU.add)\
               .then_inc(*s5V.inc(f"y{k}"))

        def place_c(k):
            dve.wait_ge(*s5P.after(f"ct{k}"))
            if k >= 2:
                dve.wait_ge(*s5P.after(f"y{k - 2}"))
            own = const("c_own").rearrange("p (j n) -> p j n", j=QUAD)
            src = [bank(4 + k % 2)[:, i * P:(i + 1) * P].unsqueeze(1).to_broadcast([P, QUAD, P]) for i in range(2)]
            dve.tensor_tensor(CT[k % 2][:, 0, :, :], src[0], own, ALU.mult)
            dve.scalar_tensor_tensor(CT[k % 2][:, 1, :, :], src[1], -1.0, own, ALU.mult, ALU.mult).then_inc(*s5V.inc(f"ct{k}"))

        def angle(k):
            dve.wait_ge(*s5A.after(f"phase{k}"))
            dve.scalar_tensor_tensor(phase, whole, ROUND, phase, ALU.subtract, ALU.subtract).then_inc(*s5V.inc(f"angle{k}"))

        angle(0)
        for k in range(KD):
            bu = psum[:, 0:QUAD, :].rearrange("p j (a n) -> p a j n", a=2)
            r = rot[:, k % 2, :, :, :]
            dve.wait_ge(*s5P.after(f"bu{k}"))
            dve.wait_ge(*s5A.after(f"rot{k}"))
            if k >= 1:
                dve.wait_ge(*s5V.after(f"scan{k - 1}"))
            for i in range(2):
                dve.tensor_tensor(w_in_s[:, i, :, :], bu[:, i, :, :], r[:, 0, :, :], ALU.mult)
                ins = dve.tensor_tensor(turned_s[:, i, :, :], bu[:, i, :, :], r[:, 1, :, :], ALU.mult)
            ins.then_inc(*s5V.inc(f"w{k}"))
            dve.wait_ge(*s5V.after(f"w{k}"))
            dve.tensor_tensor(w_in_s[:, 0, :, :], w_in_s[:, 0, :, :], turned_s[:, 1, :, :], ALU.add)
            link(dve.tensor_tensor(w_in_s[:, 1, :, :], w_in_s[:, 1, :, :], turned_s[:, 0, :, :], ALU.subtract))
            if k + 1 < KD:
                angle(k + 1)
            if k == 0:
                dve.wait_ge(*PN["s5", "scratch_s"].before)
            if k >= 2:
                dve.wait_ge(*s5G.after(f"x{k - 2}"))
            for j in range(QUAD):
                mag = l_mag[:, QUAD * k + j:QUAD * k + j + 1].to_broadcast([P, SEQ])
                for i in range(2):
                    ins = dve.tensor_tensor_scan(scanned[:, k % 2, i, j, :], mag, w_in_s[:, i, j, :], 0.0, ALU.mult, ALU.add)
            ins.then_inc(*s5V.inc(f"scan{k}"))
            if k >= 1:
                place_c(k - 1)
            if k >= 2:
                skip_u(k - 2)
        place_c(KD - 1)
        skip_u(KD - 2)
        skip_u(KD - 1)
        for i in range(4):
            h_, t = divmod(i, 2)
            dve.wait_ge(*s5A.after(f"sig{i}"))
            ins = dve.tensor_tensor(y_sum[:, t, h_ * CHUNK:(h_ + 1) * CHUNK], bank(2 * i), sig[:, i, :], ALU.mult)
        ins.then_inc(*step.one())

    def s5_turn_b_pe(pe):
        pe.wait_ge(*s5V.after("b_wide"))
        for i in range(4):
            part, half = divmod(i, 2)
            for k in range(4):
                s0 = QUAD * (4 * half + k)
                mm = pe.transpose(bank(4 + i)[:, k * P:(k + 1) * P],
                                  b_wide[:, part, s0:s0 + QUAD, :, :].rearrange("p s g h -> p (s g h)"), ident)
            mm.then_inc(*s5P.inc(f"bt{i}"))

    def s5_pe(pe):
        scanned, states = s5_states()

        def outputs(k):
            pe.wait_ge(*s5V.after(f"ct{k}"))
            pe.wait_ge(*s5G.after(f"x{k}"))
            if k >= 2:
                pe.wait_ge(*s5V.after(f"y{k - 2}"))
            for j in range(QUAD):
                for i in range(2):
                    mm = pe.matmul(bank(6 + k % 2)[:, 0:SEQ], CT[k % 2][:, i, j, :], states[:, k % 2, i, j, :],
                                   start=j == 0 and i == 0, stop=j == QUAD - 1 and i == 1)
            mm.then_inc(*s5P.inc(f"y{k}"))

        def turn_c(k):
            if k == 0:
                pe.wait_ge(c_landed, 16 * 4)
            if k >= 2:
                pe.wait_ge(*s5V.after(f"ct{k - 2}"))
            for i in range(2):
                mm = pe.transpose(bank(4 + k % 2)[:, i * P:(i + 1) * P], c_nat[:, i, k, :], ident)
            mm.then_inc(*s5P.inc(f"ct{k}"))

        pe.wait_ge(*s5A.after("bt3"))
        for k in range(KD):
            if k >= 1:
                pe.wait_ge(*s5V.after(f"w{k - 1}"))
            for j in range(QUAD):
                own_rows = slice(32 * j, 32 * j + 32)
                for i in range(2):
                    mm = pe.matmul(bank(j)[:, i * SEQ:(i + 1) * SEQ], BT[own_rows, i, k, :], xT[own_rows, k, :],
                                   start=True, stop=True)
            mm.then_inc(*s5P.inc(f"bu{k}"))
            if k >= 1:
                turn_c(k - 1)
            if k >= 2:
                outputs(k - 2)
        turn_c(KD - 1)
        outputs(KD - 2)
        outputs(KD - 1)
        pe.wait_ge(*s5A.after("gelu1"))
        pe.wait_ge(bias_landed, 16)
        for h_ in range(2):
            for gate in range(2):
                pn = PN["s5", "glu", 2 * h_ + gate]
                pe.wait_ge(*landed(pn))
                for t in range(NT):
                    i = 2 * h_ + t
                    dst = bank(2 * i + gate)
                    c0 = gate * D + h_ * CHUNK
                    for k in range(KD):
                        mm = pe.matmul(dst, xT[:, k, t * P:(t + 1) * P], panel(pn, KD, CHUNK)[:, k, :],
                                       start=k == 0, stop=False)
                    if t == NT - 1:
                        mm.then_inc(ring_freed[pn.slot], 1)
                    mm = pe.matmul(dst, ones[0:1, :], z_row[0:1, c0:c0 + CHUNK], start=False, stop=True)
                    if gate:
                        mm.then_inc(*s5P.inc(f"glu{i}"))

    r_logit, r_rest, r_eq, r_one, r_two, r_sel, r_cum = (route[:, :, 8 * i:8 * i + 8] for i in range(7))
    r_v1, r_v2, r_at, r_e, r_w1, r_w2, r_total = (route[:, :, 64 + i:65 + i] for i in range(7))
    r_rank = route[:, :, 72:72 + EXPERTS + 1]
    wide = [P, NT, EXPERTS]
    def route_pe(pe):
        for t in range(NT):
            for k in range(KD):
                mm = pe.matmul(bank(4 + t)[:, 0:EXPERTS], xT[:, k, t * P:(t + 1) * P], router[:, k, :],
                               start=k == 0, stop=k == KD - 1)
        mm.then_inc(route_done, 1)
        pe.wait_ge(chosen, 1)
        pe.matmul(bank(6)[:, 0:EXPERTS], const("upto"), r_sel[:, 0, :], start=True, stop=True)
        pe.matmul(bank(6)[:, EXPERTS:2 * EXPERTS], ones, r_sel[:, 0, :], start=True, stop=False)
        pe.matmul(bank(6)[:, EXPERTS:2 * EXPERTS], const("upto"), r_sel[:, 1, :], start=False, stop=True)
        for t in range(NT):
            mm = pe.matmul(bank(6)[:, 2 * EXPERTS:3 * EXPERTS], ones, r_sel[:, t, :], start=t == 0, stop=t == NT - 1)
        mm.then_inc(ranked, 1)

    def route_act(act):
        act.wait_ge(routed, 1)
        act.activation(r_e, r_e, ACT.Exp).then_inc(route_exp, 1)

    def route_dve(dve, step):
        def link(ins):
            ins.then_inc(*step.one())
            dve.wait_ge(*step.now())

        def largest(values, v, one):
            link(dve.tensor_reduce(v, values, AX_X, ALU.max))
            link(dve.tensor_tensor(r_eq, values, v.to_broadcast(wide), ALU.is_ge))
            link(dve.scalar_tensor_tensor(r_eq, numbers, -float(EXPERTS), r_eq, ALU.add, ALU.mult))
            link(dve.tensor_reduce(r_at, r_eq, AX_X, ALU.min))
            link(dve.scalar_tensor_tensor(one, numbers, -float(EXPERTS), r_at.to_broadcast(wide), ALU.add, ALU.is_equal))

        numbers = const("experts").unsqueeze(1).to_broadcast(wide)
        dve.memset(y_sum[:, :, :], 0.0)
        dve.memset(r_rank, -1.0)
        dve.wait_ge(route_done, 1)
        for t in range(NT):
            ins = dve.tensor_copy(r_logit[:, t, :], bank(4 + t)[:, 0:EXPERTS])
        link(ins)
        largest(r_logit, r_v1, r_one)
        link(dve.scalar_tensor_tensor(r_rest, r_one, -3e38, r_logit, ALU.mult, ALU.add))
        largest(r_rest, r_v2, r_two)
        dve.tensor_tensor(r_e, r_v2, r_v1, ALU.subtract).then_inc(routed, 1)
        dve.tensor_tensor(r_sel, r_one, r_two, ALU.add).then_inc(chosen, 1)
        dve.wait_ge(ranked, 1)
        dve.wait_ge(chosen, 1)
        counts = bank(6)[:, 0:2 * EXPERTS].rearrange("p (t e) -> p t e", t=NT)
        link(dve.tensor_tensor(r_cum, counts, r_sel, ALU.mult))
        link(dve.tensor_scalar(r_rank[:, :, 0:EXPERTS], r_cum, 1.0, None, ALU.subtract))
        link(dve.tensor_reduce(r_total[:, 0, :], bank(6)[:, 2 * EXPERTS:3 * EXPERTS], AX_X, ALU.max))
        dve.tensor_scalar(over[:, :], r_total[0:1, 0, :], float(P), None, ALU.is_gt).then_inc(over_ready, 1)
        pick_dve(dve, 0)
        dve.wait_ge(route_exp, 1)
        link(dve.tensor_scalar(r_w1, r_e, 1.0, None, ALU.add))
        link(dve.reciprocal(r_w1, r_w1))
        link(dve.tensor_tensor(r_w2, r_e, r_w1, ALU.mult))
        dve.tensor_tensor(r_one, r_one, r_w1.to_broadcast(wide), ALU.mult)
        link(dve.tensor_tensor(r_two, r_two, r_w2.to_broadcast(wide), ALU.mult))
        dve.tensor_tensor(expert_gate[:, :, :], r_one, r_two, ALU.add).then_inc(moe_added, 1)
        dve.wait_ge(moe_added, 1)

    def slots_used_up(eng):
        eng.wait_ge(over_ready, 1)
        return eng.value_load(over[0:1, 0:1], min_val=0, max_val=1)

    def pick_dve(dve, e):
        slots = const("steps")[:, 0:P]
        for t in range(NT):
            rank = r_rank[:, t, e:e + 1] if isinstance(e, int) else r_rank[:, t, bass.ds(e, 1)]
            ins = dve.tensor_scalar(pick[:, t, :], slots, rank, None, ALU.is_equal)
        ins.then_inc(pick_ready, 1)

    def spread_dve(dve, e):
        slots = const("steps")[:, 0:P]
        for t in range(NT):
            ins = dve.tensor_scalar(spread[:, t, :], slots, r_rank[:, t, bass.ds(e, 1)], expert_gate[:, t, bass.ds(e, 1)],
                                    ALU.is_equal, ALU.mult)
        ins.then_inc(spread_ready, 1)

    def gather_pe(pe, e):
        pe.wait_ge(pick_ready, e + 1)
        if not isinstance(e, int):
            pe.wait_ge(spread_copied, e)
        for k in range(KD):
            for t in range(NT):
                mm = pe.matmul(bank(6 + k // 4)[:, (k % 4) * P:(k % 4 + 1) * P], x[:, t, k * P:(k + 1) * P], pick[:, t, :],
                               start=t == 0, stop=t == NT - 1)
        mm.then_inc(gathered, 1)

    def gathered_dve(dve, e):
        dve.wait_ge(gathered, e + 1)
        for k in range(KD):
            ins = dve.tensor_scalar(xu[:, k, :], bank(6 + k // 4)[:, (k % 4) * P:(k % 4 + 1) * P],
                                    mod_col[:, 1, 4, k:k + 1], mod_col[:, 1, 3, k:k + 1], ALU.mult, ALU.add)
        ins.then_inc(xu_ready, 1)

    def gathered_act(act, e):
        act.wait_ge(xu_ready, e + 1)
        act.copy(xg[:, :, :], xu[:, :, :]).then_inc(xgh_ready, 1)

    def gathered_lower_dve(dve, e):
        dve.wait_ge(xgh_ready, e + 1)
        dve.tensor_tensor(xgl[:, :, :], xu[:, :, :], xg[:, :, :], ALU.subtract).then_inc(xg_ready, 1)

    def turn_spread(pe, e):
        pe.wait_ge(spread_ready, e + 1)
        for t in range(NT):
            mm = pe.transpose(bank(6)[:, t * P:(t + 1) * P], spread[:, t, :], ident)
        mm.then_inc(spread_turned, 1)

    def copy_spread(act, e):
        act.wait_ge(spread_turned, e + 1)
        act.copy(scatter, bank(6)[:, 0:NT * P]).then_inc(spread_copied, 1)

    def expert_pe(pe, e):
        pe.wait_ge(xg_ready, e + 1)
        ffn_pe(pe, Pass("moe", 1, e))
        pe.wait_ge(xg_ready, e + 2)
        for half in range(2):
            pe.wait_ge(half_copied, 2 * e + (half + 1))
            for t in range(NT):
                mm = pe.matmul(bank((6, 0)[half] + t), scatter[:, t * P:(t + 1) * P], y_part[:, half * 512:(half + 1) * 512],
                               start=True, stop=True)
            mm.then_inc(scattered, 1)

    def expert_act(act, e):
        r = Pass("moe", 1, e)
        ffn_act(act, r)
        for half in range(2):
            act.wait_ge(*((half_done, e + 1) if half == 0 else (halves_used, r.halves + FFN_HALVES)))
            act.copy(y_part[:, half * 512:(half + 1) * 512], acc(0, half)).then_inc(half_copied, 1)

    def expert_dve(dve, step, e):
        r = Pass("moe", 1, e)
        spread_dve(dve, e)
        dve.wait_ge(gathered, e + 1)
        pick_dve(dve, e + 1)
        ffn_dve(dve, step, r)
        for half in range(2):
            dve.wait_ge(scattered, 2 * e + (half + 1))
            for t in range(NT):
                part = y_sum[:, t, half * 512:(half + 1) * 512]
                ins = dve.tensor_tensor(part, part, bank((6, 0)[half] + t), ALU.add)
        ins.then_inc(moe_added, 1)
        dve.wait_ge(moe_added, e + 2)

    def moe_add(dve, e):
        dve.wait_ge(halves_used, (e + 6) * FFN_HALVES)
        for t in range(NT):
            ins = dve.scalar_tensor_tensor(y_sum[:, t, :], acc(t), expert_gate[:, t, bass.ds(e, 1)], y_sum[:, t, :],
                                           ALU.mult, ALU.add)
        ins.then_inc(moe_added, 1)
        dve.wait_ge(moe_added, e + 2)


    ACC_READY = {0: (halves_used, FFN_HALVES), 1: (acc_done, 1), 2: (halves_used, 2 * FFN_HALVES),
                 3: (halves_used, 3 * FFN_HALVES), 4: (acc_done, 2), 5: (halves_used, 4 * FFN_HALVES), 6: (acc_done, 3),
                 7: (halves_used, 5 * FFN_HALVES)}
    LAST_Q = max([int(s[2:]) + 1 for s in stages if s.startswith("ln")], default=0)

    def ffn_weights(n):
        if n < 4:
            return A["ffn_wg"][n // 2, n % 2], A["ffn_wu"][n // 2, n % 2], A["ffn_wd"][n // 2, n % 2]
        return A["ffn_w13_2"][0][:, 0:D_FF], A["ffn_w13_2"][0][:, D_FF:2 * D_FF], A["ffn_w2_2"][0]

    block = ctx.enter_context(nc.Block())

    @block.sync
    def _(sp):
        start_sp(sp)
        for st in stages:
            if st.startswith("ffn"):
                ffn_sp(sp, int(st[3:]), *ffn_weights(int(st[3:])))
            elif st.startswith("mix"):
                mix_sp(sp, int(st[3:]))
            elif st == "mlstm":
                mlstm_sp(sp)
            elif st == "s5":
                s5_sp(sp)
            elif st == "moe":
                for slot in range(3):
                    sp.wait_ge(*MOE_BEFORE[slot])
                with sp.Fori(0, EXPERTS) as e:
                    w13 = A["moe_w13_2"][0, e]
                    ffn_sp(sp, "moe", w13[:, 0:D_FF], w13[:, D_FF:2 * D_FF], A["moe_w2_2"][0, e], e)
        sp.wait_ge(x_ready, NT * LAST_Q)
        sp.dma_start(out.rearrange("b (t p) d -> p (b t) d", p=P), x[:, :, :]).then_inc(out_stored, 16)
        sp.wait_ge(out_stored, 16)

    @block.gpsimd
    def _(pool):
        step = Count(pool_step)
        start_pool(pool)
        for st in stages:
            if st.startswith("ffn") and int(st[3:]) < 4:
                if int(st[3:]) == 0:
                    ln_pool(pool, 0)
                gate_pool(pool, int(st[3:]))
            elif st == "ffn4" and "s5" in stages:
                s5_load_b(pool)
            elif st.startswith("ln"):
                m = int(st[2:])
                if f"ln{m + 1}" in stages:
                    ln_pool(pool, m + 1)
            elif st.startswith("mix"):
                mix_pool(pool, step, int(st[3:]))
            elif st == "mlstm":
                mlstm_pool(pool, step)
            elif st == "s5":
                s5_pool(pool, step)

    @block.scalar
    def _(act):
        step = Count(act_step)
        start_act(act)
        copy_xT_act(act, 0)
        for st, later in zip(stages, stages[1:] + [""]):
            if st.startswith("ffn"):
                r = Pass(int(st[3:]))
                if st == "ffn0":
                    ffn_begin_act(act, r)
                if st == "ffn4":
                    split_u_act(act, 0)
                ffn_act(act, r)
            elif st.startswith("ln"):
                m = int(st[2:])
                ln_act(act, m)
                if later.startswith("ffn"):
                    ffn_begin_act(act, Pass(int(later[3:])))
                elif later == "mlstm":
                    for j in range(2):
                        ml_upper_act(act, j)
                if m < 5:
                    copy_xT_act(act, m + 1)
                elif m < 9:
                    modulate_act(act, m + 1)
            elif st.startswith("mix"):
                mix_act(act, step, int(st[3:]))
            elif st == "mlstm":
                ml_split_act(act)
                if "s5" in stages:
                    s5_discrete_act(act)
                mlstm_act(act, step)
            elif st == "s5":
                s5_act(act, step)
            elif st == "moe":
                route_act(act)
                act.wait_ge(*MOE_BEFORE[3])
                ffn_begin_act(act, Pass("moe", 1, 0))
                with act.If(slots_used_up(act) < 1):
                    gathered_act(act, 0)
                    with act.Fori(0, EXPERTS) as e:
                        expert_act(act, e)
                with act.Else():
                    split_u_act(act, 1)
                    with act.Fori(0, EXPERTS) as e:
                        ffn_act(act, Pass("moe", NT, e))

    @block.vector
    def _(dve):
        step = Count(dve_step)
        start_dve(dve)
        for st, later in zip(stages, stages[1:] + [""]):
            if st.startswith("ffn"):
                r = Pass(int(st[3:]))
                if st == "ffn4":
                    split_u_dve(dve, 0)
                else:
                    split_xT_dve(dve, [q for q in FFN_OF if FFN_OF[q] == r.n][0])
                if st == "ffn0":
                    lower_dve(dve, r, 0)
                lower_dve(dve, r, 1)
                ffn_dve(dve, step, r)
                if st == "ffn4" and "s5" in stages:
                    s5_scale_b_dve(dve, step)
            elif st.startswith("ln"):
                m = int(st[2:])
                if m in ACC_READY:
                    ln_dve(dve, step, m, acc, [(first_tile_done, m + 1), ACC_READY[m]])
                elif m == 8:
                    ln_dve(dve, step, m, lambda t: y_sum[:, t, :], [step.now()] * NT)
                else:
                    ln_dve(dve, step, m, lambda t: y_sum[:, t, :], [(moe_added, EXPERTS + 1)] * NT)
                if later.startswith("ffn"):
                    lower_dve(dve, Pass(int(later[3:])), 0)
                elif later == "mlstm":
                    ml_lower_dve(dve, 0)
                if 5 <= m < 9:
                    modulate_dve(dve, m + 1)
            elif st.startswith("mix"):
                mix_dve(dve, step, int(st[3:]))
            elif st == "mlstm":
                ml_split_dve(dve)
                ml_lower_dve(dve, 1)
                if "s5" in stages:
                    s5_discrete_dve(dve, step)
                mlstm_dve(dve, step)
            elif st == "s5":
                s5_dve(dve, step)
            elif st == "moe":
                route_dve(dve, step)
                ffn_begin_dve(dve, Pass("moe", 1, 0))
                with dve.If(slots_used_up(dve) < 1):
                    gathered_dve(dve, 0)
                    gathered_lower_dve(dve, 0)
                    with dve.Fori(0, EXPERTS) as e:
                        expert_dve(dve, step, e)
                with dve.Else():
                    split_u_dve(dve, 1)
                    with dve.Fori(0, EXPERTS) as e:
                        ffn_dve(dve, step, Pass("moe", NT, e))
                        moe_add(dve, e)

    @block.tensor
    def _(pe):
        start_pe(pe)
        q = 0
        for st in stages:
            if st.startswith("ffn"):
                ffn_pe(pe, Pass(int(st[3:])))
            elif st.startswith("ln"):
                q = int(st[2:]) + 1
                if q < 10:
                    turn_x(pe, q)
                if q == 8 and "s5" in stages:
                    s5_turn_b_pe(pe)
            elif st.startswith("mix"):
                wait_xT(pe, q)
                mix_pe(pe, int(st[3:]))
            elif st == "mlstm":
                wait_xT(pe, q)
                mlstm_pe(pe)
            elif st == "s5":
                wait_xT(pe, q)
                s5_pe(pe)
            elif st == "moe":
                wait_xT(pe, q)
                route_pe(pe)
                with pe.If(slots_used_up(pe) < 1):
                    pe.wait_ge(over_ready, 1)
                    gather_pe(pe, 0)
                    with pe.Fori(0, EXPERTS) as e:
                        expert_pe(pe, e)
                with pe.Else():
                    pe.wait_ge(xl_ready, 4 * 6)
                    with pe.Fori(0, EXPERTS) as e:
                        ffn_pe(pe, Pass("moe", NT, e))


INPUTS = ["x", "ln_g", "ln_b", "ffn_wg", "ffn_wu", "ffn_wd", "w_in", "w_out", "cmp_pe", "cmp_w1", "cmp_w2", "pool_w",
          "pool_scale", "gla_wa2", "gla_ba", "gla_norm_g", "c_2", "ada_w_2", "ada_b_2", "ln_mix_g_2", "ln_mix_b_2",
          "ln_ffn_g_2", "ln_ffn_b_2", "mlstm_w_in_2", "mlstm_conv_w_2", "mlstm_conv_b_2", "mlstm_wq_2", "mlstm_wk_2",
          "mlstm_wv_2", "mlstm_w_gates_2", "mlstm_b_gates_2", "mlstm_norm_w_2", "mlstm_skip_2", "mlstm_w_out_2",
          "ffn_w13_2", "ffn_w2_2", "s5_lambda_re_2", "s5_lambda_im_2", "s5_b_re_2", "s5_b_im_2", "s5_c_re_2",
          "s5_c_im_2", "s5_d_2", "s5_log_dt_2", "s5_w_glu_2", "s5_b_glu_2", "moe_router_2", "moe_w13_2", "moe_w2_2"]


def prepare(nc, inputs, upto=None):
    const_at, consts = shape_constants()
    arrays = {"in_" + name: np.ascontiguousarray(inputs[name]) for name in INPUTS}
    arrays["in_consts"] = consts
    A = {name[3:]: nc.dram_tensor(name, a.shape, mybir.dt.from_np(a.dtype), kind="ExternalInput").ap()
         for name, a in arrays.items()}
    out = nc.dram_tensor("out", (1, SEQ, D), F32, kind="ExternalOutput").ap()
    build_program(nc, A, out, const_at, upto)
    return arrays


def kernel(**inputs):
    import concourse.bacc as bacc
    from concourse.bass_utils import run_bass_kernel_spmd

    nc = bacc.Bacc("TRN2", target_bir_lowering=False, num_devices=1)
    arrays = prepare(nc, inputs)
    result = run_bass_kernel_spmd(nc, [arrays], core_ids=[0])
    return result.results[0]["out"]
```
